# Optimizing a Trainium2 kernel written in Bass

```python
import jax, jax.numpy as jnp
from jax import lax
import numpy as np

D_MODEL = 1024
BATCH = 1
SEQ = 512
DEPTH = 1

HEAD_DIM = 64
NSA_HEADS = 8
NSA_KV = 2
DSA_HEADS = 8
IDX_HEADS = 4
IDX_DIM = 64
CMP_LEN = 32
CMP_STRIDE = 16
CMP_HIDDEN = 2 * HEAD_DIM
SLC_LEN = 64
SLC_TOPN = 16
WIN = 512
DSA_TOPK = 256
D_FF = 4 * D_MODEL
D_MIX = (NSA_HEADS + DSA_HEADS) * HEAD_DIM
ROPE_THETA = 10000.0
EPS = 1e-6
Q_BLOCK = 128
SLC_Q_BLOCK = 16
NEG = -1e30
NSA_COLS = [NSA_HEADS * HEAD_DIM] + [NSA_KV * HEAD_DIM] * 6 + [NSA_HEADS * 3]
DSA_COLS = [DSA_HEADS * HEAD_DIM, HEAD_DIM, HEAD_DIM, IDX_HEADS * IDX_DIM, IDX_DIM, IDX_HEADS]
IN_COLS = NSA_COLS + DSA_COLS
D_IN = sum(IN_COLS)


def rms_norm(x, g):
    xf = x.astype(jnp.float32)
    y = xf * lax.rsqrt(jnp.mean(xf * xf, axis=-1, keepdims=True) + EPS)
    return (y * g.astype(jnp.float32)).astype(x.dtype)

def rope(x, pos):
    half = x.shape[-1] // 2
    inv = ROPE_THETA ** (-jnp.arange(half, dtype=jnp.float32) / half)
    ang = pos.astype(jnp.float32)[:, :, None] * inv
    cos = jnp.cos(ang)[:, :, None, :]
    sin = jnp.sin(ang)[:, :, None, :]
    xf = x.astype(jnp.float32)
    x1, x2 = xf[..., :half], xf[..., half:]
    return jnp.concatenate([x1 * cos - x2 * sin, x2 * cos + x1 * sin], axis=-1).astype(x.dtype)

def masked_softmax(s, mask):
    s = jnp.where(mask, s.astype(jnp.float32), NEG)
    return jax.nn.softmax(s, axis=-1) * mask.astype(jnp.float32)

def compress(kv, pe, w1, w2):
    B, T, G, dh = kv.shape
    n_cmp = (T - CMP_LEN) // CMP_STRIDE + 1
    blk = np.arange(n_cmp)[:, None] * CMP_STRIDE + np.arange(CMP_LEN)[None, :]
    blocks = kv[:, blk] + pe[None, None, :, None, :]
    flat = blocks.transpose(0, 1, 3, 2, 4).reshape(B, n_cmp, G, CMP_LEN * dh)
    return jax.nn.gelu(flat @ w1) @ w2

def nsa_attention(q, kc, vc, ks, vs, kw, vw, gate_logits, pe_k, pe_v, w1k, w2k, w1v, w2v):
    B, T, H, dh = q.shape
    G = kc.shape[2]
    R = H // G
    scale = dh ** -0.5
    q_t = q.reshape(B, T, G, R, dh).transpose(0, 2, 3, 1, 4)
    t_idx = np.arange(T)

    k_cmp = compress(kc, pe_k, w1k, w2k)
    v_cmp = compress(vc, pe_v, w1v, w2v)
    n_cmp = k_cmp.shape[1]
    cmp_start = np.arange(n_cmp) * CMP_STRIDE
    cmp_end = cmp_start + CMP_LEN - 1
    mask_c = jnp.asarray(cmp_end[None, :] <= t_idx[:, None])
    s_c = jnp.einsum('bgrtd,bngd->bgrtn', q_t, k_cmp) * scale
    p_c = masked_softmax(s_c, mask_c)
    o_cmp = jnp.einsum('bgrtn,bngd->bgrtd', p_c.astype(v_cmp.dtype), v_cmp)

    n_slc = T // SLC_LEN
    n_sel = min(SLC_TOPN, n_slc)
    slc_start = np.arange(n_slc) * SLC_LEN
    slc_end = slc_start + SLC_LEN - 1
    overlap = ((cmp_start[:, None] <= slc_end[None, :]) & (cmp_end[:, None] >= slc_start[None, :])).astype(np.float32)
    imp = jnp.einsum('bgrtn,nj->bgtj', p_c, jnp.asarray(overlap))
    j = np.arange(n_slc)[None, :]
    cur = (t_idx // SLC_LEN)[:, None]
    valid = jnp.asarray(j <= cur)
    forced = jnp.asarray((j == 0) | (j == cur) | (j == cur - 1))
    sel_score = jnp.where(valid, jnp.where(forced, jnp.inf, imp), -jnp.inf)
    _, sel = lax.top_k(sel_score, n_sel)

    kb = ks.reshape(B, n_slc, SLC_LEN, G, dh).transpose(0, 3, 1, 2, 4)
    vb = vs.reshape(B, n_slc, SLC_LEN, G, dh).transpose(0, 3, 1, 2, 4)
    nq = T // SLC_Q_BLOCK
    n_key = n_sel * SLC_LEN
    q_ch = q_t.reshape(B, G, R, nq, SLC_Q_BLOCK, dh).transpose(3, 0, 1, 2, 4, 5)
    i_ch = sel.reshape(B, G, nq, SLC_Q_BLOCK, n_sel).transpose(2, 0, 1, 3, 4)
    t_ch = jnp.arange(T, dtype=jnp.int32).reshape(nq, SLC_Q_BLOCK)
    bi = jnp.arange(B)[:, None, None, None]
    gi = jnp.arange(G)[None, :, None, None]

    def sel_chunk(args):
        qc, ic, tc = args
        kg = kb[bi, gi, ic].reshape(B, G, SLC_Q_BLOCK, n_key, dh)
        vg = vb[bi, gi, ic].reshape(B, G, SLC_Q_BLOCK, n_key, dh)
        kpos = (ic[..., None] * SLC_LEN + jnp.arange(SLC_LEN)).reshape(B, G, SLC_Q_BLOCK, n_key)
        mask = (kpos <= tc[None, None, :, None])[:, :, None]
        s = jnp.einsum('bgrqd,bgqkd->bgrqk', qc, kg) * scale
        p = masked_softmax(s, mask)
        return jnp.einsum('bgrqk,bgqkd->bgrqd', p.astype(vg.dtype), vg)

    o_slc = lax.map(sel_chunk, (q_ch, i_ch, t_ch))
    o_slc = o_slc.transpose(1, 2, 3, 0, 4, 5).reshape(B, G, R, T, dh)

    kp = jnp.pad(kw, ((0, 0), (WIN, 0), (0, 0), (0, 0)))
    vp = jnp.pad(vw, ((0, 0), (WIN, 0), (0, 0), (0, 0)))
    nb = T // Q_BLOCK
    span = WIN + Q_BLOCK
    q_b = q_t.reshape(B, G, R, nb, Q_BLOCK, dh).transpose(3, 0, 1, 2, 4, 5)

    def win_block(args):
        qb, bidx = args
        s0 = bidx * Q_BLOCK
        kk = lax.dynamic_slice_in_dim(kp, s0, span, axis=1)
        vv = lax.dynamic_slice_in_dim(vp, s0, span, axis=1)
        kpos = s0 - WIN + jnp.arange(span)
        tq = s0 + jnp.arange(Q_BLOCK)
        mask = (kpos[None, :] <= tq[:, None]) & (kpos[None, :] > tq[:, None] - WIN) & (kpos[None, :] >= 0)
        s = jnp.einsum('bgrqd,bsgd->bgrqs', qb, kk) * scale
        p = masked_softmax(s, mask)
        return jnp.einsum('bgrqs,bsgd->bgrqd', p.astype(vv.dtype), vv)

    o_win = lax.map(win_block, (q_b, jnp.arange(nb)))
    o_win = o_win.transpose(1, 2, 3, 0, 4, 5).reshape(B, G, R, T, dh)

    g = jax.nn.sigmoid(gate_logits.astype(jnp.float32)).reshape(B, T, G, R, 3)
    g = g.transpose(0, 2, 3, 1, 4).astype(q.dtype)
    o = g[..., 0:1] * o_cmp + g[..., 1:2] * o_slc + g[..., 2:3] * o_win
    return o.transpose(0, 3, 1, 2, 4).reshape(B, T, H * dh)

def dsa_attention(q, k, v, q_idx, k_idx, w_idx):
    B, T, H, dh = q.shape
    k_top = min(DSA_TOPK, T // 4)
    scale = dh ** -0.5
    idx_scale = (IDX_HEADS ** -0.5) * (IDX_DIM ** -0.5)
    nb = T // Q_BLOCK
    bi = jnp.arange(B)[:, None, None]
    key_pos = jnp.arange(T)

    def blocks(a):
        return a.reshape((B, nb, Q_BLOCK) + a.shape[2:]).swapaxes(0, 1)

    def dsa_block(args):
        qb, qib, wb, bidx = args
        tq = bidx * Q_BLOCK + jnp.arange(Q_BLOCK)
        logits = jnp.einsum('bqhd,bsd->bqhs', qib, k_idx).astype(jnp.float32)
        score = jnp.einsum('bqh,bqhs->bqs', wb.astype(jnp.float32) * idx_scale, jax.nn.relu(logits))
        score = jnp.where(key_pos[None, None, :] <= tq[None, :, None], score, -jnp.inf)
        _, sel = lax.top_k(score, k_top)
        kg = k[bi, sel]
        vg = v[bi, sel]
        mask = (sel <= tq[None, :, None])[:, None]
        s = jnp.einsum('bqhd,bqkd->bhqk', qb, kg) * scale
        p = masked_softmax(s, mask)
        return jnp.einsum('bhqk,bqkd->bqhd', p.astype(vg.dtype), vg)

    o = lax.map(dsa_block, (blocks(q), blocks(q_idx), blocks(w_idx), jnp.arange(nb)))
    return o.swapaxes(0, 1).reshape(B, T, H * dh)

def first_inputs(seed: int = 0) -> dict:
    key = jax.random.key(seed)
    ks = jax.random.split(key, 20)

    def nrm(k, shape, s):
        return jax.random.normal(k, shape, jnp.float32) * s

    x = nrm(ks[0], (BATCH, SEQ, D_MODEL), 1.0)
    c = nrm(ks[1], (BATCH, D_MODEL), 1.0)
    start = jax.random.randint(ks[2], (BATCH, 1), 0, 4096, dtype=jnp.int32)
    positions = start + jnp.arange(SEQ, dtype=jnp.int32)[None, :]
    return {
        'x': x,
        'c': c,
        'positions': positions,
        'w_ada': nrm(ks[3], (DEPTH, D_MODEL, 6 * D_MODEL), 0.1 * D_MODEL ** -0.5),
        'b_ada': nrm(ks[4], (DEPTH, 6 * D_MODEL), 0.01),
        'g_pre_mix': 1.0 + nrm(ks[5], (DEPTH, D_MODEL), 0.05),
        'g_post_mix': 1.0 + nrm(ks[6], (DEPTH, D_MODEL), 0.05),
        'g_pre_ffn': 1.0 + nrm(ks[7], (DEPTH, D_MODEL), 0.05),
        'g_post_ffn': 1.0 + nrm(ks[8], (DEPTH, D_MODEL), 0.05),
        'w_in': nrm(ks[9], (DEPTH, D_MODEL, D_IN), D_MODEL ** -0.5),
        'cmp_pe_k': nrm(ks[10], (DEPTH, CMP_LEN, HEAD_DIM), 0.02),
        'cmp_pe_v': nrm(ks[11], (DEPTH, CMP_LEN, HEAD_DIM), 0.02),
        'cmp_w1_k': nrm(ks[12], (DEPTH, CMP_LEN * HEAD_DIM, CMP_HIDDEN), (CMP_LEN * HEAD_DIM) ** -0.5),
        'cmp_w2_k': nrm(ks[13], (DEPTH, CMP_HIDDEN, HEAD_DIM), CMP_HIDDEN ** -0.5),
        'cmp_w1_v': nrm(ks[14], (DEPTH, CMP_LEN * HEAD_DIM, CMP_HIDDEN), (CMP_LEN * HEAD_DIM) ** -0.5),
        'cmp_w2_v': nrm(ks[15], (DEPTH, CMP_HIDDEN, HEAD_DIM), CMP_HIDDEN ** -0.5),
        'w_out': nrm(ks[16], (DEPTH, D_MIX, D_MODEL), D_MIX ** -0.5),
        'w_up': nrm(ks[17], (DEPTH, D_MODEL, D_FF), D_MODEL ** -0.5),
        'w_down': nrm(ks[18], (DEPTH, D_FF, D_MODEL), D_FF ** -0.5),
    }

def first_block(x, c, positions, w_ada, b_ada, g_pre_mix, g_post_mix, g_pre_ffn, g_post_ffn,
              w_in, cmp_pe_k, cmp_pe_v, cmp_w1_k, cmp_w2_k, cmp_w1_v, cmp_w2_v,
              w_out, w_up, w_down):
    B, T, _ = x.shape
    splits = np.cumsum(IN_COLS)[:-1].tolist()

    def heads(a, n):
        return a.reshape(B, T, n, -1)

    for l in range(DEPTH):
        mod = c @ w_ada[l] + b_ada[l]
        sh1, sc1, gt1, sh2, sc2, gt2 = jnp.split(mod, 6, axis=-1)

        h = rms_norm(x, g_pre_mix[l]) * (1.0 + sc1[:, None]) + sh1[:, None]
        proj = h @ w_in[l]
        (q_n, kc, vc, ksl, vsl, kw, vw, gl,
         q_d, k_d, v_d, qi, ki, wi) = jnp.split(proj, splits, axis=-1)

        o_nsa = nsa_attention(
            rope(heads(q_n, NSA_HEADS), positions),
            rope(heads(kc, NSA_KV), positions), heads(vc, NSA_KV),
            rope(heads(ksl, NSA_KV), positions), heads(vsl, NSA_KV),
            rope(heads(kw, NSA_KV), positions), heads(vw, NSA_KV),
            gl, cmp_pe_k[l], cmp_pe_v[l], cmp_w1_k[l], cmp_w2_k[l], cmp_w1_v[l], cmp_w2_v[l])

        o_dsa = dsa_attention(
            rope(heads(q_d, DSA_HEADS), positions),
            rope(k_d[:, :, None, :], positions)[:, :, 0],
            v_d,
            rope(heads(qi, IDX_HEADS), positions),
            rope(ki[:, :, None, :], positions)[:, :, 0],
            wi)

        o = jnp.concatenate([o_nsa, o_dsa], axis=-1) @ w_out[l]
        x = x + gt1[:, None] * rms_norm(o, g_post_mix[l])

        h = rms_norm(x, g_pre_ffn[l]) * (1.0 + sc2[:, None]) + sh2[:, None]
        y = jnp.square(jax.nn.relu(h @ w_up[l])) @ w_down[l]
        x = x + gt2[:, None] * rms_norm(y, g_post_ffn[l])
    return x


CHUNK = 64
D_MIX_2 = D_MODEL
SB_HEADS = 8
SB_WIDTH = SB_HEADS * HEAD_DIM
RW_WIDTH = D_MIX_2 - SB_WIDTH
RW_HEADS = RW_WIDTH // HEAD_DIM
DECAY_LORA = 64
AAA_LORA = 64
GATE_LORA = 128
RW_PROJ = 3 * RW_WIDTH + DECAY_LORA + AAA_LORA + GATE_LORA
PROJ_WIDTH = 3 * SB_WIDTH + RW_PROJ
D_FF_2 = 2816
FFN_HALF = 0.5
RMS_EPS = 1e-6
LNX_EPS = 64e-5


def rms_norm_2(x, g, eps=RMS_EPS):
    xf = x.astype(jnp.float32)
    ms = jnp.mean(xf * xf, axis=-1, keepdims=True)
    return (xf * lax.rsqrt(ms + eps) * g.astype(jnp.float32)).astype(x.dtype)

def swiglu(x, w_gate, w_up, w_down):
    return (jax.nn.silu(x @ w_gate) * (x @ w_up)) @ w_down

def token_shift(u):
    return jnp.pad(u[:, :-1], ((0, 0), (1, 0), (0, 0)))

def stick_breaking_attention(q, k, v):
    S, Dh = q.shape[1], q.shape[-1]
    scale = Dh ** -0.5
    outs = []
    for blk in range(S // Q_BLOCK):
        q0 = blk * Q_BLOCK
        kv_len = q0 + Q_BLOCK
        qb, kb, vb = q[:, q0:kv_len], k[:, :kv_len], v[:, :kv_len]
        z = jnp.einsum('bqhd,bkhd->bhqk', qb, kb).astype(jnp.float32) * scale
        q_pos = q0 + jnp.arange(Q_BLOCK)[:, None]
        k_pos = jnp.arange(kv_len)[None, :]
        mask = k_pos < q_pos
        log_beta = jax.nn.log_sigmoid(z)
        log_1m_beta = jnp.where(mask, jax.nn.log_sigmoid(-z), 0.0)
        log_remain = lax.cumsum(log_1m_beta, axis=3, reverse=True) - log_1m_beta
        att = jnp.where(mask, jnp.exp(log_beta + log_remain), 0.0)
        outs.append(jnp.einsum('bhqk,bkhd->bqhd', att.astype(vb.dtype), vb))
    return jnp.concatenate(outs, axis=1)

def rwkv7_recurrence(r, decay, k, v, a_vec, b_vec):
    B, S, H, N = r.shape
    n_chunks = S // CHUNK

    def to_chunks(t):
        return t.astype(jnp.float32).transpose(1, 0, 2, 3).reshape(n_chunks, CHUNK, B, H, N)

    xs = (to_chunks(r), to_chunks(decay), to_chunks(k), to_chunks(v),
          to_chunks(a_vec), to_chunks(b_vec))

    def step(state, inp):
        r_t, w_t, k_t, v_t, a_t, b_t = inp
        sa = jnp.einsum('bhvk,bhk->bhv', state, a_t)
        state = (state * w_t[:, :, None, :] + sa[..., None] * b_t[:, :, None, :]
                 + v_t[..., None] * k_t[:, :, None, :])
        return state, jnp.einsum('bhvk,bhk->bhv', state, r_t)

    def chunk_step(state, chunk_xs):
        return lax.scan(step, state, chunk_xs)

    state0 = jnp.zeros((B, H, N, N), jnp.float32)
    _, y = lax.scan(chunk_step, state0, xs)
    return y.reshape(S, B, H, N).transpose(1, 0, 2, 3)

def rwkv7_time_mix(u, mu, w0, w2, a0, a2, g2, k_k, k_a, r_k, ln_w, ln_b):
    B, S, _ = u.shape
    u = u + (token_shift(u) - u) * mu
    x_r, x_k, x_v, x_w, x_a, x_g = jnp.split(
        u, [RW_WIDTH, 2 * RW_WIDTH, 3 * RW_WIDTH, 3 * RW_WIDTH + DECAY_LORA,
            3 * RW_WIDTH + DECAY_LORA + AAA_LORA], axis=-1)
    log_w = -jax.nn.softplus(-(w0 + jnp.tanh(x_w) @ w2)) - 0.5
    decay = jnp.exp(-jnp.exp(log_w.astype(jnp.float32)))
    a = jax.nn.sigmoid(a0 + x_a @ a2).astype(jnp.float32)
    g = jax.nn.sigmoid(x_g) @ g2

    def heads(t):
        return t.reshape(B, S, RW_HEADS, HEAD_DIM)

    r = heads(x_r).astype(jnp.float32)
    v = heads(x_v).astype(jnp.float32)
    kk = heads(x_k * k_k).astype(jnp.float32)
    kk = kk / jnp.maximum(jnp.linalg.norm(kk, axis=-1, keepdims=True), 1e-12)
    kf = heads(x_k * (1.0 + (a - 1.0) * k_a)).astype(jnp.float32)
    a = heads(a)
    y = rwkv7_recurrence(r, heads(decay), kf, v, -kk, kk * a)
    mean = jnp.mean(y, axis=-1, keepdims=True)
    var = jnp.mean(jnp.square(y - mean), axis=-1, keepdims=True)
    yn = (y - mean) * lax.rsqrt(var + LNX_EPS)
    yn = yn * ln_w.astype(jnp.float32).reshape(RW_HEADS, HEAD_DIM) + ln_b.astype(jnp.float32).reshape(RW_HEADS, HEAD_DIM)
    bonus = jnp.sum(r * kf * r_k.astype(jnp.float32), axis=-1, keepdims=True) * v
    return ((yn + bonus).reshape(B, S, RW_WIDTH) * g.astype(jnp.float32)).astype(u.dtype)

def second_inputs(seed: int = 0) -> dict:
    key = jax.random.key(seed)
    ks = jax.random.split(key, 26)
    L, D = DEPTH, D_MODEL
    f32 = jnp.float32

    def nrm(k, shape, scale):
        return scale * jax.random.normal(k, shape, f32)

    def gain(k, shape):
        return 1.0 + 0.05 * jax.random.normal(k, shape, f32)

    return {
        "x": jax.random.normal(ks[0], (BATCH, SEQ, D), f32),
        "norm_ffn1": gain(ks[1], (L, D)),
        "ffn1_gate": nrm(ks[2], (L, D, D_FF_2), D ** -0.5),
        "ffn1_up": nrm(ks[3], (L, D, D_FF_2), D ** -0.5),
        "ffn1_down": nrm(ks[4], (L, D_FF_2, D), D_FF_2 ** -0.5),
        "norm_mix": gain(ks[5], (L, D)),
        "w_in": nrm(ks[6], (L, D, PROJ_WIDTH), D ** -0.5),
        "sb_q_norm": gain(ks[7], (L, HEAD_DIM)),
        "sb_k_norm": gain(ks[8], (L, HEAD_DIM)),
        "sb_out_norm": gain(ks[9], (L, SB_WIDTH)),
        "rw_mu": jax.random.uniform(ks[10], (L, RW_PROJ), f32),
        "rw_w0": jax.random.uniform(ks[11], (L, RW_WIDTH), f32, minval=-5.0, maxval=-1.0),
        "rw_w2": nrm(ks[12], (L, DECAY_LORA, RW_WIDTH), 0.5 * DECAY_LORA ** -0.5),
        "rw_a0": nrm(ks[13], (L, RW_WIDTH), 0.1),
        "rw_a2": nrm(ks[14], (L, AAA_LORA, RW_WIDTH), 0.5 * AAA_LORA ** -0.5),
        "rw_g2": nrm(ks[15], (L, GATE_LORA, RW_WIDTH), GATE_LORA ** -0.5),
        "rw_k_k": 0.85 + 0.05 * jax.random.normal(ks[16], (L, RW_WIDTH), f32),
        "rw_k_a": gain(ks[17], (L, RW_WIDTH)),
        "rw_r_k": nrm(ks[18], (L, RW_HEADS, HEAD_DIM), 0.1),
        "rw_ln_w": gain(ks[19], (L, RW_WIDTH)),
        "rw_ln_b": nrm(ks[20], (L, RW_WIDTH), 0.01),
        "w_out": nrm(ks[21], (L, D_MIX_2, D), D_MIX_2 ** -0.5),
        "norm_ffn2": gain(ks[22], (L, D)),
        "ffn2_gate": nrm(ks[23], (L, D, D_FF_2), D ** -0.5),
        "ffn2_up": nrm(ks[24], (L, D, D_FF_2), D ** -0.5),
        "ffn2_down": nrm(ks[25], (L, D_FF_2, D), D_FF_2 ** -0.5),
    }

def second_block(x, norm_ffn1, ffn1_gate, ffn1_up, ffn1_down, norm_mix, w_in,
              sb_q_norm, sb_k_norm, sb_out_norm, rw_mu, rw_w0, rw_w2, rw_a0, rw_a2,
              rw_g2, rw_k_k, rw_k_a, rw_r_k, rw_ln_w, rw_ln_b, w_out, norm_ffn2,
              ffn2_gate, ffn2_up, ffn2_down):
    B, S, _ = x.shape
    for l in range(DEPTH):
        x = x + FFN_HALF * swiglu(rms_norm_2(x, norm_ffn1[l]), ffn1_gate[l], ffn1_up[l], ffn1_down[l])

        h = rms_norm_2(x, norm_mix[l])
        p = h @ w_in[l]
        sb_q, sb_k, sb_v, rw_in = jnp.split(p, [SB_WIDTH, 2 * SB_WIDTH, 3 * SB_WIDTH], axis=-1)

        q = rms_norm_2(sb_q.reshape(B, S, SB_HEADS, HEAD_DIM), sb_q_norm[l])
        k = rms_norm_2(sb_k.reshape(B, S, SB_HEADS, HEAD_DIM), sb_k_norm[l])
        v = sb_v.reshape(B, S, SB_HEADS, HEAD_DIM)
        o_sb = stick_breaking_attention(q, k, v)
        o_sb = rms_norm_2(o_sb, sb_out_norm[l].reshape(SB_HEADS, HEAD_DIM)).reshape(B, S, SB_WIDTH)

        o_rw = rwkv7_time_mix(rw_in, rw_mu[l], rw_w0[l], rw_w2[l], rw_a0[l], rw_a2[l], rw_g2[l],
                              rw_k_k[l], rw_k_a[l], rw_r_k[l], rw_ln_w[l], rw_ln_b[l])

        x = x + jnp.concatenate([o_sb, o_rw], axis=-1) @ w_out[l]

        x = x + FFN_HALF * swiglu(rms_norm_2(x, norm_ffn2[l]), ffn2_gate[l], ffn2_up[l], ffn2_down[l])
    return x


def setup_inputs(seed=0):
    out = dict(first_inputs(seed))
    for name, value in second_inputs(seed + 1).items():
        if name != "x":
            out[name + "_2"] = value
    return out


def reference(
    x, c, positions, w_ada, b_ada, g_pre_mix, g_post_mix, g_pre_ffn, g_post_ffn, w_in, cmp_pe_k,
    cmp_pe_v, cmp_w1_k, cmp_w2_k, cmp_w1_v, cmp_w2_v, w_out, w_up, w_down, norm_ffn1_2,
    ffn1_gate_2, ffn1_up_2, ffn1_down_2, norm_mix_2, w_in_2, sb_q_norm_2, sb_k_norm_2,
    sb_out_norm_2, rw_mu_2, rw_w0_2, rw_w2_2, rw_a0_2, rw_a2_2, rw_g2_2, rw_k_k_2, rw_k_a_2,
    rw_r_k_2, rw_ln_w_2, rw_ln_b_2, w_out_2, norm_ffn2_2, ffn2_gate_2, ffn2_up_2, ffn2_down_2,
):
    x = first_block(
        x, c, positions, w_ada, b_ada, g_pre_mix, g_post_mix, g_pre_ffn, g_post_ffn, w_in,
        cmp_pe_k, cmp_pe_v, cmp_w1_k, cmp_w2_k, cmp_w1_v, cmp_w2_v, w_out, w_up, w_down,
    )
    return second_block(
        x, norm_ffn1_2, ffn1_gate_2, ffn1_up_2, ffn1_down_2, norm_mix_2, w_in_2, sb_q_norm_2,
        sb_k_norm_2, sb_out_norm_2, rw_mu_2, rw_w0_2, rw_w2_2, rw_a0_2, rw_a2_2, rw_g2_2,
        rw_k_k_2, rw_k_a_2, rw_r_k_2, rw_ln_w_2, rw_ln_b_2, w_out_2, norm_ffn2_2, ffn2_gate_2,
        ffn2_up_2, ffn2_down_2,
    )


_drawn_inputs = setup_inputs


def setup_inputs(seed=0):
    import zlib

    import numpy as np

    out = dict(_drawn_inputs(seed))
    spreads = {}
    factors = {'g_pre_mix': 3.514,
     'g_post_mix': 7.688,
     'g_pre_ffn': 7.948,
     'g_post_ffn': 8.0,
     'cmp_pe_k': 8.0,
     'cmp_pe_v': 8.0,
     'sb_q_norm_2': 4.452,
     'sb_k_norm_2': 4.538,
     'rw_w2_2': 5.89,
     'rw_a0_2': 4.841,
     'rw_k_k_2': 4.789,
     'rw_k_a_2': 3.57,
     'rw_ln_w_2': 3.69,
     'rw_ln_b_2': 21.807,
     'norm_ffn2_2': 3.744,
     'sb_out_norm_2': 2.81}
    for name, (base, spread) in spreads.items():
        noise = np.random.default_rng([zlib.crc32(name.encode()), seed]).standard_normal(out[name].shape)
        drawn = base * np.exp(spread * noise) if base else spread * noise
        out[name] = __import__('jax').numpy.asarray(drawn.astype(out[name].dtype))
    for name, factor in factors.items():
        out[name] = (out[name] * factor).astype(out[name].dtype)
    return out
```

```python
from contextlib import ExitStack

import numpy as np

import concourse.bass as bass
from concourse import mybir

F32 = mybir.dt.float32
I32 = mybir.dt.int32
ALU = mybir.AluOpType
ACT = mybir.ActivationFunctionType
AX = mybir.AxisListType

P = 128
T = 512
D = 1024
KD = D // P
NT = T // P
DH = 64
HEADS = 8
FF1 = 4096
FF2 = 2816
NEG = 1e30
EPS = 1e-6
LNX_EPS = 64e-5
TOPK = 128
ROUNDS = TOPK // 8
CMP_N = 32
CMP_L = 32
CHUNK = 64
NCH = T // CHUNK
DECAY = float(np.exp(np.float32(-0.5)))
TWO_PI_INV = float(np.float32(1.0 / (2.0 * np.pi)))
PI_A = 6.28125
PI_B = float(np.float32(1.9353071795e-3) - np.float32(1.9353071795e-3) % np.float32(2.0 ** -21))
PI_C = float(2.0 * np.pi - PI_A - PI_B)
MAGIC = 12582912.0
PI_SAFE = 3.1415925

CONST = {}
_parts = []


def _const(name, a):
    at = sum(x.shape[1] for x in _parts)
    CONST[name] = (at, at + a.shape[1])
    _parts.append(np.asarray(a, np.float32))


_i = np.arange(P)
_eye = np.eye(P, dtype=np.float32)
_const("ident", _eye)
_const("ones", np.ones((P, P)))
_const("pair", (_i[:, None] // DH == _i[None, :] // DH))
_const("turn", np.where(_i[None, :] % DH < 32, -(_i[:, None] == _i[None, :] + 32).astype(np.float32),
                        (_i[:, None] == _i[None, :] - 32).astype(np.float32)))
_const("causal", np.concatenate([np.zeros((P, T - P)), NEG * (_i[None, :] > _i[:, None])], 1))
_ends = np.arange(CMP_N) * 16 + CMP_L - 1
_cm = np.stack([(_ends[None, :] <= (t * P + _i)[:, None]) for t in range(NT)], 1).astype(np.float32)
_const("cmp_keep", _cm.reshape(P, -1))
_const("cmp_drop", (NEG * (1.0 - _cm)).reshape(P, -1))
_same = _i[:, None] // CHUNK == _i[None, :] // CHUNK
_lt = (_same & (_i[:, None] < _i[None, :])).astype(np.float32)
_le = (_same & (_i[:, None] <= _i[None, :])).astype(np.float32)
_const("chunk4", np.concatenate([_lt, _le, _lt, _le], 1))
_const("chunkT", _lt.T)
_const("suffix", -(_i[:, None] >= _i[None, :]).astype(np.float32))
_const("minus", -np.ones((P, P)))
_const("before", (_i[:, None] < _i[None, :]))
_const("notbefore", np.concatenate([-NEG * (_i[:, None] >= _i[None, :]), np.zeros((P, T - P))], 1))
_const("ident64", (_i[:, None] % DH == np.arange(DH)[None, :]))
_half = np.float32(10000.0) ** (-np.arange(32, dtype=np.float32) / np.float32(32))
_const("inv", np.tile(_half, 4)[:, None])
CONSTS = np.ascontiguousarray(np.concatenate(_parts, 1), np.float32)
NCONST = CONSTS.shape[1]

COLS = {}
_at = 0
for _name, _n in [("c", 8), ("b_ada", 48), ("g_pre_mix", 8), ("g_post_mix", 8), ("g_pre_ffn", 8),
                  ("g_post_ffn", 8), ("norm_ffn1_2", 8), ("norm_mix_2", 8), ("norm_ffn2_2", 8),
                  ("sb_q", 1), ("sb_k", 1), ("sb_out", 4), ("rw_mu", 14), ("rw_w0", 4), ("rw_a0", 4),
                  ("rw_k_k", 4), ("rw_k_a", 4), ("rw_r_k", 4), ("rw_ln_w", 4), ("rw_ln_b", 4),
                  ("pe_k", 32), ("pe_v", 32)]:
    COLS[_name] = (_at, _at + _n)
    _at += _n
NCOLS = _at

SLOT = 11 * P
RING = 8
VCOLS = 348
ADA = 512
NADA = 6 * D // ADA


def weight_stream():
    out = [("w_v", n, 4 * VCOLS) for n in range(2)]
    out += [("w_in", n, 8 * P) for n in range(16)]
    out += [("cmp1k", n, SLOT) for n in range(3)] + [("cmp1v", n, SLOT) for n in range(3)]
    out += [("w_out", n, 8 * P) for n in range(8)]
    out += [("w_up", n, 8 * P) for n in range(FF1 // P)]
    out += [("w_down", n, 8 * P) for n in range(4 * 8)]
    for m in ("1", "2"):
        out += [(w + m, n, 8 * P) for n in range(FF2 // P) for w in ("gate", "up")]
        out += [("down" + m, n, 11 * P) for n in range(2 * 8)]
        if m == "1":
            out += [("w_in2", n, 8 * P) for n in range(8)]
            out += [("w_v2", n, 2 * T) for n in range(4)]
            out += [("w_in2", n, 8 * P) for n in range(8, 22)]
            out += [("w_out2", n, 8 * P) for n in range(8)]
    return out


STREAM = weight_stream()


def build(nc, xt, consts, cols, pos, ada, mats, extra, out, stop=99, dumps=None):
    ctx = ExitStack()
    with ctx:
        sems = {}

        def S(name):
            if name not in sems:
                sems[name] = ctx.enter_context(nc.semaphore(name))
            return sems[name]

        def sb(name, shape, dt=F32):
            return ctx.enter_context(nc.sbuf_tensor(name, shape, dt))

        x = sb("x", [P, KD, T])
        h = sb("h", [P, KD, T])
        ring = sb("ring", [P, RING, SLOT])
        cst = sb("cst", [P, NCONST])
        col = sb("col", [P, NCOLS])
        ext = sb("ext", [P, 2 * T + 2 * DH])
        arena = sb("arena", [P, 23 * 1024])
        mod = sb("mod", [P, 48])
        gain = sb("gain", [P, 32])
        gates = sb("gates", [P, NT, 24])
        widx = sb("widx", [P, NT, 4])
        best8 = sb("best8", [P, 8])
        smin = sb("smin", [P, 3])
        ssum = sb("ssum", [P, 2, HEADS])
        coef = sb("coef", [P, HEADS])
        coef2 = sb("coef2", [P, HEADS])
        cmin = sb("cmin", [P, HEADS])
        epsc = sb("epsc", [P, 3])
        sbg = sb("sbg", [P, 2])
        omka = sb("omka", [P, 4])
        ends = sb("ends", [P, 4, NCH])
        ropein = sb("ropein", [P, 2, T])
        ropet = sb("ropet", [P, 2, T])
        relu_t = sb("relu_t", [P, 2, T])
        bank = ctx.enter_context(nc.psum_tensor("bank", [P, 8, T], F32))

        def const(name):
            a, b = CONST[name]
            return cst[:, a:b]

        def vec(name, i=0, n=1):
            return col[:, COLS[name][0] + i:COLS[name][0] + i + n]

        def area(at, shape):
            n = int(np.prod(shape))
            v = arena[:, at:at + n]
            if len(shape) == 2:
                v = v.rearrange("p (a b) -> p a b", a=shape[0])
            if len(shape) == 3:
                v = v.rearrange("p (a b c) -> p a b c", a=shape[0], b=shape[1])
            if len(shape) == 4:
                v = v.rearrange("p (a b c d) -> p a b c d", a=shape[0], b=shape[1], c=shape[2])
            return v

        K = 1024 // 4
        ada_in = area(0, (2, KD, ADA))
        ada_acc = area(32 * K, (2, ADA))
        proj = area(36 * K, (16, T))
        cos, sin = area(68 * K, (T,)), area(70 * K, (T,))
        vtok = area(72 * K, (NT, VCOLS))
        score = area(78 * K, (3, T))
        choose = area(84 * K, (3, T))
        QI, KI, QD, KDD, KC, VC, KSL, KW, QN = 0, 2, 3, 7, 8, 9, 10, 11, 12
        sneg = area(0, (3, T))
        prob = area(6 * K, (3, T))
        probT = area(12 * K, (3, T))
        otok = area(18 * K, (2, D))
        blk = area(26 * K, (CMP_L, CMP_N))
        hidc = area(30 * K, (2, 2, CMP_N))
        kcmp = area(30 * K + 128, (CMP_N,))
        vcmp = area(31 * K, (2, 4 * DH))
        cs = area(33 * K, (2, HEADS, CMP_N))
        cpt = area(35 * K, (2, P))
        hid = area(0, (32, T))
        sq = area(64 * K, (KD, T))
        ftmp = area(80 * K, (2, T))
        rstd = area(84 * K, (T,))
        root_ms = area(86 * K, (T,))
        ybuf = area(36 * K, (KD, T))
        qk2 = area(0, (8, T))
        vtok2 = area(16 * K, (NT, T))
        AT0 = (0, 512, 896, 1152)
        sp = area(24 * K, (2, 1280))
        att = area(34 * K, (2, 1280))
        u = area(44 * K, (14, T))
        ztmp = area(72 * K, (3, T))
        osb = area(78 * K, (4, T))
        shift = area(86 * K, (2, T))
        ar = area(0, (4, NT, 2, P))
        bt, kt = area(16 * K, (4, T)), area(24 * K, (4, T))
        sg, csum, e1, e2, e3, av = [area((32 + 2 * i) * K, (T,)) for i in range(6)]
        AT = area(32 * K, (4, 4 * P))
        Z = area(44 * K, (4, P))
        MT = area(48 * K, (2, 4, DH))
        St = area(50 * K, (2, 4, DH))
        PP = area(52 * K, (2, 2, 4 * P))
        vtk = area(72 * K, (NT, T))
        tok3 = area(80 * K, (3, T))
        reset = area(90 * K, (T,))
        UR, UK, UV, UWA, UG = 0, 4, 8, 12, 13
        RW_ORDER = [12] + list(range(4, 8)) + list(range(0, 4)) + list(range(8, 12)) + [13]

        jobs = [(t, br, hh) for t in range(NT) for br in range(3) for hh in range(HEADS)]
        steps = [(hh, c) for hh in range(HEADS) for c in (3, 2, 1, 0)]
        SLOTS = 14
        slot_steps = [list(range(3 * n, min(3 * n + 3, 32))) for n in range(SLOTS)]

        NORMS = ["pre1", "post1", "f1", "post2", "g1", "mix", "g2"]
        HNORMS = ["pre1", "f1", "g1", "mix", "g2"]
        NG = FF2 // P
        last = {}
        tile_done = []
        block = ctx.enter_context(nc.Block())

        @block.tensor
        def _(pe):
            def claim(b, sem, value):
                if b in last:
                    pe.wait_ge(*last[b])
                last[b] = (S(sem), value)

            def take(name, sem, value):
                i = len(tile_done)
                assert STREAM[i][0] == name, (STREAM[i], name)
                tile_done.append((S(sem), value))
                pe.wait_ge(S(f"slot{i % RING}"), 16 * (i // RING + 1))
                return ring[:, i % RING, 0:STREAM[i][2]]

            def gemm(name, b, kc, parts, src, full, value, ready=None):
                for part in range(parts):
                    w = take(name, full, value).rearrange("p (k m) -> p k m", m=P)
                    for k in range(kc // parts):
                        kk = part * (kc // parts) + k
                        if ready:
                            pe.wait_ge(S("h"), KD * HNORMS.index(ready) + kk + 1)
                        mm = pe.matmul(bank[:, b, :], w[:, k, :], src[:, kk, :], start=(kk == 0), stop=(kk == kc - 1))
                mm.then_inc(S(full), 1)

            def sumsq(tag, k, src=sq):
                pe.wait_ge(S("sq"), KD * NORMS.index(tag) + k + 1)
                mm = pe.matmul(bank[:, 4, :], const("ones"), src[:, k, :], start=(k == 0), stop=(k == KD - 1))
                if k == KD - 1:
                    mm.then_inc(S("ms"), 1)

            def norm(tag, src=sq):
                claim(4, "rms", NORMS.index(tag) + 1)
                for k in range(KD):
                    sumsq(tag, k, src)

            def ada_cols(i):
                pe.wait_ge(S("ada_acc"), i + 1)
                claim(7, "mod", i + 1)
                for j in range(4):
                    mm = pe.matmul(bank[:, 7, 4 * i + j:4 * i + j + 1], ada_acc[:, i % 2, j * P:(j + 1) * P],
                                   const("ones")[:, 0:1], start=True, stop=True)
                mm.then_inc(S("ada_cols"), 1)

            pe.wait_ge(S("consts"), 16)
            norm("pre1", h)
            for i in range(4):
                ada_cols(i)
            ws = [take("w_v", "vtok_full", 4).rearrange("p (k m) -> p k m", m=VCOLS) for _ in range(2)]
            for t in range(NT):
                claim(t, "vtok", t + 1)
                for k in range(KD):
                    if t == 0:
                        pe.wait_ge(S("h"), k + 1)
                    mm = pe.matmul(bank[:, t, 0:VCOLS], h[:, k, t * P:(t + 1) * P], ws[k // 4][:, k % 4, :],
                                   start=(k == 0), stop=(k == KD - 1))
                mm.then_inc(S("vtok_full"), 1)

            def turn(n):
                pe.wait_ge(S("ropein"), n + 1)
                if n == VC:
                    return
                claim(4 + n % 2, "roped", n + 1)
                pe.matmul(bank[:, 4 + n % 2, :], const("turn"), ropein[:, n % 2, :], start=True, stop=True)\
                  .then_inc(S("turned"), 1)

            def logits(j):
                t, i = 1 + j // 4, j % 4
                pe.wait_ge(S("roped"), 3)
                claim(6, "relu_logits", j + 1)
                b = 64 * (i % 2)
                pe.matmul(bank[:, 6, 0:(t + 1) * P], proj[b:b + DH, QI + i // 2, t * P:(t + 1) * P],
                          proj[b:b + DH, KI, 0:(t + 1) * P], start=True, stop=True).then_inc(S("logits"), 1)

            for n in range(16):
                claim(n % 4, "ropein", n + 1)
                gemm("w_in", n % 4, KD, 1, h, "proj_full", n + 1)
                if n >= 1:
                    turn(n - 1)
                if 4 <= n < 7:
                    for j in range(4):
                        logits(4 * (n - 4) + j)
                if 2 <= n < 10:
                    ada_cols(n + 2)
            turn(15)
            if stop < 2:
                return
            for m, name in enumerate(("cmp1k", "cmp1v")):
                ws = [take(name, "cmp_hid", m + 1).rearrange("p (l m) -> p l m", m=P) for _ in range(3)]
                pe.wait_ge(S("cmp_blocks"), m + 1)
                for g in range(2):
                    claim(2 * m + g, "cmp_gelu", 2 * m + g + 1)
                for l in range(CMP_L):
                    for g in range(2):
                        mm = pe.matmul(bank[:, 2 * m + g, 0:CMP_N],
                                       ws[l // 11][64 * g:64 * g + DH, l % 11, :], blk[64 * g:64 * g + DH, l, :],
                                       start=(l == 0), stop=(l == CMP_L - 1))
                mm.then_inc(S("cmp_hid"), 1)
            pe.wait_ge(S("cmp_gelu"), 4)
            claim(5, "cmp_kv", 1)
            for g in range(2):
                pe.matmul(bank[64 * g:64 * g + DH, 5, 0:CMP_N], ext[:, 2 * T:2 * T + DH], hidc[:, 0, g, :],
                          start=True, stop=True)
                for i in range(4):
                    mm = pe.matmul(bank[32 * i:32 * i + CMP_N, 5, 64 + 64 * g:128 + 64 * g], hidc[:, 1, g, :],
                                   ext[:, 2 * T + DH:2 * T + 2 * DH], start=True, stop=True)
            mm.then_inc(S("cmp_out"), 1)
            if stop < 3:
                return

            def qk(j):
                t, br, hh = jobs[j]
                kv = (t + 1) * P
                b = 64 * (hh // 4) if br < 2 else 64 * (hh % 2)
                q = QN + hh % 4 if br < 2 else QD + hh // 2
                claim(j % 3, "smin", j + 1)
                pe.matmul(bank[:, j % 3, 0:kv], proj[b:b + DH, q, t * P:(t + 1) * P],
                          proj[b:b + DH, (KSL, KW, KDD)[br], 0:kv], start=True, stop=True).then_inc(S("scores"), 1)

            def turn_probs(j):
                pe.wait_ge(S("probs"), j + 1)
                claim(3 + j % 2, "probT", j + 1)
                for i in range(jobs[j][0] + 1):
                    mm = pe.transpose(bank[:, 3 + j % 2, i * P:(i + 1) * P], prob[:, j % 3, i * P:(i + 1) * P],
                                      const("ident"))
                mm.then_inc(S("probs_turned"), 1)

            def pv(j):
                t, br, hh = jobs[j]
                vc = ((hh // 4) * DH, P + (hh // 4) * DH, 2 * P)[br]
                pe.wait_ge(S("probT"), j + 1)
                o = 3 * t + br
                if hh == 0:
                    claim(5 + o % 2, "otok", o + 1)
                for i in range(t + 1):
                    mm = pe.matmul(bank[:, 5 + o % 2, hh * DH:(hh + 1) * DH], probT[:, j % 3, i * P:(i + 1) * P],
                                   vtok[:, i, vc:vc + DH], start=(i == 0), stop=(i == t))
                mm.then_inc(S("pv"), 1)

            def cmp_scores(t):
                claim(7, "cmp_masked", t + 1)
                for hh in range(HEADS):
                    b = 64 * (hh // 4)
                    mm = pe.matmul(bank[:, 7, hh * CMP_N:(hh + 1) * CMP_N],
                                   proj[b:b + DH, QN + hh % 4, t * P:(t + 1) * P], kcmp[b:b + DH, :],
                                   start=True, stop=True)
                    if hh == 3:
                        mm.then_inc(S("cmp_half"), 1)
                        pe.wait_ge(S("cmp_half"), t + 1)
                mm.then_inc(S("cmp_scores"), 1)

            def cmp_turn(t):
                pe.wait_ge(S("cmp_probs"), t + 1)
                claim(7, "cmp_probT", t + 1)
                for g in range(2):
                    mm = pe.transpose(bank[:, 7, g * P:(g + 1) * P],
                                      cs[:, 1, 4 * g:4 * g + 4, :].rearrange("p a b -> p (a b)"), const("ident"))
                mm.then_inc(S("cmp_turned"), 1)

            def cmp_out(t):
                pe.wait_ge(S("cmp_probT"), t + 1)
                claim(7, "cmp_otok", t + 1)
                for g in range(2):
                    mm = pe.matmul(bank[:, 7, g * 256:(g + 1) * 256], cpt[:, g, :], vcmp[:, g, :],
                                   start=True, stop=True)
                mm.then_inc(S("cmp_pv"), 1)

            def turn_out(t):
                pe.wait_ge(S("otok"), 3 * t + 3)
                for half in range(2):
                    claim(7, "oT", 2 * t + half + 1)
                    for c in range(4):
                        mm = pe.transpose(bank[:, 7, c * P:(c + 1) * P],
                                          otok[:, t % 2, (4 * half + c) * P:(4 * half + c + 1) * P], const("ident"))
                    mm.then_inc(S("out_turned"), 1)

            pe.wait_ge(S("cmp_kv"), 1)
            pe.wait_ge(S("roped"), 16)
            n = len(jobs)
            for j in range(n + 3):
                if j < n:
                    qk(j)
                    if j % 24 == 0:
                        cmp_scores(j // 24)
                    if j % 24 == 4:
                        cmp_turn(j // 24)
                    if j % 24 == 7:
                        cmp_out(j // 24)
                if 2 <= j < n + 2:
                    turn_probs(j - 2)
                if 3 <= j:
                    pv(j - 3)
                if j >= 24 and j % 24 == 11:
                    turn_out(j // 24 - 1)
            turn_out(NT - 1)
            if stop < 4:
                return

            def post_gemm(tag, name, kc, parts, src, ready, count):
                claim(4, "rms", NORMS.index("post" + tag) + 1)
                pe.wait_ge(S(ready), count)
                for n in range(KD):
                    v = KD * (int(tag) - 1) + n + 1
                    claim(n % 4, "y_read", v)
                    gemm(name, n % 4, kc, parts, src, "y_full", v)
                    if n >= 1:
                        sumsq("post" + tag, n - 1)
                sumsq("post" + tag, KD - 1)

            post_gemm("1", "w_out", KD, 1, h, "oT", 2 * NT)
            norm("f1")
            if stop < 5:
                return
            for n in range(FF1 // P):
                claim(n % 4, "relu", n + 1)
                gemm("w_up", n % 4, KD, 1, h, "up_full", n + 1, "f1" if n == 0 else None)
            post_gemm("2", "w_down", FF1 // P, 4, hid, "hid", FF1 // P)
            norm("g1")
            if stop < 6:
                return

            def swiglu_up(m):
                for n in range(FF2 // P):
                    b = 2 * (n % 2)
                    v = NG * (int(m) - 1) + n + 1
                    claim(b, "silu", v)
                    gemm("gate" + m, b, KD, 1, h, "gate_full", v, "g" + m if n == 0 else None)
                    claim(b + 1, "gated", v)
                    gemm("up" + m, b + 1, KD, 1, h, "gate_up_full", v)
                pe.wait_ge(S("gated"), NG * int(m))

            swiglu_up("1")
            claim(4, "rms", NORMS.index("mix") + 1)
            for n in range(KD):
                claim(n % 4, "x_added", n + 1)
                gemm("down1", n % 4, FF2 // P, 2, hid, "add_full", n + 1)
                if n >= 1:
                    sumsq("mix", n - 1)
            sumsq("mix", KD - 1)
            if stop < 7:
                return

            def head_norm(n):
                pe.wait_ge(S("qk_sq"), n + 1)
                claim(4 + n % 2, "qk_root", n + 1)
                pe.matmul(bank[:, 4 + n % 2, :], const("pair"), ropein[:, n % 2, :], start=True, stop=True)\
                  .then_inc(S("qk_ms"), 1)

            for n in range(8):
                claim(n % 4, "qk2", n + 1)
                gemm("w_in2", n % 4, KD, 1, h, "qk_full", n + 1, "mix" if n == 0 else None)
                if n >= 1:
                    head_norm(n - 1)
            head_norm(7)
            ws = [take("w_v2", "vtok2_full", 4).rearrange("p (k m) -> p k m", m=T) for _ in range(4)]
            for t in range(NT):
                claim(t, "vtok2", t + 1)
                for k in range(KD):
                    mm = pe.matmul(bank[:, t, :], h[:, k, t * P:(t + 1) * P], ws[k // 2][:, k % 2, :],
                                   start=(k == 0), stop=(k == KD - 1))
                mm.then_inc(S("vtok2_full"), 1)
            if stop < 8:
                return

            def sb_scores(s):
                hh, c = steps[s]
                b = 64 * (hh % 2)
                claim(2 + s % 3, "att_copy", s + 1)
                pe.matmul(bank[:, 2 + s % 3, 0:T - c * P], qk2[b:b + DH, 4 + hh // 2, c * P:(c + 1) * P],
                          qk2[b:b + DH, hh // 2, c * P:T], start=True, stop=True).then_inc(S("sb_scores"), 1)

            def sb_suffix(s):
                hh, c = steps[s]
                pe.wait_ge(S("softplus"), s + 1)
                w = T - c * P
                mm = pe.matmul(bank[:, 2 + s % 3, 0:w], const("suffix"), sp[:, hh % 2, AT0[c]:AT0[c] + w],
                               start=False, stop=(c == 3), skip_group_check=True)
                for cc in range(c + 1, NT):
                    ww = T - cc * P
                    mm = pe.matmul(bank[:, 2 + s % 3, w - ww:w], const("minus"), sp[:, hh % 2, AT0[cc]:AT0[cc] + ww],
                                   start=False, stop=(cc == NT - 1), skip_group_check=True)
                mm.then_inc(S("sb_suffix"), 1)

            def sb_pv(hh):
                pe.wait_ge(S("att"), 4 * hh + 4)
                b, o = 64 * (hh % 2), 5 + (hh // 2) % 2
                if hh % 2 == 0:
                    claim(o, "osb", hh // 2 + 1)
                for c in range(NT):
                    mm = pe.matmul(bank[b:b + DH, o, c * P:T], vtok2[:, c, hh * DH:(hh + 1) * DH],
                                   att[:, hh % 2, AT0[c]:AT0[c] + T - c * P], start=(c == 0), stop=(c == NT - 1),
                                   skip_group_check=True)
                mm.then_inc(S("sb_pv"), 1)

            pe.wait_ge(S("qk2"), 8)
            pe.wait_ge(S("vtok2"), NT)
            for n in range(SLOTS):
                for s in slot_steps[n]:
                    sb_scores(s)
                claim(n % 2, "u_raw", n + 1)
                gemm("w_in2", n % 2, KD, 1, h, "u_full", n + 1)
                if n >= 1:
                    for s in slot_steps[n - 1]:
                        if s % 4 == 3:
                            sb_pv(s // 4)
                for s in slot_steps[n]:
                    sb_suffix(s)
            if stop < 9:
                return
            for n in range(4):
                pe.wait_ge(S("osb_sq"), n + 1)
                claim(2 + n % 2, "osb_root", n + 1)
                pe.matmul(bank[:, 2 + n % 2, :], const("pair"), ropein[:, n % 2, :], start=True, stop=True)\
                  .then_inc(S("osb_ms"), 1)
            pe.wait_ge(S("shifted"), 14)
            for t in range(NT):
                claim(4 + t % 2, "vtk", t + 1)
                for c in range(4):
                    mm = pe.transpose(bank[:, 4 + t % 2, c * P:(c + 1) * P], u[:, UV + c, t * P:(t + 1) * P],
                                      const("ident"))
                mm.then_inc(S("v_turned"), 1)
            pe.wait_ge(S("tanh"), 1)
            for c in range(4):
                claim(0, "sg", c + 1)
                pe.matmul(bank[:, 0, :], ext[0:DH, c * P:(c + 1) * P], u[0:DH, UWA, :], start=True, stop=True)\
                  .then_inc(S("w_full"), 1)
                claim(1, "av", c + 1)
                pe.matmul(bank[:, 1, :], ext[DH:P, c * P:(c + 1) * P], u[DH:P, UWA, :], start=True, stop=True)\
                  .then_inc(S("a_full"), 1)
                pe.wait_ge(S("kk_sq"), c + 1)
                claim(6, "kk_root", c + 1)
                pe.matmul(bank[:, 6, :], const("pair"), ropein[:, 1, :], start=True, stop=True)\
                  .then_inc(S("kk_ms"), 1)
                pe.wait_ge(S("rkr"), c + 1)
                claim(7, "bonus", c + 1)
                pe.matmul(bank[:, 7, :], const("pair"), ropet[:, 1, :], start=True, stop=True)\
                  .then_inc(S("bonus_full"), 1)
            if stop < 10:
                return
            pe.wait_ge(S("wkv_in"), 4)
            pe.wait_ge(S("vtk"), NT)
            pe.wait_ge(S("state0"), 1)

            def head_at(hf, i):
                hh = 4 * hf + i
                return hh, hh // 2, 64 * (hh % 2)

            for w in range(NT):
                for i, src in enumerate(("a", "b", "k")):
                    claim(5 + i, "tok3", 3 * w + i + 1)
                    for c in range(4):
                        f = ar[:, c, w, 0, :] if i == 0 else (bt, kt)[i - 1][:, c, w * P:(w + 1) * P]
                        mm = pe.transpose(bank[:, 5 + i, c * P:(c + 1) * P], f, const("ident"))
                    mm.then_inc(S("tok3_full"), 1)
                for hf in range(2):
                    g = 2 * w + hf
                    for i in range(4):
                        hh, c, b = head_at(hf, i)
                        claim(i, "pairs", 4 * g + i + 1)
                        arw = ar[b:b + DH, c, w, :, :].rearrange("p a t -> p (a t)")
                        pe.matmul(bank[:, i, 0:256], bt[b:b + DH, c, w * P:(w + 1) * P], arw, start=True, stop=True)
                        pe.matmul(bank[:, i, 256:512], kt[b:b + DH, c, w * P:(w + 1) * P], arw,
                                  start=True, stop=True).then_inc(S("pairs_full"), 1)
                    claim(4, "power", 5 * g + 1)
                    claim(7, "power", 5 * g + 1)
                    for i in range(4):
                        hh, c, b = head_at(hf, i)
                        mm = pe.matmul(bank[:, 4 + 3 * (i % 2), (i // 2) * P:(i // 2 + 1) * P], ar[b:b + DH, c, w, 0, :],
                                       bt[b:b + DH, c, w * P:(w + 1) * P], start=True, stop=True)
                    mm.then_inc(S("power_full"), 1)
                    claim(5, "z", 7 * g + 1)
                    for i in range(4):
                        hh, c, b = head_at(hf, i)
                        pe.wait_ge(S("pairs"), 4 * g + i + 1)
                        mm = pe.matmul(bank[:, 5, i * DH:(i + 1) * DH], AT[:, i, 2 * P:3 * P],
                                       vtk[:, w, hh * DH:(hh + 1) * DH], start=True, stop=True)
                    mm.then_inc(S("z_full"), 1)
                    for lv in range(6):
                        now, nxt = lv % 2, (lv + 1) % 2

                        def powT(i):
                            return AT[:, i, 0:P] if lv == 0 else PP[:, now, 1, i * P:(i + 1) * P]

                        pe.wait_ge(S("power"), 5 * g + min(lv, 4) + 1)
                        if lv >= 1:
                            pe.wait_ge(S("powerT"), 5 * g + lv)
                        if lv < 5:
                            claim(6, "powerT", 5 * g + lv + 1)
                            for i in range(4):
                                mm = pe.matmul(bank[:, 6, i * P:(i + 1) * P], PP[:, now, 0, i * P:(i + 1) * P],
                                               powT(i), start=True, stop=True)
                            mm.then_inc(S("powerT_full"), 1)
                            if lv < 4:
                                claim(4, "power", 5 * g + lv + 2)
                                for i in range(4):
                                    mm = pe.matmul(bank[:, 4, i * P:(i + 1) * P], powT(i),
                                                   PP[:, now, 0, i * P:(i + 1) * P], start=True, stop=True)
                                mm.then_inc(S("power_full"), 1)
                        pe.wait_ge(S("z"), 7 * g + lv + 1)
                        claim(5, "z", 7 * g + lv + 2)
                        for i in range(4):
                            mm = pe.matmul(bank[:, 5, i * P:(i + 1) * P], powT(i), Z[:, i, :], start=True, stop=True)
                        mm.then_inc(S("z_full"), 1)
                    pe.wait_ge(S("z"), 7 * g + 7)
                    for bb in (7, 3, 6):
                        claim(bb, "mt", g + 1)
                    for i in range(4):
                        hh, c, b = head_at(hf, i)
                        pe.matmul(bank[b:b + DH, 7, (i // 2) * P:(i // 2 + 1) * P], Z[:, i, 0:DH], AT[:, i, P:2 * P],
                                  start=True, stop=True)
                        for j in range(2):
                            mm = pe.matmul(bank[b:b + DH, 3 + 3 * j, (i // 2) * DH:(i // 2 + 1) * DH],
                                           Z[64 * j:64 * j + DH, i, 0:DH],
                                           tok3[64 * j:64 * j + DH, 1, hh * DH:(hh + 1) * DH], start=True, stop=True)
                    mm.then_inc(S("mt_full"), 1)
                    claim(0, "wkv", g + 1)
                    for i in range(4):
                        hh, c, b = head_at(hf, i)
                        o = bank[b:b + DH, 0, (i // 2) * P:(i // 2 + 1) * P]
                        pe.matmul(o, vtk[:, w, hh * DH:(hh + 1) * DH], AT[:, i, 3 * P:4 * P], start=(i < 2), stop=False,
                                  skip_group_check=True)
                        pe.matmul(o, Z[:, i, DH:P], AT[:, i, P:2 * P], start=False, stop=False, skip_group_check=True)
                    for j in range(2):
                        claim(1 + j, "state", 2 * g + j + 1)
                        for i in range(4):
                            hh, c, b = head_at(hf, i)
                            rows = slice(64 * j, 64 * j + DH)
                            o = bank[b:b + DH, 1 + j, (i // 2) * DH:(i // 2 + 1) * DH]
                            pe.matmul(o, tok3[rows, 1, hh * DH:(hh + 1) * DH], Z[rows, i, DH:P], start=(i < 2), stop=False,
                                      skip_group_check=True)
                            mm = pe.matmul(o, tok3[rows, 2, hh * DH:(hh + 1) * DH], vtk[rows, w, hh * DH:(hh + 1) * DH],
                                           start=False, stop=False, skip_group_check=True)
                        mm.then_inc(S("state_part"), 1)
                    pe.wait_ge(S("mt"), g + 1)
                    pe.wait_ge(S("state_part"), 2 * g + 2)
                    for j in range(2):
                        n2 = 2 * g + j
                        if n2 >= 1:
                            pe.wait_ge(S("state"), n2)
                        for i in range(4):
                            hh, c, b = head_at(hf, i)
                            o = bank[b:b + DH, 1 + j, (i // 2) * DH:(i // 2 + 1) * DH]
                            mm = pe.matmul(o, MT[b:b + DH, j, c, :], St[b:b + DH, 0, c, :] if j == 0 else St[b:b + DH, 1, c, :],
                                           start=False, stop=True, skip_group_check=True)
                        mm.then_inc(S("state_full"), 1)
                        for i in range(4):
                            hh, c, b = head_at(hf, i)
                            mm = pe.matmul(bank[b:b + DH, 0, (i // 2) * P + 64 * j:(i // 2) * P + 64 * j + 64],
                                           St[b:b + DH, j, c, :], ar[b:b + DH, c, w, 1, 64 * j:64 * j + 64],
                                           start=False, stop=(j == 1), skip_group_check=True)
                    mm.then_inc(S("wkv_full"), 1)
            if stop < 11:
                return
            pe.wait_ge(S("wkv"), 8)
            pe.wait_ge(S("sig_g"), 1)
            for c in range(4):
                claim(0, "yc", c + 1)
                pe.matmul(bank[:, 0, :], const("pair"), h[:, 4 + c, :], start=True, stop=True).then_inc(S("y_sum"), 1)
                pe.wait_ge(S("yc_sq"), c + 1)
                claim(1, "y_root", c + 1)
                pe.matmul(bank[:, 1, :], const("pair"), ropein[:, 1, :], start=True, stop=True)\
                  .then_inc(S("y_ms"), 1)
                claim(2, "o_rw", c + 1)
                pe.matmul(bank[:, 2, :], ext[:, T + c * P:T + (c + 1) * P], u[:, UG, :], start=True, stop=True)\
                  .then_inc(S("g_full"), 1)
            pe.wait_ge(S("o_sb"), 4)
            claim(4, "rms", NORMS.index("g2") + 1)
            for n in range(KD):
                claim(n % 4, "x_added", KD * 1 + n + 1)
                if n == 0:
                    pe.wait_ge(S("o_rw"), 4)
                gemm("w_out2", n % 4, KD, 1, h, "add_full", KD * 1 + n + 1)
                if n >= 1:
                    sumsq("g2", n - 1)
            sumsq("g2", KD - 1)
            if stop < 12:
                return
            swiglu_up("2")
            for n in range(KD):
                claim(n % 4, "x_added", KD * 2 + n + 1)
                gemm("down2", n % 4, FF2 // P, 2, hid, "add_full", KD * 2 + n + 1)

        @block.scalar
        def _(act):
            step = [0]

            mine = {}

            def own(name):
                mine[name] = mine.get(name, 0) + 1
                act.wait_ge(S(name), mine[name])

            def do(ins):
                step[0] += 1
                ins.then_inc(S("act_step"), 1)
                act.wait_ge(S("act_step"), step[0])

            def squares(tag, k, src, dst=sq):
                act.activation(dst[:, k, :], src, ACT.Square).then_inc(S("sq"), 1)
                own("sq")

            def root(tag):
                act.wait_ge(S("ms"), NORMS.index(tag) + 1)
                act.activation(root_ms, bank[:, 4, :], ACT.Sqrt, scale=1.0 / D, bias=epsc[:, 0:1])\
                   .then_inc(S("rms"), 1)
                own("rms")

            act.wait_ge(S("eps"), 3)
            act.wait_ge(S("x_in"), 16)
            for k in range(KD):
                squares("pre1", k, x[:, k, :], h)
            root("pre1")
            act.wait_ge(S("angles"), 2)
            do(act.activation(sin, sin, ACT.Sin))
            do(act.activation(cos, cos, ACT.Sin))
            act.sem_inc(S("cossin"), 1)
            for t in range(NT):
                act.wait_ge(S("vtok_full"), t + 1)
                act.activation(vtok[:, t, :], bank[:, t, 0:VCOLS], ACT.Copy).then_inc(S("vtok"), 1)
                own("vtok")
            act.wait_ge(S("vtok"), NT)
            act.activation(gates[:, :, :], vtok[:, :, 320:344], ACT.Sigmoid).then_inc(S("gates"), 1)
            own("gates")
            act.activation(widx[:, :, :], vtok[:, :, 344:348], ACT.Copy, scale=1.0 / 16).then_inc(S("gates"), 1)
            own("gates")
            for n in range(16):
                act.wait_ge(S("proj_full"), n + 1)
                if n >= 2:
                    act.wait_ge(S("roped"), n - 1)
                act.activation(ropein[:, n % 2, :], bank[:, n % 4, :], ACT.Copy).then_inc(S("ropein"), 1)
                own("ropein")
                if n < NADA - 4:
                    i = n + 4
                    act.wait_ge(S(f"ada_in{i % 2}"), 16 * (i // 2 + 1))
                    for kk in range(KD):
                        ins = act.activation(ada_in[:, i % 2, kk, :], ada_in[:, i % 2, kk, :], ACT.Copy,
                                             scale=vec("c", kk))
                    ins.then_inc(S("ada_scaled"), 1)
                if 4 <= n < 7:
                    for j in range(4 * (n - 4), 4 * (n - 4) + 4):
                        t = 1 + j // 4
                        act.wait_ge(S("logits"), j + 1)
                        if j >= 2:
                            act.wait_ge(S("scored"), j - 1)
                        act.activation(relu_t[:, j % 2, 0:(t + 1) * P], bank[:, 6, 0:(t + 1) * P], ACT.Relu)\
                           .then_inc(S("relu_logits"), 1)
                        own("relu_logits")
            if stop < 2:
                return
            for m in range(2):
                act.wait_ge(S("cmp_hid"), m + 1)
                for g in range(2):
                    act.activation(hidc[:, m, g, :], bank[:, 2 * m + g, 0:CMP_N],
                                   ACT.Gelu_apprx_tanh).then_inc(S("cmp_gelu"), 1)
                    own("cmp_gelu")
            if stop < 3:
                return

            def turned_out(t):
                for half in range(2):
                    act.wait_ge(S("out_turned"), 2 * t + half + 1)
                    act.activation(h[:, 4 * half:4 * half + 4, t * P:(t + 1) * P],
                                   bank[:, 7, :].rearrange("p (c t) -> p c t", c=4), ACT.Copy).then_inc(S("oT"), 1)
                    own("oT")

            for j, (t, br, hh) in enumerate(jobs):
                kv = (t + 1) * P
                act.wait_ge(S("smin"), j + 1)
                if j >= 3:
                    act.wait_ge(S("probs_turned"), j - 2)
                o = j // HEADS
                if hh == 0 and o >= 2:
                    act.wait_ge(S("otok"), o - 1)
                act.activation(prob[:, j % 3, 0:kv], sneg[:, j % 3, 0:kv], ACT.Exp, scale=-1.0,
                               bias=smin[:, j % 3:j % 3 + 1], accum_out=ssum[:, o % 2, hh:hh + 1])\
                   .then_inc(S("probs"), 1)
                if j % 24 == 0:
                    act.wait_ge(S("cmp_shift"), t + 1)
                    act.activation(cs[:, 1, :, :], cs[:, 0, :, :], ACT.Exp, scale=-1.0).then_inc(S("cmp_exp"), 1)
                    own("cmp_exp")
                if j >= 24 and j % 24 == 11:
                    turned_out(t - 1)
            turned_out(NT - 1)
            if stop < 4:
                return

            def post(tag):
                for n in range(KD):
                    act.wait_ge(S("y_full"), KD * (int(tag) - 1) + n + 1)
                    squares("post" + tag, n, bank[:, n % 4, :])
                root("post" + tag)

            def pre(tag, ready, at):
                for k in range(KD):
                    act.wait_ge(S(ready), at + k + 1)
                    squares(tag, k, x[:, k, :])
                root(tag)

            post("1")
            pre("f1", "x_post", 0)
            if stop < 5:
                return
            for n in range(FF1 // P):
                act.wait_ge(S("up_full"), n + 1)
                if n >= 2:
                    act.wait_ge(S("hid"), n - 1)
                act.activation(ftmp[:, n % 2, :], bank[:, n % 4, :], ACT.Relu).then_inc(S("relu"), 1)
                own("relu")
            post("2")
            pre("g1", "x_post", KD)
            if stop < 6:
                return

            def silu(m):
                for n in range(FF2 // P):
                    v = NG * (int(m) - 1) + n
                    act.wait_ge(S("gate_full"), v + 1)
                    if n >= 2:
                        act.wait_ge(S("gated"), v - 1)
                    act.activation(ftmp[:, n % 2, :], bank[:, 2 * (n % 2), :], ACT.Silu).then_inc(S("silu"), 1)
                    own("silu")

            silu("1")
            pre("mix", "x_added", 0)
            if stop < 7:
                return
            for n in range(8):
                act.wait_ge(S("qk_full"), n + 1)
                act.activation(ropein[:, n % 2, :], bank[:, n % 4, :], ACT.Square).then_inc(S("qk_sq"), 1)
                own("qk_sq")
                act.wait_ge(S("qk_ms"), n + 1)
                if n >= 2:
                    act.wait_ge(S("qk2"), n - 1)
                act.activation(ropet[:, n % 2, :], bank[:, 4 + n % 2, :], ACT.Sqrt, scale=1.0 / DH, bias=epsc[:, 0:1])\
                   .then_inc(S("qk_root"), 1)
                own("qk_root")
            for t in range(NT):
                act.wait_ge(S("vtok2_full"), t + 1)
                act.activation(vtok2[:, t, :], bank[:, t, :], ACT.Copy).then_inc(S("vtok2"), 1)
                own("vtok2")
            if stop < 8:
                return
            for n in range(SLOTS + 1):
                if n < SLOTS:
                    for s in slot_steps[n]:
                        w = T - steps[s][1] * P
                        z = ztmp[:, s % 3, 0:w]
                        act.wait_ge(S("sb_scores"), s + 1)
                        if s >= 3:
                            act.wait_ge(S("softplus"), s - 2)
                        do(act.activation(z, bank[:, 2 + s % 3, 0:w], ACT.Abs))
                        do(act.activation(z, z, ACT.Exp, scale=-1.0))
                        act.activation(z, z, ACT.Ln, bias=epsc[:, 2:3]).then_inc(S("log1p"), 1)
                        own("log1p")
                    act.wait_ge(S("u_full"), n + 1)
                    act.activation(u[:, RW_ORDER[n], :], bank[:, n % 2, :], ACT.Copy).then_inc(S("u_raw"), 1)
                    own("u_raw")
                    for s in slot_steps[n]:
                        hh, c = steps[s]
                        a = att[:, hh % 2, AT0[c]:AT0[c] + T - c * P]
                        act.wait_ge(S("att_copy"), s + 1)
                        act.activation(a, a, ACT.Exp).then_inc(S("att"), 1)
                        own("att")
                if n >= 1:
                    for s in slot_steps[n - 1]:
                        hh = s // 4
                        if s % 8 == 7:
                            act.wait_ge(S("sb_pv"), hh + 1)
                            act.activation(osb[:, hh // 2, :], bank[:, 5 + (hh // 2) % 2, :], ACT.Copy)\
                               .then_inc(S("osb"), 1)
                            own("osb")
            if stop < 9:
                return
            for n in range(4):
                act.wait_ge(S("osb"), n + 1)
                if n >= 2:
                    act.wait_ge(S("osb_ms"), n - 1)
                act.activation(ropein[:, n % 2, :], osb[:, n, :], ACT.Square).then_inc(S("osb_sq"), 1)
                own("osb_sq")
                act.wait_ge(S("osb_ms"), n + 1)
                if n >= 2:
                    act.wait_ge(S("o_sb"), n - 1)
                act.activation(ropet[:, n % 2, :], bank[:, 2 + n % 2, :], ACT.Sqrt, scale=1.0 / DH, bias=epsc[:, 0:1])\
                   .then_inc(S("osb_root"), 1)
                own("osb_root")
            act.wait_ge(S("o_sb"), 4)
            act.wait_ge(S("shifted"), 14)
            act.activation(u[0:DH, UWA, :], u[0:DH, UWA, :], ACT.Tanh).then_inc(S("tanh"), 1)
            own("tanh")
            act.activation(u[:, UG, :], u[:, UG, :], ACT.Sigmoid).then_inc(S("sig_g"), 1)
            own("sig_g")
            for t in range(NT):
                act.wait_ge(S("v_turned"), t + 1)
                act.activation(vtk[:, t, :], bank[:, 4 + t % 2, :], ACT.Copy).then_inc(S("vtk"), 1)
                own("vtk")
            for c in range(4):
                act.wait_ge(S("w_full"), c + 1)
                if c:
                    act.wait_ge(S("wkv_in"), c)
                act.activation(sg, bank[:, 0, :], ACT.Sigmoid, bias=vec("rw_w0", c)).then_inc(S("sg"), 1)
                own("sg")
                act.wait_ge(S("a_full"), c + 1)
                act.activation(av, bank[:, 1, :], ACT.Sigmoid, bias=vec("rw_a0", c)).then_inc(S("av"), 1)
                own("av")
                act.wait_ge(S("kk0"), c + 1)
                act.activation(ropein[:, 1, :], ropein[:, 0, :], ACT.Square).then_inc(S("kk_sq"), 1)
                own("kk_sq")
                act.wait_ge(S("kk_ms"), c + 1)
                act.activation(ropet[:, 0, :], bank[:, 6, :], ACT.Sqrt).then_inc(S("kk_root"), 1)
                own("kk_root")
                act.wait_ge(S("csum"), 2 * c + 2)
                act.activation(e1, csum, ACT.Exp, scale=-DECAY).then_inc(S("exps"), 1)
                own("exps")
                act.activation(e2, csum, ACT.Exp, scale=DECAY).then_inc(S("exps"), 1)
                own("exps")
                act.activation(e3, e3, ACT.Exp, scale=-DECAY).then_inc(S("exps"), 1)
                own("exps")
            if stop < 10:
                return
            for w in range(NT):
                for i in range(3):
                    act.wait_ge(S("tok3_full"), 3 * w + i + 1)
                    act.activation(tok3[:, i, :], bank[:, 5 + i, :], ACT.Copy).then_inc(S("tok3"), 1)
                    own("tok3")
                for hf in range(2):
                    g = 2 * w + hf
                    for lv in range(5):
                        act.wait_ge(S("powerT_full"), 5 * g + lv + 1)
                        act.activation(PP[:, (lv + 1) % 2, 1, :], bank[:, 6, :], ACT.Copy).then_inc(S("powerT"), 1)
                        own("powerT")
                    act.wait_ge(S("wkv_full"), g + 1)
                    act.activation(h[:, 4 + 2 * hf:6 + 2 * hf, w * P:(w + 1) * P],
                                   bank[:, 0, 0:256].rearrange("p (c t) -> p c t", c=2), ACT.Copy).then_inc(S("wkv"), 1)
                    own("wkv")
            if stop < 11:
                return
            for c in range(4):
                act.wait_ge(S("yc"), c + 1)
                act.activation(ropein[:, 1, :], ropein[:, 0, :], ACT.Square).then_inc(S("yc_sq"), 1)
                own("yc_sq")
                act.wait_ge(S("y_ms"), c + 1)
                act.activation(ropet[:, 0, :], bank[:, 1, :], ACT.Sqrt, scale=1.0 / DH, bias=epsc[:, 1:2])\
                   .then_inc(S("y_root"), 1)
                own("y_root")
            pre("g2", "x_added", KD)
            if stop < 12:
                return
            silu("2")

        @block.vector
        def _(dve):
            step = [0]

            mine = {}

            def own(name):
                mine[name] = mine.get(name, 0) + 1
                dve.wait_ge(S(name), mine[name])

            def do(ins):
                step[0] += 1
                ins.then_inc(S("dve_step"), 1)
                dve.wait_ge(S("dve_step"), step[0])

            for i, e in enumerate((EPS, LNX_EPS, 1.0)):
                dve.memset(epsc[:, i:i + 1], e).then_inc(S("eps"), 1)
                own("eps")
            ipos = ropet[:, 0, :]
            dve.wait_ge(S("pos_in"), 16)
            dve.wait_ge(S("consts"), 16)
            ang, k = ropein[:, 0, :], ropein[:, 1, :]
            do(dve.tensor_copy(ang, ipos.bitcast(I32)))
            do(dve.tensor_scalar(ang, ang, const("inv"), None, ALU.mult))
            do(dve.tensor_scalar(k, ang, TWO_PI_INV, MAGIC, ALU.mult, ALU.add))
            do(dve.tensor_scalar(k, k, MAGIC, None, ALU.subtract))
            for part in (PI_A, PI_B, PI_C):
                do(dve.scalar_tensor_tensor(out=ang, in0=k, scalar=-part, in1=ang, op0=ALU.mult, op1=ALU.add))
            dve.tensor_scalar(sin, ang, -PI_SAFE, PI_SAFE, ALU.max, ALU.min).then_inc(S("angles"), 1)
            own("angles")
            do(dve.tensor_scalar(k, ang, -1.0, None, ALU.mult))
            do(dve.tensor_tensor(k, k, ang, ALU.max))
            dve.tensor_scalar(cos, k, -1.0, float(np.pi / 2), ALU.mult, ALU.add).then_inc(S("angles"), 1)
            own("angles")

            def ada_piece(i):
                dve.wait_ge(S(f"ada_in{i % 2}"), 16 * (i // 2 + 1))
                if i >= 2:
                    dve.wait_ge(S("ada_cols"), i - 1)
                acc = ada_acc[:, i % 2, :]
                do(dve.tensor_scalar(acc, ada_in[:, i % 2, 0, :], vec("c", 0), None, ALU.mult))
                for kk in range(1, KD):
                    ins = dve.scalar_tensor_tensor(out=acc, in0=ada_in[:, i % 2, kk, :], scalar=vec("c", kk),
                                                   in1=acc, op0=ALU.mult, op1=ALU.add)
                    if kk < KD - 1:
                        do(ins)
                ins.then_inc(S("ada_acc"), 1)
                own("ada_acc")

            def mod_cols(i):
                dve.wait_ge(S("ada_cols"), i + 1)
                dve.tensor_tensor(mod[:, 4 * i:4 * i + 4], bank[:, 7, 4 * i:4 * i + 4], vec("b_ada", 4 * i, 4),
                                  ALU.add).then_inc(S("mod"), 1)
                own("mod")

            def modulate(i, scale_at, g):
                dve.scalar_tensor_tensor(out=gain[:, 8 * i:8 * i + 8], in0=mod[:, scale_at:scale_at + 8],
                                         scalar=1.0, in1=vec(g, 0, 8), op0=ALU.add, op1=ALU.mult)\
                   .then_inc(S("gain"), 1)
                own("gain")

            def normalize(tag, scale, add=None):
                dve.wait_ge(S("rms"), NORMS.index(tag) + 1)
                do(dve.reciprocal(rstd, root_ms))
                for kk in range(KD):
                    ins = dve.scalar_tensor_tensor(out=h[:, kk, :], in0=x[:, kk, :], scalar=scale(kk), in1=rstd,
                                                   op0=ALU.mult, op1=ALU.mult)
                    if add:
                        do(ins)
                        ins = dve.tensor_scalar(h[:, kk, :], h[:, kk, :], add(kk), None, ALU.add)
                    ins.then_inc(S("h"), 1)
                    own("h")

            for i in range(4):
                ada_piece(i)
                if i:
                    mod_cols(i - 1)
            mod_cols(3)
            dve.wait_ge(S("mod"), 4)
            modulate(0, 8, "g_pre_mix")
            dve.wait_ge(S("gain"), 1)
            normalize("pre1", lambda k: gain[:, k:k + 1], lambda k: mod[:, k:k + 1])

            def rope(n):
                src = ropein[:, n % 2, :]
                dve.wait_ge(S("ropein"), n + 1)
                if n == VC:
                    dve.tensor_copy(proj[:, n, :], src).then_inc(S("roped"), 1)
                    own("roped")
                    return
                scale = -DH ** -0.5 if QD <= n < QD + 4 or n >= QN else 1.0
                do(dve.scalar_tensor_tensor(out=ropet[:, 0, :], in0=src, scalar=scale, in1=cos,
                                            op0=ALU.mult, op1=ALU.mult))
                dve.wait_ge(S("turned"), n + 1 - (n > VC))
                do(dve.scalar_tensor_tensor(out=ropet[:, 1, :], in0=bank[:, 4 + n % 2, :], scalar=scale, in1=sin,
                                            op0=ALU.mult, op1=ALU.mult))
                dve.tensor_tensor(proj[:, n, :], ropet[:, 0, :], ropet[:, 1, :], ALU.add).then_inc(S("roped"), 1)
                own("roped")

            def index_score(j):
                t, i = 1 + j // 4, j % 4
                kv = (t + 1) * P
                dve.wait_ge(S("relu_logits"), j + 1)
                s = score[:, t - 1, 0:kv]
                r = relu_t[:, j % 2, 0:kv]
                if i == 0:
                    dve.tensor_scalar(s, r, widx[:, t, 0:1], None, ALU.mult).then_inc(S("scored"), 1)
                    own("scored")
                else:
                    dve.wait_ge(S("scored"), j)
                    dve.scalar_tensor_tensor(out=s, in0=r, scalar=widx[:, t, i:i + 1], in1=s, op0=ALU.mult,
                                             op1=ALU.add).then_inc(S("scored"), 1)
                    own("scored")
                if i == 3:
                    dve.wait_ge(S("scored"), j + 1)
                    do(dve.tensor_tensor(s, s, const("causal")[:, T - kv:T], ALU.subtract))

            def top_round(r):
                t, n = 1 + r // ROUNDS, r % ROUNDS
                s = score[:, t - 1, 0:(t + 1) * P]
                do(dve.max(best8[:, :], s))
                do(dve.match_replace(s, best8[:, :], s, -3.0 * NEG))
                if n == ROUNDS - 1:
                    do(dve.tensor_scalar(choose[:, t - 1, 0:(t + 1) * P], s, -2.0 * NEG, NEG, ALU.is_gt, ALU.mult))

            dve.wait_ge(S("cossin"), 1)
            dve.wait_ge(S("gates"), 2)
            rounds = 0
            for n in range(16):
                if n >= 1:
                    rope(n - 1)
                if 4 <= n < 7:
                    for j in range(4 * (n - 4), 4 * (n - 4) + 4):
                        index_score(j)
                if 2 <= n < 10:
                    mod_cols(n + 2)
                while n >= 7 and rounds < 48 * (n - 6) // 9:
                    top_round(rounds)
                    rounds += 1
            rope(15)
            dve.wait_ge(S("mod"), NADA)
            dve.tensor_tensor(gain[:, 8:16], mod[:, 16:24], vec("g_post_mix", 0, 8), ALU.mult).then_inc(S("gain"), 1)
            own("gain")
            modulate(2, 32, "g_pre_ffn")
            dve.tensor_tensor(gain[:, 24:32], mod[:, 40:48], vec("g_post_ffn", 0, 8), ALU.mult).then_inc(S("gain"), 1)
            own("gain")
            dve.wait_ge(S("gain"), 4)
            if stop < 2:
                return
            do(dve.memset(blk, 0.0))
            for m, (src, pe_name) in enumerate(((KC, "pe_k"), (VC, "pe_v"))):
                dve.wait_ge(S("roped"), src + 1)
                if m:
                    dve.wait_ge(S("cmp_hid"), 1)
                for half in range(2):
                    v = proj[:, src, 256 * 0 + 16 * half:16 * half + 16 * 31].rearrange("p (n l) -> p l n", l=16)
                    pe_b = vec(pe_name, 16 * half, 16)[:, :, None].to_broadcast([P, 16, 31])
                    ins = dve.tensor_tensor(blk[:, 16 * half:16 * half + 16, 0:31], v, pe_b, ALU.add)
                    if half == 0:
                        do(ins)
                ins.then_inc(S("cmp_blocks"), 1)
                own("cmp_blocks")
            do(dve.memset(vcmp, 0.0))
            dve.wait_ge(S("cmp_out"), 1)
            do(dve.tensor_copy(kcmp, bank[:, 5, 0:CMP_N]))
            for g in range(2):
                for i in range(4):
                    do(dve.tensor_copy(vcmp[32 * i:32 * i + 32, g, i * DH:(i + 1) * DH],
                                       bank[32 * i:32 * i + 32, 5, 64 + 64 * g:128 + 64 * g]))
            dve.sem_inc(S("cmp_kv"), 1)
            if stop < 3:
                return

            def masked(j):
                t, br, hh = jobs[j]
                kv = (t + 1) * P
                dve.wait_ge(S("scores"), j + 1)
                if j >= 3:
                    dve.wait_ge(S("probs"), j - 2)
                mask = choose[:, t - 1, 0:kv] if br == 2 and t else const("causal")[:, T - kv:T]
                dve.tensor_tensor_reduce(sneg[:, j % 3, 0:kv], bank[:, j % 3, 0:kv], mask, 1.0, 3e38, ALU.add, ALU.min,
                                         smin[:, j % 3:j % 3 + 1]).then_inc(S("smin"), 1)

            def probs_turned(j):
                kv = (jobs[j][0] + 1) * P
                dve.wait_ge(S("probs_turned"), j + 1)
                if j >= 3:
                    dve.wait_ge(S("pv"), j - 2)
                dve.tensor_copy(probT[:, j % 3, 0:kv], bank[:, 3 + j % 2, 0:kv]).then_inc(S("probT"), 1)

            def wide(c):
                return c[:, :, None].to_broadcast([P, HEADS, DH])

            def add_heads(o):
                t, br = o // 3, o % 3
                dve.wait_ge(S("pv"), 8 * o + 8)
                do(dve.reciprocal(coef[:, :], ssum[:, o % 2, :]))
                pvb = bank[:, 5 + o % 2, :].rearrange("p (a b) -> p a b", a=HEADS)
                if br == 2:
                    if t >= 2:
                        dve.wait_ge(S("out_turned"), 2 * (t - 1))
                    dve.tensor_tensor(otok[:, t % 2, T:D].rearrange("p (a b) -> p a b", a=HEADS), pvb,
                                      wide(coef), ALU.mult).then_inc(S("otok"), 1)
                    own("otok")
                    return
                gate = gates[:, t, :].rearrange("p (h i) -> p h i", i=3)[:, :, br + 1]
                do(dve.tensor_tensor(coef2[:, :], coef[:, :], gate, ALU.mult))
                do(dve.tensor_tensor(heads8, pvb, wide(coef2), ALU.mult))
                dst = otok[:, t % 2, 0:T]
                dve.tensor_tensor(dst, dst, heads8.rearrange("p a b -> p (a b)"), ALU.add).then_inc(S("otok"), 1)
                own("otok")

            heads8 = ropet[:, 0, :].rearrange("p (a b) -> p a b", a=HEADS)

            def cmp_masked(t):
                keep = const("cmp_keep")[:, t * CMP_N:(t + 1) * CMP_N]
                drop = const("cmp_drop")[:, t * CMP_N:(t + 1) * CMP_N]
                c0 = cs[:, 0, :, :]
                dve.wait_ge(S("cmp_scores"), t + 1)
                dve.tensor_tensor(c0, bank[:, 7, 0:256].rearrange("p (a b) -> p a b", a=HEADS),
                                  keep[:, None, :].to_broadcast([P, HEADS, CMP_N]), ALU.mult)\
                   .then_inc(S("cmp_masked"), 1)
                own("cmp_masked")
                dve.wait_ge(S("cmp_masked"), t + 1)
                do(dve.tensor_tensor(c0, c0, drop[:, None, :].to_broadcast([P, HEADS, CMP_N]), ALU.add))
                do(dve.tensor_reduce(cmin[:, :], c0, AX.X, ALU.min))
                dve.tensor_tensor(c0, c0, cmin[:, :, None].to_broadcast([P, HEADS, CMP_N]), ALU.subtract)\
                   .then_inc(S("cmp_shift"), 1)
                own("cmp_shift")

            def cmp_probs(t):
                keep = const("cmp_keep")[:, t * CMP_N:(t + 1) * CMP_N]
                c1 = cs[:, 1, :, :]
                dve.wait_ge(S("cmp_exp"), t + 1)
                do(dve.tensor_reduce(cmin[:, :], c1, AX.X, ALU.add))
                do(dve.reciprocal(coef[:, :], cmin[:, :]))
                gate = gates[:, t, :].rearrange("p (h i) -> p h i", i=3)[:, :, 0]
                do(dve.tensor_tensor(coef2[:, :], coef[:, :], gate, ALU.mult))
                do(dve.tensor_tensor(c1, c1, keep[:, None, :].to_broadcast([P, HEADS, CMP_N]), ALU.mult))
                dve.tensor_tensor(c1, c1, coef2[:, :, None].to_broadcast([P, HEADS, CMP_N]), ALU.mult)\
                   .then_inc(S("cmp_probs"), 1)
                own("cmp_probs")

            n = len(jobs)
            for j in range(n + 3):
                if j < n:
                    masked(j)
                    t = j // 24
                    if j % 24 == 0:
                        cmp_masked(t)
                    if j % 24 == 2:
                        cmp_probs(t)
                    if j % 24 == 5:
                        dve.wait_ge(S("cmp_turned"), t + 1)
                        dve.tensor_copy(cpt.rearrange("p a b -> p (a b)"), bank[:, 7, 0:256]).then_inc(S("cmp_probT"), 1)
                        own("cmp_probT")
                    if j % 24 == 8:
                        dve.wait_ge(S("cmp_pv"), t + 1)
                        if t >= 2:
                            dve.wait_ge(S("out_turned"), 2 * (t - 1))
                        dve.tensor_copy(otok[:, t % 2, 0:T], bank[:, 7, :]).then_inc(S("cmp_otok"), 1)
                        own("cmp_otok")
                        dve.wait_ge(S("cmp_otok"), t + 1)
                if 2 <= j < n + 2:
                    probs_turned(j - 2)
                if j >= 11 and (j - 11) % 8 == 0:
                    add_heads((j - 11) // 8)
            add_heads(11) if (n + 3 - 1 - 11) // 8 < 11 else None
            if stop < 4:
                return

            def post(tag, y, g_at):
                for nn in range(KD):
                    dve.wait_ge(S("sq"), KD * NORMS.index("post" + tag) + nn + 1)
                    dve.tensor_copy(y[:, nn, :], bank[:, nn % 4, :]).then_inc(S("y_read"), 1)
                    own("y_read")
                dve.wait_ge(S("y_read"), KD * int(tag))
                dve.wait_ge(S("rms"), NORMS.index("post" + tag) + 1)
                do(dve.reciprocal(rstd, root_ms))
                for nn in range(KD):
                    do(dve.tensor_tensor(y[:, nn, :], y[:, nn, :], rstd, ALU.mult))
                    dve.scalar_tensor_tensor(out=x[:, nn, :], in0=y[:, nn, :], scalar=gain[:, g_at + nn:g_at + nn + 1],
                                             in1=x[:, nn, :], op0=ALU.mult, op1=ALU.add).then_inc(S("x_post"), 1)
                    own("x_post")

            post("1", ybuf, 8)
            dve.wait_ge(S("x_post"), KD)
            normalize("f1", lambda k: gain[:, 16 + k:17 + k], lambda k: mod[:, 24 + k:25 + k])
            if stop < 5:
                return
            for nn in range(FF1 // P):
                dve.wait_ge(S("relu"), nn + 1)
                dve.tensor_tensor(hid[:, nn, :], ftmp[:, nn % 2, :], ftmp[:, nn % 2, :], ALU.mult)\
                   .then_inc(S("hid"), 1)
                own("hid")
            post("2", h, 24)
            dve.wait_ge(S("x_post"), 2 * KD)
            normalize("g1", lambda k: vec("norm_ffn1_2", k))
            if stop < 6:
                return

            def swiglu(m):
                for nn in range(FF2 // P):
                    v = NG * (int(m) - 1) + nn + 1
                    dve.wait_ge(S("silu"), v)
                    dve.wait_ge(S("gate_up_full"), v)
                    dve.tensor_tensor(hid[:, nn, :], ftmp[:, nn % 2, :], bank[:, 2 * (nn % 2) + 1, :], ALU.mult)\
                       .then_inc(S("gated"), 1)
                    own("gated")

            def add_to_x(i, scale):
                for nn in range(KD):
                    dve.wait_ge(S("add_full"), KD * i + nn + 1)
                    dve.scalar_tensor_tensor(out=x[:, nn, :], in0=bank[:, nn % 4, :], scalar=scale, in1=x[:, nn, :],
                                             op0=ALU.mult, op1=ALU.add).then_inc(S("x_added"), 1)
                    own("x_added")

            swiglu("1")
            add_to_x(0, 0.5)
            dve.wait_ge(S("x_added"), KD)
            normalize("mix", lambda k: vec("norm_mix_2", k))
            if stop < 7:
                return
            do(dve.tensor_scalar(sbg[:, 0:1], vec("sb_q"), DH ** -0.5, None, ALU.mult))
            do(dve.tensor_copy(sbg[:, 1:2], vec("sb_k")))
            for nn in range(8):
                dve.wait_ge(S("qk_root"), nn + 1)
                do(dve.reciprocal(ropet[:, nn % 2, :], ropet[:, nn % 2, :]))
                dve.scalar_tensor_tensor(out=qk2[:, nn, :], in0=bank[:, nn % 4, :], scalar=sbg[:, nn // 4:nn // 4 + 1],
                                         in1=ropet[:, nn % 2, :], op0=ALU.mult, op1=ALU.mult).then_inc(S("qk2"), 1)
                own("qk2")
            if stop < 8:
                return
            for nn in range(SLOTS):
                for s in slot_steps[nn]:
                    hh, c = steps[s]
                    w = T - c * P
                    d = sp[:, hh % 2, AT0[c]:AT0[c] + w]
                    dve.wait_ge(S("log1p"), s + 1)
                    if s >= 8 and s % 4 == 0:
                        dve.wait_ge(S("sb_suffix"), s - 4)
                    do(dve.scalar_tensor_tensor(out=d, in0=bank[:, 2 + s % 3, 0:w], scalar=0.0,
                                                in1=ztmp[:, s % 3, 0:w], op0=ALU.max, op1=ALU.add))
                    dve.tensor_tensor(d[:, 0:P], d[:, 0:P], const("before"), ALU.mult).then_inc(S("softplus"), 1)
                    own("softplus")
                for s in slot_steps[nn]:
                    hh, c = steps[s]
                    w = T - c * P
                    dve.wait_ge(S("sb_suffix"), s + 1)
                    if hh >= 2 and c == 3:
                        dve.wait_ge(S("sb_pv"), hh - 1)
                    dve.tensor_tensor(att[:, hh % 2, AT0[c]:AT0[c] + w], bank[:, 2 + s % 3, 0:w],
                                      const("notbefore")[:, 0:w], ALU.add).then_inc(S("att_copy"), 1)
                    own("att_copy")
            if stop < 9:
                return
            for nn in range(4):
                dve.wait_ge(S("osb_root"), nn + 1)
                do(dve.reciprocal(ropet[:, nn % 2, :], ropet[:, nn % 2, :]))
                dve.scalar_tensor_tensor(out=h[:, nn, :], in0=osb[:, nn, :], scalar=vec("sb_out", nn),
                                         in1=ropet[:, nn % 2, :], op0=ALU.mult, op1=ALU.mult).then_inc(S("o_sb"), 1)
                own("o_sb")
            dve.wait_ge(S("o_sb"), 4)
            dve.wait_ge(S("shifted"), 14)
            do(dve.memset(reset, 1.0))
            do(dve.memset(reset.rearrange("p (c t) -> p c t", t=CHUNK)[:, :, 0:1], 0.0))
            do(dve.tensor_scalar(omka[:, :], vec("rw_k_a", 0, 4), -1.0, 1.0, ALU.mult, ALU.add))
            for c in range(4):
                kk, r, kx = ropein[:, 0, :], u[:, UR + c, :], u[:, UK + c, :]

                def wins(v):
                    return v.rearrange("p (w t) -> p w t", w=NT)

                if c:
                    dve.wait_ge(S("wkv_in"), c)
                dve.tensor_scalar(kk, kx, vec("rw_k_k", c), None, ALU.mult).then_inc(S("kk0"), 1)
                own("kk0")
                dve.wait_ge(S("sg"), c + 1)
                if c:
                    dve.wait_ge(S("exps"), 3 * c)
                dve.tensor_tensor_scan(csum, reset, sg, 0.0, ALU.mult, ALU.add).then_inc(S("csum"), 1)
                own("csum")
                dve.wait_ge(S("csum"), 2 * c + 1)
                dve.tensor_tensor(e3, csum, sg, ALU.subtract).then_inc(S("csum"), 1)
                own("csum")
                dve.wait_ge(S("av"), c + 1)
                do(dve.tensor_scalar(sg, av, vec("rw_k_a", c), omka[:, c:c + 1], ALU.mult, ALU.add))
                do(dve.tensor_tensor(sg, sg, kx, ALU.mult))
                if c:
                    dve.wait_ge(S("bonus_full"), c)
                dve.scalar_tensor_tensor(out=ropet[:, 1, :], in0=r, scalar=vec("rw_r_k", c), in1=sg,
                                         op0=ALU.mult, op1=ALU.mult).then_inc(S("rkr"), 1)
                own("rkr")
                dve.wait_ge(S("kk_root"), c + 1)
                do(dve.tensor_scalar(ropet[:, 0, :], ropet[:, 0, :], 1e-12, None, ALU.max))
                do(dve.reciprocal(ropet[:, 0, :], ropet[:, 0, :]))
                do(dve.tensor_tensor(kk, kk, ropet[:, 0, :], ALU.mult))
                dve.wait_ge(S("exps"), 3 * c + 3)
                do(dve.tensor_tensor(kt[:, c, :], sg, e2, ALU.mult))
                do(dve.scalar_tensor_tensor(out=ar[:, c, :, 0, :], in0=wins(kk), scalar=-1.0, in1=wins(e3),
                                            op0=ALU.mult, op1=ALU.mult))
                do(dve.tensor_tensor(ar[:, c, :, 1, :], wins(r), wins(e1), ALU.mult))
                do(dve.tensor_tensor(kk, kk, av, ALU.mult))
                do(dve.tensor_tensor(bt[:, c, :], kk, e2, ALU.mult))
                do(dve.tensor_copy(ends[:, c, :], e1.rearrange("p (j t) -> p j t", t=CHUNK)[:, :, CHUNK - 1]))
                dve.wait_ge(S("bonus_full"), c + 1)
                dve.wait_ge(S("v_turned"), NT)
                dve.tensor_tensor(u[:, UV + c, :], bank[:, 7, :], u[:, UV + c, :], ALU.mult).then_inc(S("bonus"), 1)
                own("bonus")
                dve.wait_ge(S("bonus"), c + 1)
                dve.sem_inc(S("wkv_in"), 1)
            if stop < 10:
                return
            dve.memset(St[:, :, :, :], 0.0).then_inc(S("state0"), 1)
            own("state0")
            dve.wait_ge(S("state0"), 1)
            quad = [P, 4, P]
            for w in range(NT):
                for hf in range(2):
                    g = 2 * w + hf
                    for i in range(4):
                        dve.wait_ge(S("pairs_full"), 4 * g + i + 1)
                        dve.tensor_tensor(AT[:, i, :], bank[:, i, :], const("chunk4"), ALU.mult).then_inc(S("pairs"), 1)
                    dve.wait_ge(S("power_full"), 5 * g + 1)
                    for i in range(2):
                        ins = dve.tensor_tensor(PP[:, 0, 0, :].rearrange("p (a o b) -> p a o b", a=2, o=2)[:, :, i, :],
                                                bank[:, 4 + 3 * i, 0:256].rearrange("p (a b) -> p a b", a=2),
                                                const("chunkT")[:, None, :].to_broadcast([P, 2, P]), ALU.mult)
                        if i == 0:
                            do(ins)
                    ins.then_inc(S("power"), 1)
                    own("power")
                    dve.wait_ge(S("tok3"), 3 * w + 3)
                    dve.wait_ge(S("z_full"), 7 * g + 1)
                    do(dve.tensor_copy(Z[:, :, DH:P], bank[:, 5, 0:256].rearrange("p (a b) -> p a b", a=4)))
                    dve.tensor_copy(Z[:, :, 0:DH], tok3[:, 0, 256 * hf:256 * hf + 256].rearrange("p (a b) -> p a b", a=4))\
                       .then_inc(S("z"), 1)
                    own("z")
                    for lv in range(6):
                        if lv < 4:
                            dve.wait_ge(S("power_full"), 5 * g + lv + 2)
                            dve.tensor_copy(PP[:, (lv + 1) % 2, 0, :], bank[:, 4, :]).then_inc(S("power"), 1)
                            own("power")
                        dve.wait_ge(S("z_full"), 7 * g + lv + 2)
                        dve.wait_ge(S("z"), 7 * g + lv + 1)
                        dve.tensor_tensor(Z[:, :, :], Z[:, :, :], bank[:, 5, :].rearrange("p (a b) -> p a b", a=4),
                                          ALU.add).then_inc(S("z"), 1)
                        own("z")
                    dve.wait_ge(S("mt_full"), g + 1)
                    rr = ar[:, 2 * hf:2 * hf + 2, w, 1, :]
                    do(dve.tensor_tensor(rr, rr, bank[:, 7, 0:256].rearrange("p (c t) -> p c t", c=2), ALU.add))
                    for j in range(2):
                        ins = dve.tensor_tensor(MT[:, j, 2 * hf:2 * hf + 2, :],
                                                bank[:, 3 + 3 * j, 0:P].rearrange("p (c k) -> p c k", c=2),
                                                const("ident64")[:, None, :].to_broadcast([P, 2, DH]), ALU.add)
                        if j == 0:
                            do(ins)
                    ins.then_inc(S("mt"), 1)
                    own("mt")
                    for j in range(2):
                        n2 = 2 * g + j
                        dve.wait_ge(S("state_full"), n2 + 1)
                        if j == 1:
                            dve.wait_ge(S("wkv_full"), g + 1)
                        e = ends[:, 2 * hf:2 * hf + 2, 2 * w + j:2 * w + j + 1].to_broadcast([P, 2, DH])
                        dve.tensor_tensor(St[:, (j + 1) % 2, 2 * hf:2 * hf + 2, :],
                                          bank[:, 1 + j, 0:128].rearrange("p (c v) -> p c v", c=2), e, ALU.mult)\
                           .then_inc(S("state"), 1)
                        own("state")
            if stop < 11:
                return
            for c in range(4):
                yy, yc = h[:, 4 + c, :], ropein[:, 0, :]
                dve.wait_ge(S("y_sum"), c + 1)
                dve.scalar_tensor_tensor(out=yc, in0=bank[:, 0, :], scalar=-1.0 / DH, in1=yy, op0=ALU.mult,
                                         op1=ALU.add).then_inc(S("yc"), 1)
                own("yc")
                dve.wait_ge(S("y_root"), c + 1)
                do(dve.reciprocal(ropet[:, 0, :], ropet[:, 0, :]))
                do(dve.tensor_tensor(yc, yc, ropet[:, 0, :], ALU.mult))
                do(dve.tensor_scalar(yc, yc, vec("rw_ln_w", c), vec("rw_ln_b", c), ALU.mult, ALU.add))
                do(dve.tensor_tensor(yc, yc, u[:, UV + c, :], ALU.add))
                dve.wait_ge(S("g_full"), c + 1)
                dve.tensor_tensor(yy, yc, bank[:, 2, :], ALU.mult).then_inc(S("o_rw"), 1)
                own("o_rw")
                dve.wait_ge(S("o_rw"), c + 1)
            add_to_x(1, 1.0)
            dve.wait_ge(S("x_added"), 2 * KD)
            normalize("g2", lambda k: vec("norm_ffn2_2", k))
            if stop < 12:
                return
            swiglu("2")
            add_to_x(2, 0.5)

        @block.gpsimd
        def _(pool):
            step = [0]

            mine = {"ada_acc": 4}

            def own(name):
                mine[name] = mine.get(name, 0) + 1
                pool.wait_ge(S(name), mine[name])

            def do(ins):
                step[0] += 1
                ins.then_inc(S("pool_step"), 1)
                pool.wait_ge(S("pool_step"), step[0])

            pool.wait_ge(S("ada_acc"), 4)
            for i in range(4, NADA):
                v = ada_in[:, i % 2, :, :]
                pool.wait_ge(S("ada_scaled"), i - 3)
                pool.wait_ge(S("ada_cols"), i - 1)
                do(pool.tensor_tensor(v[:, 0:4, :], v[:, 0:4, :], v[:, 4:8, :], ALU.add))
                do(pool.tensor_tensor(v[:, 0:2, :], v[:, 0:2, :], v[:, 2:4, :], ALU.add))
                pool.tensor_tensor(ada_acc[:, i % 2, :], v[:, 0, :], v[:, 1, :], ALU.add).then_inc(S("ada_acc"), 1)
                own("ada_acc")
            if stop < 8:
                return
            for n in range(SLOTS):
                f = u[:, RW_ORDER[n], :]
                d = shift[:, n % 2, :]
                pool.wait_ge(S("u_raw"), n + 1)
                do(pool.tensor_scalar(d[:, 0:1], f[:, 0:1], -1.0, None, ALU.mult))
                do(pool.tensor_tensor(d[:, 1:T], f[:, 0:T - 1], f[:, 1:T], ALU.subtract))
                do(pool.tensor_scalar(d, d, vec("rw_mu", RW_ORDER[n]), None, ALU.mult))
                pool.tensor_tensor(f, f, d, ALU.add).then_inc(S("shifted"), 1)
                own("shifted")

        @block.sync
        def _(sp_eng):
            sy = sp_eng

            def ada_load(i):
                if i >= 2:
                    sy.wait_ge(S("ada_acc"), i - 1)
                sy.dma_start(ada_in[:, i % 2, :, :].rearrange("p k n -> p (k n)"), ada[i]).then_inc(S(f"ada_in{i % 2}"), 16)

            def tile_load(i):
                name, n, size = STREAM[i]
                if i >= RING:
                    sy.wait_ge(*tile_done[i - RING])
                sy.dma_start(ring[:, i % RING, 0:size], mats[name][n]).then_inc(S(f"slot{i % RING}"), 16)

            sy.dma_start(x[:, :, :].rearrange("p k t -> p (k t)"), xt).then_inc(S("x_in"), 16)
            sy.dma_start(cst[:, :], consts).then_inc(S("consts"), 16)
            sy.dma_start(ropet[:, 0, :].bitcast(I32), pos.to_broadcast([P, T])).then_inc(S("pos_in"), 16)
            sy.dma_start(col[:, :], cols).then_inc(S("cols_in"), 16)
            sy.wait_ge(S("cols_in"), 16)
            sy.dma_start(ext[:, :], extra).then_inc(S("ext_in"), 16)
            sy.wait_ge(S("ext_in"), 16)
            for i in range(4):
                ada_load(i)
            for i in range(len(tile_done)):
                name, n, size = STREAM[i]
                if name == "w_in" and n < 8:
                    ada_load(n + 4)
                tile_load(i)
            if stop >= 12:
                for n in range(KD):
                    sy.wait_ge(S("x_added"), 2 * KD + n + 1)
                    sy.dma_start(out[:, n * T:(n + 1) * T], x[:, n, :]).then_inc(S("stored"), 16)
                sy.wait_ge(S("stored"), 16 * KD)
            else:
                env = dict(x=x[:, :, :], h=h[:, :, :], arena=arena[:, :], mod=mod[:, :], gates=gates[:, :, :], ends=ends[:, :, :])
                for nm, val in dumps["wait"]:
                    sy.wait_ge(S(nm), val)
                for nm, dst in dumps["out"].items():
                    v = env[nm] if nm in env else arena[:, int(nm.split("_")[1]) * K:int(nm.split("_")[2]) * K]
                    if len(v.shape) == 3:
                        v = v.rearrange("p a b -> p (a b)")
                    sy.dma_start(dst, v).then_inc(S("stored"), 16)
                sy.wait_ge(S("stored"), 16 * len(dumps["out"]))
        if dumps is not None:
            dumps["nsem"] = len(sems)


def columns(v):
    return np.ascontiguousarray(np.asarray(v).reshape(-1, P).T)


def tiles(w, parts=1):
    kd, n = w.shape
    kc = kd // P // parts
    t = w.reshape(parts, kc, P, n // P, P).transpose(3, 0, 2, 1, 4)
    return np.ascontiguousarray(t.reshape(n // P * parts, P, kc * P))


def lay_out(inp):
    f = {k: np.asarray(v) for k, v in inp.items()}
    w_in = f["w_in"][0]
    cuts = np.cumsum([0, 512, 128, 128, 128, 128, 128, 128, 24, 512, 64, 64, 256, 64, 4])
    qn, kc, vc, ksl, vsl, kw, vw, gl, qd, kd, vd, qi, ki, wi = [w_in[:, a:b] for a, b in zip(cuts[:-1], cuts[1:])]
    qn = qn.reshape(D, 2, 4, DH).transpose(0, 2, 1, 3).reshape(D, 512)
    feat = np.concatenate([qi, ki, ki, qd, kd, kd, kc, vc, ksl, kw, qn], 1)
    tok = np.concatenate([vsl, vw, vd, gl, wi], 1)
    mats = {"w_in": tiles(feat),
            "w_v": np.ascontiguousarray(tok.reshape(2, 4, P, VCOLS).transpose(0, 2, 1, 3).reshape(2, P, 4 * VCOLS))}
    for name in ("k", "v"):
        w1 = f["cmp_w1_" + name][0].reshape(CMP_L, DH, P).transpose(1, 0, 2)
        w1 = np.concatenate([w1, w1], 0)
        w1 = np.concatenate([w1, np.zeros((P, 1, P), np.float32)], 1)
        mats["cmp1" + name] = np.ascontiguousarray(w1.reshape(P, 3, SLOT).transpose(1, 0, 2))
    mats["w_out"] = tiles(f["w_out"][0])
    mats["w_up"] = tiles(f["w_up"][0])
    mats["w_down"] = tiles(f["w_down"][0], 4)
    for m in ("1", "2"):
        mats["gate" + m] = tiles(f[f"ffn{m}_gate_2"][0])
        mats["up" + m] = tiles(f[f"ffn{m}_up_2"][0])
        mats["down" + m] = tiles(f[f"ffn{m}_down_2"][0], 2)
    w2 = f["w_in_2"][0]
    u = w2[:, 1536:].reshape(D, 14, P)[:, [12] + list(range(4, 8)) + list(range(4)) + list(range(8, 12)) + [13]]
    mats["w_in2"] = tiles(np.concatenate([w2[:, 0:1024], u.reshape(D, -1)], 1))
    mats["w_v2"] = np.ascontiguousarray(w2[:, 1024:1536].reshape(4, 2, P, T).transpose(0, 2, 1, 3).reshape(4, P, 2 * T))
    mats["w_out2"] = tiles(f["w_out_2"][0])
    ada = np.ascontiguousarray(f["w_ada"][0].reshape(KD, P, NADA, ADA).transpose(2, 1, 0, 3).reshape(NADA, P, KD * ADA))
    pair = lambda v: np.concatenate([v, v], -1)
    cols = [columns(f["c"][0]), columns(f["b_ada"][0])] + [columns(f[n][0]) for n in (
        "g_pre_mix", "g_post_mix", "g_pre_ffn", "g_post_ffn", "norm_ffn1_2", "norm_mix_2", "norm_ffn2_2")]
    cols += [columns(pair(f["sb_q_norm_2"][0])), columns(pair(f["sb_k_norm_2"][0])), columns(f["sb_out_norm_2"][0])]
    cols += [columns(f[n][0]) for n in ("rw_mu_2", "rw_w0_2", "rw_a0_2", "rw_k_k_2", "rw_k_a_2", "rw_r_k_2",
                                        "rw_ln_w_2", "rw_ln_b_2")]
    cols += [np.concatenate([f["cmp_pe_" + n][0].T] * 2, 0) for n in ("k", "v")]
    cols = np.ascontiguousarray(np.concatenate(cols, 1))
    lora = np.concatenate([f["rw_w2_2"][0], f["rw_a2_2"][0]], 0)
    extra = np.ascontiguousarray(np.concatenate([lora, f["rw_g2_2"][0], f["cmp_w2_k"][0], f["cmp_w2_v"][0]], 1))
    xt = np.ascontiguousarray(f["x"][0].T.reshape(KD, P, T).transpose(1, 0, 2).reshape(P, KD * T))
    arrays = {"xt": xt, "consts": CONSTS, "cols": cols, "pos": np.ascontiguousarray(f["positions"]), "ada": ada,
              "extra": extra}
    arrays.update({"m_" + k: v for k, v in mats.items()})
    return arrays


def declare(nc, arrays):
    aps = {}
    for name, a in arrays.items():
        aps[name] = nc.dram_tensor(name, a.shape, mybir.dt.from_np(a.dtype), kind="ExternalInput").ap()
    return aps


def kernel(**inputs):
    from concourse import bacc
    from concourse.bass_utils import run_bass_kernel_spmd

    nc = bacc.Bacc("TRN2", target_bir_lowering=False, num_devices=1)
    arrays = lay_out(inputs)
    aps = declare(nc, arrays)
    out = nc.dram_tensor("out", (P, KD * T), F32, kind="ExternalOutput").ap()
    mats = {k[2:]: v for k, v in aps.items() if k.startswith("m_")}
    build(nc, aps["xt"], aps["consts"], aps["cols"], aps["pos"], aps["ada"], mats, aps["extra"], out)
    r = run_bass_kernel_spmd(nc, [arrays], core_ids=[0])
    y = r.results[0]["out"]
    return np.ascontiguousarray(y.reshape(P, KD, T).transpose(2, 1, 0).reshape(1, T, D))
```

```python
from contextlib import ExitStack

import numpy as np

import concourse.bass as bass
from concourse import mybir

F32 = mybir.dt.float32
F32R = mybir.dt.float32r
I32 = mybir.dt.int32
ALU = mybir.AluOpType
ACT = mybir.ActivationFunctionType
AX = mybir.AxisListType

P = 128
T = 512
D = 1024
KD = D // P
NT = T // P
DH = 64
HEADS = 8
FF1 = 4096
FF2 = 2816
NEG = 1e30
EPS = 1e-6
LNX_EPS = 64e-5
TOPK = 128
ROUNDS = TOPK // 8
CMP_N = 32
CMP_L = 32
CHUNK = 64
NCH = T // CHUNK
DECAY = float(np.exp(np.float32(-0.5)))
TWO_PI_INV = float(np.float32(1.0 / (2.0 * np.pi)))
PI_A = 6.28125
PI_B = float(np.float32(1.9353071795e-3) - np.float32(1.9353071795e-3) % np.float32(2.0 ** -21))
PI_C = float(2.0 * np.pi - PI_A - PI_B)
MAGIC = 12582912.0
PI_SAFE = 3.1415925

CONST = {}
_parts = []


def _const(name, a):
    at = sum(x.shape[1] for x in _parts)
    CONST[name] = (at, at + a.shape[1])
    _parts.append(np.asarray(a, np.float32))


_i = np.arange(P)
_eye = np.eye(P, dtype=np.float32)
_const("ident", _eye)
_const("ones", np.ones((P, P)))
_const("pair", (_i[:, None] // DH == _i[None, :] // DH))
_const("turn", np.where(_i[None, :] % DH < 32, -(_i[:, None] == _i[None, :] + 32).astype(np.float32),
                        (_i[:, None] == _i[None, :] - 32).astype(np.float32)))
_const("causal", np.concatenate([np.zeros((P, T - P)), NEG * (_i[None, :] > _i[:, None])], 1))
_ends = np.arange(CMP_N) * 16 + CMP_L - 1
_cm = np.stack([(_ends[None, :] <= (t * P + _i)[:, None]) for t in range(NT)], 1).astype(np.float32)
_const("cmp_keep", _cm.reshape(P, -1))
_const("cmp_drop", (NEG * (1.0 - _cm)).reshape(P, -1))
_same = _i[:, None] // CHUNK == _i[None, :] // CHUNK
_lt = (_same & (_i[:, None] < _i[None, :])).astype(np.float32)
_le = (_same & (_i[:, None] <= _i[None, :])).astype(np.float32)
_const("chunk4", np.concatenate([_lt, _le, _lt, _le], 1))
_const("chunkT", _lt.T)
_const("suffix", -(_i[:, None] >= _i[None, :]).astype(np.float32))
_const("minus", -np.ones((P, P)))
_const("before", (_i[:, None] < _i[None, :]))
_const("notbefore", np.concatenate([-NEG * (_i[:, None] >= _i[None, :]), np.zeros((P, T - P))], 1))
_const("ident64", (_i[:, None] % DH == np.arange(DH)[None, :]))
_half = np.float32(10000.0) ** (-np.arange(32, dtype=np.float32) / np.float32(32))
_const("inv", np.tile(_half, 4)[:, None])
CONSTS = np.ascontiguousarray(np.concatenate(_parts, 1), np.float32)
NCONST = CONSTS.shape[1]

COLS = {}
_at = 0
for _name, _n in [("c", 8), ("b_ada", 48), ("g_pre_mix", 8), ("g_post_mix", 8), ("g_pre_ffn", 8),
                  ("g_post_ffn", 8), ("norm_ffn1_2", 8), ("norm_mix_2", 8), ("norm_ffn2_2", 8),
                  ("sb_q", 1), ("sb_k", 1), ("sb_out", 4), ("rw_mu", 14), ("rw_w0", 4), ("rw_a0", 4),
                  ("rw_k_k", 4), ("rw_k_a", 4), ("rw_r_k", 4), ("rw_ln_w", 4), ("rw_ln_b", 4),
                  ("pe_k", 32), ("pe_v", 32)]:
    COLS[_name] = (_at, _at + _n)
    _at += _n
NCOLS = _at

SBUF_START = 16896
SLOT = 11 * P
RING = 4
SPLIT = 3
FF1_PARTS = 4
NG = FF2 // P // 2
VCOLS = 348
ADA = 256
NADA = 6 * D // ADA


def weight_stream():
    out = [("w_v", n, 4 * VCOLS) for n in range(2)]
    out += [("w_in", n, 8 * P) for n in range(16)]
    out += [("cmp1k", n, SLOT) for n in range(3)] + [("cmp1v", n, SLOT) for n in range(3)]
    out += [("w_out", n, 8 * P) for n in range(8)]
    for q in range(FF1_PARTS):
        out += [("w_up", 8 * q + n, 8 * P) for n in range(8)]
        out += [("w_down", FF1_PARTS * n + q, 8 * P) for n in range(KD)]
    for m in ("1", "2"):
        for half in range(2):
            out += [(w + m, NG * half + n, 8 * P) for n in range(NG) for w in ("gate", "up")]
            out += [("down" + m, 2 * n + half, NG * P) for n in range(KD)]
        if m == "1":
            out += [("w_in2", n, 8 * P) for n in range(8)]
            out += [("w_v2", n, 2 * T) for n in range(4)]
            out += [("w_in2", n, 8 * P) for n in range(8, 22)]
            out += [("w_out2", n, 8 * P) for n in range(8)]
    return out


STREAM = weight_stream()


WHOLE = [i for i, t in enumerate(STREAM) if t[0].startswith("cmp1")]
PARTED = [i for i in range(len(STREAM)) if i not in WHOLE]
PINDEX = {STREAM[i][:2]: s for s, i in enumerate(PARTED)}
def build(nc, xt, consts, cols, pos, ada, mats, extra, out, stop=99, dumps=None):
    ctx = ExitStack()
    with ctx:
        sems = {}

        def S(name):
            if name not in sems:
                sems[name] = ctx.enter_context(nc.semaphore(name))
            return sems[name]

        def sb(name, shape, dt=F32):
            return ctx.enter_context(nc.sbuf_tensor(name, shape, dt))

        place = [SBUF_START]

        def at(name, shape, dt=F32, offset=None):
            size = 4 * int(np.prod(shape[1:]))
            if offset is None:
                offset = place[0]
                place[0] += (size + 31) // 32 * 32
            return nc.alloc_sbuf_tensor_at(name, shape, dt, offset=offset), offset

        x, _ = at("x", [P, KD, T])
        hs, _ = at("hs", [P, 2, KD, T], F32R)
        ring, _ = at("ring", [P, RING, SLOT])
        wsp, wsp_at = at("wsp", [P, SPLIT, 2, SLOT], F32R)
        wal, _ = at("wal", [P, SPLIT * 2 * SLOT], F32, wsp_at)
        cst, _ = at("cst", [P, NCONST])
        col, _ = at("col", [P, NCOLS])
        ext, _ = at("ext", [P, 2 * T + 2 * DH])
        tmp, _ = at("tmp", [P, 6, T])
        arena, arena_at = at("arena", [P, 74 * 256])
        hids, _ = at("hids", [P, 2, NG, T], F32R, arena_at)
        mod, _ = at("mod", [P, 48])
        gain, _ = at("gain", [P, 32])
        gates, _ = at("gates", [P, NT, 24])
        widx, _ = at("widx", [P, NT, 4])
        best8, _ = at("best8", [P, 8])
        smin, _ = at("smin", [P, 3])
        ssum, _ = at("ssum", [P, 2, HEADS])
        coef, _ = at("coef", [P, HEADS])
        coef2, _ = at("coef2", [P, HEADS])
        cmin, _ = at("cmin", [P, HEADS])
        epsc, _ = at("epsc", [P, 3])
        sbg, _ = at("sbg", [P, 2])
        omka, _ = at("omka", [P, 4])
        ends, _ = at("ends", [P, 4, NCH])
        ropein, ropet, relu_t = tmp[:, 0:2, :], tmp[:, 2:4, :], tmp[:, 4:6, :]
        bank = ctx.enter_context(nc.psum_tensor("bank", [P, 8, T], F32))

        def const(name):
            a, b = CONST[name]
            return cst[:, a:b]

        def vec(name, i=0, n=1):
            return col[:, COLS[name][0] + i:COLS[name][0] + i + n]

        def area(at, shape):
            n = int(np.prod(shape))
            v = arena[:, at:at + n]
            if len(shape) == 2:
                v = v.rearrange("p (a b) -> p a b", a=shape[0])
            if len(shape) == 3:
                v = v.rearrange("p (a b c) -> p a b c", a=shape[0], b=shape[1])
            if len(shape) == 4:
                v = v.rearrange("p (a b c d) -> p a b c d", a=shape[0], b=shape[1], c=shape[2])
            return v

        K = 1024 // 4
        ybuf, sq = area(38 * K, (KD, T)), area(54 * K, (KD, T))
        ftmp, ht = tmp[:, 0:2, :], tmp[:, 0:4, :]
        rstd, root_ms = tmp[:, 4, :], tmp[:, 5, :]
        ada_in, ada_acc = area(0, (2, KD, ADA)), area(16 * K, (2, ADA))
        proj = area(18 * K, (16, T))
        cos, sin = area(50 * K, (T,)), area(52 * K, (T,))
        vtok = area(54 * K, (NT, VCOLS))
        score = area(60 * K, (3, T))
        QI, KI, QD, KDD, KC, VC, KSL, KW, QN = 0, 2, 3, 7, 8, 9, 10, 11, 12
        blk = area(0, (CMP_L, CMP_N))
        hidc = area(4 * K, (2, 2, CMP_N))
        kcmp = area(4 * K + 128, (CMP_N,))
        vcmp = area(5 * K, (2, 4 * DH))
        cs = area(7 * K, (2, HEADS, CMP_N))
        cpt = area(9 * K, (2, P))
        otok = area(10 * K, (2, D))
        sneg = [area(at * K, (T,)) for at in (66, 68, 70)]
        prob = [area(at * K, (T,)) for at in (50, 52, 72)]
        probT = [tmp[:, at, :] for at in (3, 4, 5)]
        heads8 = tmp[:, 2, :].rearrange("p (a b) -> p a b", a=HEADS)
        qk2 = area(0, (8, T))
        vtok2 = area(16 * K, (NT, T))
        AT0 = (0, 512, 896, 1152)
        sp = area(24 * K, (2, 1280))
        att = area(34 * K, (2, 1280))
        u = area(44 * K, (14, T))
        osb, shift = tmp[:, 0:4, :], tmp[:, 4:6, :]
        osb_tmp = area(24 * K, (4, T))
        ar = area(0, (4, NT, 2, P))
        bt, kt = area(16 * K, (4, T)), area(24 * K, (4, T))
        sg, csum, e1, e2, e3, av = [area((32 + 2 * i) * K, (T,)) for i in range(6)]
        AT = area(32 * K, (4, 4 * P))
        Z = area(44 * K, (4, P))
        MT = area(48 * K, (2, 4, DH))
        St = area(50 * K, (2, 4, DH))
        ywkv = area(52 * K, (4, T))
        reset = area(72 * K, (T,))
        vtk = wal[:, 0:NT * T].rearrange("p (a b) -> p a b", a=NT)
        tok3 = wal[:, 8 * K:14 * K].rearrange("p (a b) -> p a b", a=3)
        PP = wal[:, 14 * K:22 * K].rearrange("p (a b c) -> p a b c", a=2, b=2)
        UR, UK, UV, UWA, UG = 0, 4, 8, 12, 13
        RW_ORDER = [12] + list(range(4, 8)) + list(range(0, 4)) + list(range(8, 12)) + [13]

        jobs = [(t, br, hh) for t in range(NT) for br in range(3) for hh in range(HEADS)]
        steps = [(hh, c) for hh in range(HEADS) for c in (3, 2, 1, 0)]
        SLOTS = 14
        slot_steps = [list(range(3 * n, min(3 * n + 3, 32))) for n in range(SLOTS)]

        NORMS = ["pre1", "post1", "f1", "post2", "g1", "mix", "g2"]
        HNORMS = ["pre1", "f1", "g1", "mix", "g2"]
        last = {}
        tile_done = []
        parts_done = []
        block = ctx.enter_context(nc.Block())

        @block.tensor
        def _(pe):
            def claim(b, sem, value):
                if b in last:
                    pe.wait_ge(*last[b])
                last[b] = (S(sem), value)

            def take_whole(name, sem, value):
                i = len(tile_done)
                assert STREAM[i][0] == name, (STREAM[i], name)
                tile_done.append((S(sem), value))
                pe.wait_ge(S(f"slot{i % RING}"), 16 * (i // RING + 1))
                return ring[:, i % RING, 0:STREAM[i][2]]

            def take(name, width, sem, value):
                i, s = len(tile_done), len(parts_done)
                assert STREAM[i][0] == name, (STREAM[i], name)
                tile_done.append((S("w_lo"), s + 1))
                parts_done.append((S(sem), value))
                pe.wait_ge(S("w_lo"), s + 1)
                return [wsp[:, s % SPLIT, part, 0:STREAM[i][2]].rearrange("p (k m) -> p k m", m=width) for part in (0, 1)]

            def product(out, lhs, rhs, start, stop):
                pe.matmul(out, lhs[0], rhs[0], start=start, stop=False)
                pe.matmul(out, lhs[0], rhs[1], start=False, stop=False)
                return pe.matmul(out, lhs[1], rhs[0], start=False, stop=stop)

            def gemm(name, b, kc, src, full, value, ready=None):
                w = take(name, P, full, value)
                for k in range(kc):
                    if ready:
                        pe.wait_ge(S(ready[0]), ready[1] + k + 1)
                    mm = product(bank[:, b, :], [v[:, k, :] for v in w], [src[:, part, k, :] for part in (0, 1)],
                                 k == 0, k == kc - 1)
                mm.then_inc(S(full), 1)

            def token_gemm(name, tiles, kc, width, full, freed):
                for t in range(NT):
                    claim(t, freed, t + 1)
                for j in range(tiles):
                    end = j == tiles - 1
                    w = take(name, width, full if end else name + "_part", NT if end else j + 1)
                    for t in range(NT):
                        for kk in range(kc):
                            k = kc * j + kk
                            if t == 0 and name == "w_v":
                                pe.wait_ge(S("h"), k + 1)
                            mm = product(bank[:, t, 0:width], [hs[:, part, k, t * P:(t + 1) * P] for part in (0, 1)],
                                         [v[:, kk, :] for v in w], k == 0, k == KD - 1)
                        if end:
                            mm.then_inc(S(full), 1)
                    if not end:
                        mm.then_inc(S(name + "_part"), 1)

            def sumsq(tag, k, src=sq):
                pe.wait_ge(S("sq"), KD * NORMS.index(tag) + k + 1)
                mm = pe.matmul(bank[:, 4, :], const("ones"), src[:, k, :], start=(k == 0), stop=(k == KD - 1))
                if k == KD - 1:
                    mm.then_inc(S("ms"), 1)

            def norm(tag, src=sq):
                claim(4, "rms", NORMS.index(tag) + 1)
                for k in range(KD):
                    sumsq(tag, k, src)

            def ada_cols(i):
                pe.wait_ge(S("ada_acc"), i + 1)
                claim(7, "mod", i + 1)
                for j in range(2):
                    mm = pe.matmul(bank[:, 7, 2 * i + j:2 * i + j + 1], ada_acc[:, i % 2, j * P:(j + 1) * P],
                                   const("ones")[:, 0:1], start=True, stop=True)
                mm.then_inc(S("ada_cols"), 1)

            pe.wait_ge(S("consts"), 16)
            norm("pre1")
            for i in range(8):
                ada_cols(i)
            token_gemm("w_v", 2, 4, VCOLS, "vtok_full", "vtok")

            def turn(n):
                pe.wait_ge(S("ropein"), n + 1)
                if n == VC:
                    return
                claim(4 + n % 2, "roped", n + 1)
                pe.matmul(bank[:, 4 + n % 2, :], const("turn"), ropein[:, n % 2, :], start=True, stop=True)\
                  .then_inc(S("turned"), 1)

            def logits(j):
                t, i = 1 + j // 4, j % 4
                pe.wait_ge(S("roped"), 3)
                claim(6, "relu_logits", j + 1)
                b = 64 * (i % 2)
                pe.matmul(bank[:, 6, 0:(t + 1) * P], proj[b:b + DH, QI + i // 2, t * P:(t + 1) * P],
                          proj[b:b + DH, KI, 0:(t + 1) * P], start=True, stop=True).then_inc(S("logits"), 1)

            for n in range(16):
                claim(n % 4, "ropein", n + 1)
                gemm("w_in", n % 4, KD, hs, "proj_full", n + 1)
                if n >= 1:
                    turn(n - 1)
                if 4 <= n < 7:
                    for j in range(4):
                        logits(4 * (n - 4) + j)
                if n >= 1:
                    ada_cols(8 + n - 1)
            turn(15)
            ada_cols(NADA - 1)
            if stop < 2:
                return
            for m, name in enumerate(("cmp1k", "cmp1v")):
                ws = [take_whole(name, "cmp_hid", m + 1).rearrange("p (l m) -> p l m", m=P) for _ in range(3)]
                pe.wait_ge(S("cmp_blocks"), m + 1)
                for g in range(2):
                    claim(2 * m + g, "cmp_gelu", 2 * m + g + 1)
                for l in range(CMP_L):
                    for g in range(2):
                        mm = pe.matmul(bank[:, 2 * m + g, 0:CMP_N],
                                       ws[l // 11][64 * g:64 * g + DH, l % 11, :], blk[64 * g:64 * g + DH, l, :],
                                       start=(l == 0), stop=(l == CMP_L - 1))
                mm.then_inc(S("cmp_hid"), 1)
            pe.wait_ge(S("cmp_gelu"), 4)
            claim(5, "cmp_kv", 1)
            for g in range(2):
                pe.matmul(bank[64 * g:64 * g + DH, 5, 0:CMP_N], ext[:, 2 * T:2 * T + DH], hidc[:, 0, g, :],
                          start=True, stop=True)
                for i in range(4):
                    mm = pe.matmul(bank[32 * i:32 * i + CMP_N, 5, 64 + 64 * g:128 + 64 * g], hidc[:, 1, g, :],
                                   ext[:, 2 * T + DH:2 * T + 2 * DH], start=True, stop=True)
            mm.then_inc(S("cmp_out"), 1)
            if stop < 3:
                return

            def qk(j):
                t, br, hh = jobs[j]
                kv = (t + 1) * P
                b = 64 * (hh // 4) if br < 2 else 64 * (hh % 2)
                q = QN + hh % 4 if br < 2 else QD + hh // 2
                claim(j % 3, "smin", j + 1)
                pe.matmul(bank[:, j % 3, 0:kv], proj[b:b + DH, q, t * P:(t + 1) * P],
                          proj[b:b + DH, (KSL, KW, KDD)[br], 0:kv], start=True, stop=True).then_inc(S("scores"), 1)

            def turn_probs(j):
                pe.wait_ge(S("probs"), j + 1)
                claim(3 + j % 2, "probT", j + 1)
                for i in range(jobs[j][0] + 1):
                    mm = pe.transpose(bank[:, 3 + j % 2, i * P:(i + 1) * P], prob[j % 3][:, i * P:(i + 1) * P],
                                      const("ident"))
                mm.then_inc(S("probs_turned"), 1)

            def pv(j):
                t, br, hh = jobs[j]
                vc = ((hh // 4) * DH, P + (hh // 4) * DH, 2 * P)[br]
                pe.wait_ge(S("probT"), j + 1)
                o = 3 * t + br
                if hh == 0:
                    claim(5 + o % 2, "otok", o + 1)
                for i in range(t + 1):
                    mm = pe.matmul(bank[:, 5 + o % 2, hh * DH:(hh + 1) * DH], probT[j % 3][:, i * P:(i + 1) * P],
                                   vtok[:, i, vc:vc + DH], start=(i == 0), stop=(i == t))
                mm.then_inc(S("pv"), 1)

            def cmp_scores(t):
                claim(7, "cmp_masked", t + 1)
                for hh in range(HEADS):
                    b = 64 * (hh // 4)
                    mm = pe.matmul(bank[:, 7, hh * CMP_N:(hh + 1) * CMP_N],
                                   proj[b:b + DH, QN + hh % 4, t * P:(t + 1) * P], kcmp[b:b + DH, :],
                                   start=True, stop=True)
                    if hh == 3:
                        mm.then_inc(S("cmp_half"), 1)
                        pe.wait_ge(S("cmp_half"), t + 1)
                mm.then_inc(S("cmp_scores"), 1)

            def cmp_turn(t):
                pe.wait_ge(S("cmp_probs"), t + 1)
                claim(7, "cmp_probT", t + 1)
                for g in range(2):
                    mm = pe.transpose(bank[:, 7, g * P:(g + 1) * P],
                                      cs[:, 1, 4 * g:4 * g + 4, :].rearrange("p a b -> p (a b)"), const("ident"))
                mm.then_inc(S("cmp_turned"), 1)

            def cmp_out(t):
                pe.wait_ge(S("cmp_probT"), t + 1)
                claim(7, "cmp_otok", t + 1)
                for g in range(2):
                    mm = pe.matmul(bank[:, 7, g * 256:(g + 1) * 256], cpt[:, g, :], vcmp[:, g, :],
                                   start=True, stop=True)
                mm.then_inc(S("cmp_pv"), 1)

            def turn_out(t):
                pe.wait_ge(S("otok"), 3 * t + 3)
                for half in range(2):
                    claim(7, "oT", 2 * t + half + 1)
                    for c in range(4):
                        mm = pe.transpose(bank[:, 7, c * P:(c + 1) * P],
                                          otok[:, t % 2, (4 * half + c) * P:(4 * half + c + 1) * P], const("ident"))
                    mm.then_inc(S("out_turned"), 1)

            pe.wait_ge(S("cmp_kv"), 1)
            pe.wait_ge(S("roped"), 16)
            n = len(jobs)
            for j in range(n + 3):
                if j < n:
                    qk(j)
                    if j % 24 == 0:
                        cmp_scores(j // 24)
                    if j % 24 == 4:
                        cmp_turn(j // 24)
                    if j % 24 == 7:
                        cmp_out(j // 24)
                if 2 <= j < n + 2:
                    turn_probs(j - 2)
                if 3 <= j:
                    pv(j - 3)
                if j >= 24 and j % 24 == 11:
                    turn_out(j // 24 - 1)
            turn_out(NT - 1)
            if stop < 4:
                return

            def post_gemm(tag, name, n_parts, part, kc, src, ready, at):
                if part == n_parts - 1:
                    claim(4, "rms", NORMS.index("post" + tag) + 1)
                for n in range(KD):
                    v = KD * (int(tag) - 1 + part) + n + 1
                    claim(n % 4, "y_read", v)
                    gemm(name, n % 4, kc, src, "y_full", v, (ready, at) if n == 0 else None)
                    if part == n_parts - 1 and n >= 1:
                        sumsq("post" + tag, n - 1)
                if part == n_parts - 1:
                    sumsq("post" + tag, KD - 1)

            pe.wait_ge(S("oT"), 2 * NT)
            post_gemm("1", "w_out", 1, 0, KD, hs, "oT", 0)
            norm("f1")
            if stop < 5:
                return
            for q in range(FF1_PARTS):
                for n in range(8):
                    claim(n % 4, "relu", 8 * q + n + 1)
                    gemm("w_up", n % 4, KD, hs, "up_full", 8 * q + n + 1,
                         ("h", KD * HNORMS.index("f1")) if q == 0 and n == 0 else None)
                post_gemm("2", "w_down", FF1_PARTS, q, 8, hids, "hid", 8 * q)
            norm("g1")
            if stop < 6:
                return

            def swiglu_gemms(m, i, tag=None):
                for half in range(2):
                    for n in range(NG):
                        b = 2 * (n % 2)
                        v = NG * (2 * (int(m) - 1) + half) + n + 1
                        claim(b, "silu", v)
                        gemm("gate" + m, b, KD, hs, "gate_full", v,
                             ("h", KD * HNORMS.index("g" + m)) if n == 0 and half == 0 else None)
                        claim(b + 1, "gated", v)
                        gemm("up" + m, b + 1, KD, hs, "gate_up_full", v)
                    if tag and half:
                        claim(4, "rms", NORMS.index(tag) + 1)
                    for n in range(KD):
                        v = KD * (i + half) + n + 1
                        claim(n % 4, "x_added", v)
                        gemm("down" + m, n % 4, NG, hids, "add_full", v,
                             ("hid2", NG * (2 * (int(m) - 1) + half)) if n == 0 else None)
                        if tag and half and n >= 1:
                            sumsq(tag, n - 1)
                if tag:
                    sumsq(tag, KD - 1)

            swiglu_gemms("1", 0, "mix")
            if stop < 7:
                return

            def head_norm(n):
                pe.wait_ge(S("qk_sq"), n + 1)
                claim(4 + n % 2, "qk_root", n + 1)
                pe.matmul(bank[:, 4 + n % 2, :], const("pair"), ropein[:, n % 2, :], start=True, stop=True)\
                  .then_inc(S("qk_ms"), 1)

            for n in range(8):
                claim(n % 4, "qk2", n + 1)
                gemm("w_in2", n % 4, KD, hs, "qk_full", n + 1, ("h", KD * HNORMS.index("mix")) if n == 0 else None)
                if n >= 1:
                    head_norm(n - 1)
            head_norm(7)
            token_gemm("w_v2", 4, 2, T, "vtok2_full", "vtok2")
            if stop < 8:
                return

            def sb_scores(s):
                hh, c = steps[s]
                b = 64 * (hh % 2)
                claim(2 + s % 3, "att_copy", s + 1)
                pe.matmul(bank[:, 2 + s % 3, 0:T - c * P], qk2[b:b + DH, 4 + hh // 2, c * P:(c + 1) * P],
                          qk2[b:b + DH, hh // 2, c * P:T], start=True, stop=True).then_inc(S("sb_scores"), 1)

            def sb_suffix(s):
                hh, c = steps[s]
                pe.wait_ge(S("softplus"), s + 1)
                w = T - c * P
                mm = pe.matmul(bank[:, 2 + s % 3, 0:w], const("suffix"), sp[:, hh % 2, AT0[c]:AT0[c] + w],
                               start=False, stop=(c == 3), skip_group_check=True)
                for cc in range(c + 1, NT):
                    ww = T - cc * P
                    mm = pe.matmul(bank[:, 2 + s % 3, w - ww:w], const("minus"), sp[:, hh % 2, AT0[cc]:AT0[cc] + ww],
                                   start=False, stop=(cc == NT - 1), skip_group_check=True)
                mm.then_inc(S("sb_suffix"), 1)

            def sb_pv(hh):
                pe.wait_ge(S("att"), 4 * hh + 4)
                b, o = 64 * (hh % 2), 5 + (hh // 2) % 2
                if hh % 2 == 0:
                    claim(o, "osb", hh // 2 + 1)
                for c in range(NT):
                    mm = pe.matmul(bank[b:b + DH, o, c * P:T], vtok2[:, c, hh * DH:(hh + 1) * DH],
                                   att[:, hh % 2, AT0[c]:AT0[c] + T - c * P], start=(c == 0), stop=(c == NT - 1),
                                   skip_group_check=True)
                mm.then_inc(S("sb_pv"), 1)

            pe.wait_ge(S("qk2"), 8)
            pe.wait_ge(S("vtok2"), NT)
            for n in range(SLOTS):
                for s in slot_steps[n]:
                    sb_scores(s)
                claim(n % 2, "u_raw", n + 1)
                gemm("w_in2", n % 2, KD, hs, "u_full", n + 1)
                if n >= 1:
                    for s in slot_steps[n - 1]:
                        if s % 4 == 3:
                            sb_pv(s // 4)
                for s in slot_steps[n]:
                    sb_suffix(s)
            if stop < 9:
                return
            for n in range(4):
                pe.wait_ge(S("osb_sq"), n + 1)
                claim(2 + n % 2, "osb_root", n + 1)
                pe.matmul(bank[:, 2 + n % 2, :], const("pair"), osb_tmp[:, n % 2, :], start=True, stop=True)\
                  .then_inc(S("osb_ms"), 1)
            pe.wait_ge(S("shifted"), 14)
            for t in range(NT):
                claim(4 + t % 2, "vtk", t + 1)
                for c in range(4):
                    mm = pe.transpose(bank[:, 4 + t % 2, c * P:(c + 1) * P], u[:, UV + c, t * P:(t + 1) * P],
                                      const("ident"))
                mm.then_inc(S("v_turned"), 1)
            pe.wait_ge(S("tanh"), 1)
            for c in range(4):
                claim(0, "sg", c + 1)
                pe.matmul(bank[:, 0, :], ext[0:DH, c * P:(c + 1) * P], u[0:DH, UWA, :], start=True, stop=True)\
                  .then_inc(S("w_full"), 1)
                claim(1, "av", c + 1)
                pe.matmul(bank[:, 1, :], ext[DH:P, c * P:(c + 1) * P], u[DH:P, UWA, :], start=True, stop=True)\
                  .then_inc(S("a_full"), 1)
                pe.wait_ge(S("kk_sq"), c + 1)
                claim(6, "kk_max", c + 1)
                pe.matmul(bank[:, 6, :], const("pair"), ropein[:, 1, :], start=True, stop=True)\
                  .then_inc(S("kk_ms"), 1)
                pe.wait_ge(S("rkr"), c + 1)
                claim(7, "bonus", c + 1)
                pe.matmul(bank[:, 7, :], const("pair"), ropet[:, 1, :], start=True, stop=True)\
                  .then_inc(S("bonus_full"), 1)
            if stop < 10:
                return
            pe.wait_ge(S("wkv_in"), 4)
            pe.wait_ge(S("vtk"), NT)
            pe.wait_ge(S("state0"), 1)

            def head_at(hf, i):
                hh = 4 * hf + i
                return hh, hh // 2, 64 * (hh % 2)

            for w in range(NT):
                for i, src in enumerate(("a", "b", "k")):
                    claim(5 + i, "tok3", 3 * w + i + 1)
                    for c in range(4):
                        f = ar[:, c, w, 0, :] if i == 0 else (bt, kt)[i - 1][:, c, w * P:(w + 1) * P]
                        mm = pe.transpose(bank[:, 5 + i, c * P:(c + 1) * P], f, const("ident"))
                    mm.then_inc(S("tok3_full"), 1)
                for hf in range(2):
                    g = 2 * w + hf
                    for i in range(4):
                        hh, c, b = head_at(hf, i)
                        claim(i, "pairs", 4 * g + i + 1)
                        arw = ar[b:b + DH, c, w, :, :].rearrange("p a t -> p (a t)")
                        pe.matmul(bank[:, i, 0:256], bt[b:b + DH, c, w * P:(w + 1) * P], arw, start=True, stop=True)
                        pe.matmul(bank[:, i, 256:512], kt[b:b + DH, c, w * P:(w + 1) * P], arw,
                                  start=True, stop=True).then_inc(S("pairs_full"), 1)
                    claim(4, "power", 5 * g + 1)
                    claim(7, "power", 5 * g + 1)
                    for i in range(4):
                        hh, c, b = head_at(hf, i)
                        mm = pe.matmul(bank[:, 4 + 3 * (i % 2), (i // 2) * P:(i // 2 + 1) * P], ar[b:b + DH, c, w, 0, :],
                                       bt[b:b + DH, c, w * P:(w + 1) * P], start=True, stop=True)
                    mm.then_inc(S("power_full"), 1)
                    claim(5, "z", 7 * g + 1)
                    for i in range(4):
                        hh, c, b = head_at(hf, i)
                        pe.wait_ge(S("pairs"), 4 * g + i + 1)
                        mm = pe.matmul(bank[:, 5, i * DH:(i + 1) * DH], AT[:, i, 2 * P:3 * P],
                                       vtk[:, w, hh * DH:(hh + 1) * DH], start=True, stop=True)
                    mm.then_inc(S("z_full"), 1)
                    for lv in range(6):
                        now, nxt = lv % 2, (lv + 1) % 2

                        def powT(i):
                            return AT[:, i, 0:P] if lv == 0 else PP[:, now, 1, i * P:(i + 1) * P]

                        pe.wait_ge(S("power"), 5 * g + min(lv, 4) + 1)
                        if lv >= 1:
                            pe.wait_ge(S("powerT"), 5 * g + lv)
                        if lv < 5:
                            claim(6, "powerT", 5 * g + lv + 1)
                            for i in range(4):
                                mm = pe.matmul(bank[:, 6, i * P:(i + 1) * P], PP[:, now, 0, i * P:(i + 1) * P],
                                               powT(i), start=True, stop=True)
                            mm.then_inc(S("powerT_full"), 1)
                            if lv < 4:
                                claim(4, "power", 5 * g + lv + 2)
                                for i in range(4):
                                    mm = pe.matmul(bank[:, 4, i * P:(i + 1) * P], powT(i),
                                                   PP[:, now, 0, i * P:(i + 1) * P], start=True, stop=True)
                                mm.then_inc(S("power_full"), 1)
                        pe.wait_ge(S("z"), 7 * g + lv + 1)
                        claim(5, "z", 7 * g + lv + 2)
                        for i in range(4):
                            mm = pe.matmul(bank[:, 5, i * P:(i + 1) * P], powT(i), Z[:, i, :], start=True, stop=True)
                        mm.then_inc(S("z_full"), 1)
                    pe.wait_ge(S("z"), 7 * g + 7)
                    for bb in (7, 3, 6):
                        claim(bb, "mt", g + 1)
                    for i in range(4):
                        hh, c, b = head_at(hf, i)
                        pe.matmul(bank[b:b + DH, 7, (i // 2) * P:(i // 2 + 1) * P], Z[:, i, 0:DH], AT[:, i, P:2 * P],
                                  start=True, stop=True)
                        for j in range(2):
                            mm = pe.matmul(bank[b:b + DH, 3 + 3 * j, (i // 2) * DH:(i // 2 + 1) * DH],
                                           Z[64 * j:64 * j + DH, i, 0:DH],
                                           tok3[64 * j:64 * j + DH, 1, hh * DH:(hh + 1) * DH], start=True, stop=True)
                    mm.then_inc(S("mt_full"), 1)
                    claim(0, "wkv", g + 1)
                    for i in range(4):
                        hh, c, b = head_at(hf, i)
                        o = bank[b:b + DH, 0, (i // 2) * P:(i // 2 + 1) * P]
                        pe.matmul(o, vtk[:, w, hh * DH:(hh + 1) * DH], AT[:, i, 3 * P:4 * P], start=(i < 2), stop=False,
                                  skip_group_check=True)
                        pe.matmul(o, Z[:, i, DH:P], AT[:, i, P:2 * P], start=False, stop=False, skip_group_check=True)
                    for j in range(2):
                        claim(1 + j, "state", 2 * g + j + 1)
                        for i in range(4):
                            hh, c, b = head_at(hf, i)
                            rows = slice(64 * j, 64 * j + DH)
                            o = bank[b:b + DH, 1 + j, (i // 2) * DH:(i // 2 + 1) * DH]
                            pe.matmul(o, tok3[rows, 1, hh * DH:(hh + 1) * DH], Z[rows, i, DH:P], start=(i < 2), stop=False,
                                      skip_group_check=True)
                            mm = pe.matmul(o, tok3[rows, 2, hh * DH:(hh + 1) * DH], vtk[rows, w, hh * DH:(hh + 1) * DH],
                                           start=False, stop=False, skip_group_check=True)
                        mm.then_inc(S("state_part"), 1)
                    pe.wait_ge(S("mt"), g + 1)
                    pe.wait_ge(S("state_part"), 2 * g + 2)
                    for j in range(2):
                        n2 = 2 * g + j
                        if n2 >= 1:
                            pe.wait_ge(S("state"), n2)
                        for i in range(4):
                            hh, c, b = head_at(hf, i)
                            o = bank[b:b + DH, 1 + j, (i // 2) * DH:(i // 2 + 1) * DH]
                            mm = pe.matmul(o, MT[b:b + DH, j, c, :], St[b:b + DH, 0, c, :] if j == 0 else St[b:b + DH, 1, c, :],
                                           start=False, stop=True, skip_group_check=True)
                        mm.then_inc(S("state_full"), 1)
                        for i in range(4):
                            hh, c, b = head_at(hf, i)
                            mm = pe.matmul(bank[b:b + DH, 0, (i // 2) * P + 64 * j:(i // 2) * P + 64 * j + 64],
                                           St[b:b + DH, j, c, :], ar[b:b + DH, c, w, 1, 64 * j:64 * j + 64],
                                           start=False, stop=(j == 1), skip_group_check=True)
                    mm.then_inc(S("wkv_full"), 1)
            if stop < 11:
                return
            pe.wait_ge(S("wkv"), 8)
            pe.wait_ge(S("sig_g"), 1)
            for c in range(4):
                claim(0, "yc", c + 1)
                pe.matmul(bank[:, 0, :], const("pair"), ywkv[:, c, :], start=True, stop=True).then_inc(S("y_sum"), 1)
                pe.wait_ge(S("yc_sq"), c + 1)
                claim(1, "y_root", c + 1)
                pe.matmul(bank[:, 1, :], const("pair"), ropein[:, 1, :], start=True, stop=True)\
                  .then_inc(S("y_ms"), 1)
                claim(2, "o_rw", c + 1)
                pe.matmul(bank[:, 2, :], ext[:, T + c * P:T + (c + 1) * P], u[:, UG, :], start=True, stop=True)\
                  .then_inc(S("g_full"), 1)
            pe.wait_ge(S("o_sb"), 4)
            claim(4, "rms", NORMS.index("g2") + 1)
            for n in range(KD):
                claim(n % 4, "x_added", KD * 2 + n + 1)
                if n == 0:
                    pe.wait_ge(S("o_rw"), 4)
                gemm("w_out2", n % 4, KD, hs, "add_full", KD * 2 + n + 1)
                if n >= 1:
                    sumsq("g2", n - 1)
            sumsq("g2", KD - 1)
            if stop < 12:
                return
            swiglu_gemms("2", 3)

        @block.scalar
        def _(act):
            step = [0]

            mine = {}

            def own(name):
                mine[name] = mine.get(name, 0) + 1
                act.wait_ge(S(name), mine[name])

            def do(ins):
                step[0] += 1
                ins.then_inc(S("act_step"), 1)
                act.wait_ge(S("act_step"), step[0])

            def split(upto):
                while mine.get("w_hi", 0) <= upto:
                    s = mine.get("w_hi", 0)
                    i = PARTED[s]
                    size = STREAM[i][2]
                    act.wait_ge(S(f"slot{i % RING}"), 16 * (i // RING + 1))
                    if s >= SPLIT:
                        act.wait_ge(*parts_done[s - SPLIT])
                    act.activation(wsp[:, s % SPLIT, 0, 0:size], ring[:, i % RING, 0:size], ACT.Copy)\
                       .then_inc(S("w_hi"), 1)
                    mine["w_hi"] = s + 1

            def ahead(name, n, last=None):
                split(min(PINDEX[name, n] + SPLIT, PINDEX[last or STREAM[PARTED[-1]][:2]]))

            def squares(tag, k, src):
                act.activation(sq[:, k, :], src, ACT.Square).then_inc(S("sq"), 1)

            def inverse_root(dst, src, width, eps, name):
                do(act.activation(dst, src, ACT.Ln, scale=1.0 / width, bias=eps))
                act.activation(dst, dst, ACT.Exp, scale=-0.5).then_inc(S(name), 1)
                own(name)

            def root(tag):
                act.wait_ge(S("ms"), NORMS.index(tag) + 1)
                inverse_root(rstd, bank[:, 4, :], D, epsc[:, 0:1], "rms")

            def norm_high(tag, add=None):
                for k in range(KD):
                    act.wait_ge(S("normed"), KD * HNORMS.index(tag) + k + 1)
                    if add:
                        ins = act.activation(hs[:, 0, k, :], ht[:, k % 4, :], ACT.Identity, bias=add(k))
                    else:
                        ins = act.activation(hs[:, 0, k, :], ht[:, k % 4, :], ACT.Copy)
                    ins.then_inc(S("h_hi"), 1)

            act.wait_ge(S("eps"), 3)
            act.wait_ge(S("x_in"), 16)
            for k in range(KD):
                squares("pre1", k, x[:, k, :])
            root("pre1")
            act.wait_ge(S("angles"), 2)
            do(act.activation(sin, sin, ACT.Sin))
            do(act.activation(cos, cos, ACT.Sin))
            act.sem_inc(S("cossin"), 1)
            split(2)
            norm_high("pre1", lambda k: mod[:, k:k + 1])
            for t in range(NT):
                act.wait_ge(S("vtok_full"), t + 1)
                act.activation(vtok[:, t, :], bank[:, t, 0:VCOLS], ACT.Copy).then_inc(S("vtok"), 1)
                own("vtok")
            act.wait_ge(S("vtok"), NT)
            act.activation(gates[:, :, :], vtok[:, :, 320:344], ACT.Sigmoid).then_inc(S("gates"), 1)
            own("gates")
            act.activation(widx[:, :, :], vtok[:, :, 344:348], ACT.Copy, scale=1.0 / 16).then_inc(S("gates"), 1)
            own("gates")
            split(4)
            for n in range(16):
                ahead("w_in", n, ("w_in", 15))
                act.wait_ge(S("proj_full"), n + 1)
                if n >= 2:
                    act.wait_ge(S("roped"), n - 1)
                act.activation(ropein[:, n % 2, :], bank[:, n % 4, :], ACT.Copy).then_inc(S("ropein"), 1)
                own("ropein")
                if n < NADA - 8:
                    i = n + 8
                    act.wait_ge(S(f"ada_in{i % 2}"), 16 * (i // 2 + 1))
                    for kk in range(KD):
                        ins = act.activation(ada_in[:, i % 2, kk, :], ada_in[:, i % 2, kk, :], ACT.Copy,
                                             scale=vec("c", kk))
                    ins.then_inc(S("ada_scaled"), 1)
                if 4 <= n < 7:
                    for j in range(4 * (n - 4), 4 * (n - 4) + 4):
                        t = 1 + j // 4
                        act.wait_ge(S("logits"), j + 1)
                        if j >= 2:
                            act.wait_ge(S("scored"), j - 1)
                        act.activation(relu_t[:, j % 2, 0:(t + 1) * P], bank[:, 6, 0:(t + 1) * P], ACT.Relu)\
                           .then_inc(S("relu_logits"), 1)
                        own("relu_logits")
            if stop < 2:
                return
            for m in range(2):
                act.wait_ge(S("cmp_hid"), m + 1)
                for g in range(2):
                    act.activation(hidc[:, m, g, :], bank[:, 2 * m + g, 0:CMP_N],
                                   ACT.Gelu_apprx_tanh).then_inc(S("cmp_gelu"), 1)
                    own("cmp_gelu")
            if stop < 3:
                return
            split(PINDEX["w_out", 2])

            def turned_out(t):
                for half in range(2):
                    act.wait_ge(S("out_turned"), 2 * t + half + 1)
                    act.activation(hs[:, 0, 4 * half:4 * half + 4, t * P:(t + 1) * P],
                                   bank[:, 7, :].rearrange("p (c t) -> p c t", c=4), ACT.Copy).then_inc(S("oT_hi"), 1)

            for j, (t, br, hh) in enumerate(jobs):
                kv = (t + 1) * P
                act.wait_ge(S("smin"), j + 1)
                if j >= 3:
                    act.wait_ge(S("probs_turned"), j - 2)
                o = j // HEADS
                if hh == 0 and o >= 2:
                    act.wait_ge(S("otok"), o - 1)
                act.activation(prob[j % 3][:, 0:kv], sneg[j % 3][:, 0:kv], ACT.Exp, scale=-1.0,
                               bias=smin[:, j % 3:j % 3 + 1], accum_out=ssum[:, o % 2, hh:hh + 1])\
                   .then_inc(S("probs"), 1)
                if j % 24 == 0:
                    act.wait_ge(S("cmp_shift"), t + 1)
                    act.activation(cs[:, 1, :, :], cs[:, 0, :, :], ACT.Exp, scale=-1.0).then_inc(S("cmp_exp"), 1)
                    own("cmp_exp")
                if j >= 24 and j % 24 == 11:
                    turned_out(t - 1)
            turned_out(NT - 1)
            if stop < 4:
                return

            def post(tag, name, n_parts, part):
                for n in range(KD):
                    ahead(name, n_parts * n + part)
                    if part == n_parts - 1:
                        act.wait_ge(S("y_read"), KD * (int(tag) - 1 + part) + n + 1)
                        squares("post" + tag, n, ybuf[:, n, :])
                if part == n_parts - 1:
                    root("post" + tag)

            def pre(tag, ready, at, add=None):
                for k in range(KD):
                    act.wait_ge(S(ready), at + k + 1)
                    squares(tag, k, x[:, k, :])
                root(tag)
                norm_high(tag, add)

            post("1", "w_out", 1, 0)
            pre("f1", "x_post", 0, lambda k: mod[:, 24 + k:25 + k])
            if stop < 5:
                return
            for q in range(FF1_PARTS):
                for n in range(8):
                    nn = 8 * q + n
                    ahead("w_up", nn)
                    act.wait_ge(S("up_full"), nn + 1)
                    if nn >= 2:
                        act.wait_ge(S("hid"), nn - 1)
                    act.activation(ftmp[:, n % 2, :], bank[:, n % 4, :], ACT.Relu).then_inc(S("relu"), 1)
                    own("relu")
                    act.activation(hids[:, 0, n, :], ftmp[:, n % 2, :], ACT.Square).then_inc(S("hid_hi"), 1)
                post("2", "w_down", FF1_PARTS, q)
            pre("g1", "x_post", KD)
            if stop < 6:
                return

            def silu(m, i, tag=None):
                for half in range(2):
                    for n in range(NG):
                        v = NG * (2 * (int(m) - 1) + half) + n
                        ahead("gate" + m, NG * half + n)
                        act.wait_ge(S("gate_full"), v + 1)
                        if v >= 2:
                            act.wait_ge(S("hid2"), v - 1)
                        act.activation(ftmp[:, n % 2, :], bank[:, 2 * (n % 2), :], ACT.Silu).then_inc(S("silu"), 1)
                        ahead("up" + m, NG * half + n)
                        act.wait_ge(S("gated"), v + 1)
                        act.activation(hids[:, 0, n, :], ftmp[:, n % 2, :], ACT.Copy).then_inc(S("hid2_hi"), 1)
                    for n in range(KD):
                        ahead("down" + m, 2 * n + half)
                        if tag and half:
                            act.wait_ge(S("x_added"), KD * (i + half) + n + 1)
                            squares(tag, n, x[:, n, :])

            silu("1", 0, "mix")
            root("mix")
            norm_high("mix")
            if stop < 7:
                return
            for n in range(8):
                ahead("w_in2", n)
                act.wait_ge(S("qk_full"), n + 1)
                act.activation(ropein[:, n % 2, :], bank[:, n % 4, :], ACT.Square).then_inc(S("qk_sq"), 1)
                own("qk_sq")
                act.wait_ge(S("qk_ms"), n + 1)
                if n >= 2:
                    act.wait_ge(S("qk2"), n - 1)
                inverse_root(ropet[:, n % 2, :], bank[:, 4 + n % 2, :], DH, epsc[:, 0:1], "qk_root")
            for j in range(3):
                ahead("w_v2", j)
            for t in range(NT):
                act.wait_ge(S("vtok2_full"), t + 1)
                act.activation(vtok2[:, t, :], bank[:, t, :], ACT.Copy).then_inc(S("vtok2"), 1)
                own("vtok2")
            if stop < 8:
                return
            ahead("w_v2", 3)
            for n in range(SLOTS + 1):
                if n < SLOTS:
                    for s in slot_steps[n]:
                        w = T - steps[s][1] * P
                        hh, c = steps[s]
                        z = att[:, hh % 2, AT0[c]:AT0[c] + w]
                        act.wait_ge(S("sb_scores"), s + 1)
                        if hh >= 2 and c == 3:
                            act.wait_ge(S("sb_pv"), hh - 1)
                        do(act.activation(z, bank[:, 2 + s % 3, 0:w], ACT.Abs))
                        do(act.activation(z, z, ACT.Exp, scale=-1.0))
                        act.activation(z, z, ACT.Ln, bias=epsc[:, 2:3]).then_inc(S("log1p"), 1)
                        own("log1p")
                    ahead("w_in2", 8 + n, ("w_out2", 0))
                    act.wait_ge(S("u_full"), n + 1)
                    act.activation(u[:, RW_ORDER[n], :], bank[:, n % 2, :], ACT.Copy).then_inc(S("u_raw"), 1)
                    own("u_raw")
                    for s in slot_steps[n]:
                        hh, c = steps[s]
                        a = att[:, hh % 2, AT0[c]:AT0[c] + T - c * P]
                        act.wait_ge(S("att_copy"), s + 1)
                        act.activation(a, a, ACT.Exp).then_inc(S("att"), 1)
                        own("att")
                if n >= 1:
                    for s in slot_steps[n - 1]:
                        hh = s // 4
                        if s % 8 == 7:
                            act.wait_ge(S("sb_pv"), hh + 1)
                            act.activation(osb[:, hh // 2, :], bank[:, 5 + (hh // 2) % 2, :], ACT.Copy)\
                               .then_inc(S("osb"), 1)
                            own("osb")
            if stop < 9:
                return
            for n in range(4):
                act.wait_ge(S("osb"), n + 1)
                if n >= 2:
                    act.wait_ge(S("osb_ms"), n - 1)
                act.activation(osb_tmp[:, n % 2, :], osb[:, n, :], ACT.Square).then_inc(S("osb_sq"), 1)
                own("osb_sq")
                act.wait_ge(S("osb_ms"), n + 1)
                if n >= 2:
                    act.wait_ge(S("o_sb"), n - 1)
                inverse_root(osb_tmp[:, 2 + n % 2, :], bank[:, 2 + n % 2, :], DH, epsc[:, 0:1], "osb_root")
                act.wait_ge(S("osb_normed"), n + 1)
                act.activation(hs[:, 0, n, :], osb[:, n, :], ACT.Copy).then_inc(S("o_sb_hi"), 1)
            act.wait_ge(S("o_sb"), 4)
            act.wait_ge(S("shifted"), 14)
            act.activation(u[0:DH, UWA, :], u[0:DH, UWA, :], ACT.Tanh).then_inc(S("tanh"), 1)
            own("tanh")
            act.activation(u[:, UG, :], u[:, UG, :], ACT.Sigmoid).then_inc(S("sig_g"), 1)
            own("sig_g")
            for t in range(NT):
                act.wait_ge(S("v_turned"), t + 1)
                act.activation(vtk[:, t, :], bank[:, 4 + t % 2, :], ACT.Copy).then_inc(S("vtk"), 1)
                own("vtk")
            for c in range(4):
                act.wait_ge(S("w_full"), c + 1)
                if c:
                    act.wait_ge(S("wkv_in"), c)
                act.activation(sg, bank[:, 0, :], ACT.Sigmoid, bias=vec("rw_w0", c)).then_inc(S("sg"), 1)
                own("sg")
                act.wait_ge(S("a_full"), c + 1)
                act.activation(av, bank[:, 1, :], ACT.Sigmoid, bias=vec("rw_a0", c)).then_inc(S("av"), 1)
                own("av")
                act.wait_ge(S("kk0"), c + 1)
                act.activation(ropein[:, 1, :], ropein[:, 0, :], ACT.Square).then_inc(S("kk_sq"), 1)
                own("kk_sq")
                act.wait_ge(S("kk_max"), c + 1)
                do(act.activation(ropet[:, 0, :], ropet[:, 0, :], ACT.Ln))
                act.activation(ropet[:, 0, :], ropet[:, 0, :], ACT.Exp, scale=-0.5).then_inc(S("kk_root"), 1)
                own("kk_root")
                act.wait_ge(S("csum"), 2 * c + 2)
                act.activation(e1, csum, ACT.Exp, scale=-DECAY).then_inc(S("exps"), 1)
                own("exps")
                act.activation(e2, csum, ACT.Exp, scale=DECAY).then_inc(S("exps"), 1)
                own("exps")
                act.activation(e3, e3, ACT.Exp, scale=-DECAY).then_inc(S("exps"), 1)
                own("exps")
            if stop < 10:
                return
            for w in range(NT):
                for i in range(3):
                    act.wait_ge(S("tok3_full"), 3 * w + i + 1)
                    act.activation(tok3[:, i, :], bank[:, 5 + i, :], ACT.Copy).then_inc(S("tok3"), 1)
                    own("tok3")
                for hf in range(2):
                    g = 2 * w + hf
                    for lv in range(5):
                        act.wait_ge(S("powerT_full"), 5 * g + lv + 1)
                        act.activation(PP[:, (lv + 1) % 2, 1, :], bank[:, 6, :], ACT.Copy).then_inc(S("powerT"), 1)
                        own("powerT")
                    act.wait_ge(S("wkv_full"), g + 1)
                    act.activation(ywkv[:, 2 * hf:2 * hf + 2, w * P:(w + 1) * P],
                                   bank[:, 0, 0:256].rearrange("p (c t) -> p c t", c=2), ACT.Copy).then_inc(S("wkv"), 1)
                    own("wkv")
            if stop < 11:
                return
            split(PINDEX["w_out2", 2])
            for c in range(4):
                act.wait_ge(S("yc"), c + 1)
                act.activation(ropein[:, 1, :], ropein[:, 0, :], ACT.Square).then_inc(S("yc_sq"), 1)
                own("yc_sq")
                act.wait_ge(S("y_ms"), c + 1)
                inverse_root(ropet[:, 0, :], bank[:, 1, :], DH, epsc[:, 1:2], "y_root")
                act.wait_ge(S("y_gated"), c + 1)
                act.activation(hs[:, 0, 4 + c, :], ropein[:, 0, :], ACT.Copy).then_inc(S("o_rw_hi"), 1)
            for n in range(KD):
                ahead("w_out2", n)
                act.wait_ge(S("x_added"), KD * 2 + n + 1)
                squares("g2", n, x[:, n, :])
            root("g2")
            norm_high("g2")
            if stop < 12:
                return
            silu("2", 3)

        @block.vector
        def _(dve):
            step = [0]

            mine = {}

            def own(name):
                mine[name] = mine.get(name, 0) + 1
                dve.wait_ge(S(name), mine[name])

            def do(ins):
                step[0] += 1
                ins.then_inc(S("dve_step"), 1)
                dve.wait_ge(S("dve_step"), step[0])

            for i, e in enumerate((EPS, LNX_EPS, 1.0)):
                dve.memset(epsc[:, i:i + 1], e).then_inc(S("eps"), 1)
                own("eps")
            ipos = ropet[:, 0, :]
            dve.wait_ge(S("pos_in"), 16)
            dve.wait_ge(S("consts"), 16)
            ang, k = ropein[:, 0, :], ropein[:, 1, :]
            do(dve.tensor_copy(ang, ipos.bitcast(I32)))
            do(dve.tensor_scalar(ang, ang, const("inv"), None, ALU.mult))
            do(dve.tensor_scalar(k, ang, TWO_PI_INV, MAGIC, ALU.mult, ALU.add))
            do(dve.tensor_scalar(k, k, MAGIC, None, ALU.subtract))
            for part in (PI_A, PI_B, PI_C):
                do(dve.scalar_tensor_tensor(out=ang, in0=k, scalar=-part, in1=ang, op0=ALU.mult, op1=ALU.add))
            dve.tensor_scalar(sin, ang, -PI_SAFE, PI_SAFE, ALU.max, ALU.min).then_inc(S("angles"), 1)
            own("angles")
            do(dve.tensor_scalar(k, ang, -1.0, None, ALU.mult))
            do(dve.tensor_tensor(k, k, ang, ALU.max))
            dve.tensor_scalar(cos, k, -1.0, float(np.pi / 2), ALU.mult, ALU.add).then_inc(S("angles"), 1)
            own("angles")

            def lo(upto):
                while mine.get("w_lo", 0) <= upto:
                    s = mine.get("w_lo", 0)
                    i = PARTED[s]
                    size = STREAM[i][2]
                    dve.wait_ge(S("w_hi"), s + 1)
                    dve.tensor_tensor(wsp[:, s % SPLIT, 1, 0:size], ring[:, i % RING, 0:size],
                                      wsp[:, s % SPLIT, 0, 0:size].bitcast(F32), ALU.subtract).then_inc(S("w_lo"), 1)
                    mine["w_lo"] = s + 1

            def ahead(name, n, last=None):
                lo(min(PINDEX[name, n] + SPLIT, PINDEX[last or STREAM[PARTED[-1]][:2]]))

            def ada_piece(i):
                dve.wait_ge(S(f"ada_in{i % 2}"), 16 * (i // 2 + 1))
                if i >= 2:
                    dve.wait_ge(S("ada_cols"), i - 1)
                acc = ada_acc[:, i % 2, :]
                do(dve.tensor_scalar(acc, ada_in[:, i % 2, 0, :], vec("c", 0), None, ALU.mult))
                for kk in range(1, KD):
                    ins = dve.scalar_tensor_tensor(out=acc, in0=ada_in[:, i % 2, kk, :], scalar=vec("c", kk),
                                                   in1=acc, op0=ALU.mult, op1=ALU.add)
                    if kk < KD - 1:
                        do(ins)
                ins.then_inc(S("ada_acc"), 1)
                own("ada_acc")

            def mod_cols(i):
                dve.wait_ge(S("ada_cols"), i + 1)
                dve.tensor_tensor(mod[:, 2 * i:2 * i + 2], bank[:, 7, 2 * i:2 * i + 2], vec("b_ada", 2 * i, 2),
                                  ALU.add).then_inc(S("mod"), 1)
                own("mod")

            def modulate(i, scale_at, g):
                dve.scalar_tensor_tensor(out=gain[:, 8 * i:8 * i + 8], in0=mod[:, scale_at:scale_at + 8],
                                         scalar=1.0, in1=vec(g, 0, 8), op0=ALU.add, op1=ALU.mult)\
                   .then_inc(S("gain"), 1)
                own("gain")

            def normalize(tag, scale, add=None):
                at = KD * HNORMS.index(tag)
                dve.wait_ge(S("rms"), NORMS.index(tag) + 1)
                for kk in range(KD + 1):
                    if kk < KD:
                        if kk >= 4:
                            dve.wait_ge(S("h"), at + kk - 3)
                        dve.scalar_tensor_tensor(out=ht[:, kk % 4, :], in0=x[:, kk, :], scalar=scale(kk), in1=rstd,
                                                 op0=ALU.mult, op1=ALU.mult).then_inc(S("normed"), 1)
                    if kk >= 1:
                        k = kk - 1
                        dve.wait_ge(S("h_hi"), at + k + 1)
                        v, high = ht[:, k % 4, :], hs[:, 0, k, :].bitcast(F32)
                        if add:
                            ins = dve.scalar_tensor_tensor(out=hs[:, 1, k, :], in0=v, scalar=add(k), in1=high,
                                                           op0=ALU.add, op1=ALU.subtract)
                        else:
                            ins = dve.tensor_tensor(hs[:, 1, k, :], v, high, ALU.subtract)
                        ins.then_inc(S("h"), 1)

            for i in range(8):
                ada_piece(i)
                if i:
                    mod_cols(i - 1)
            mod_cols(7)
            lo(2)
            dve.wait_ge(S("mod"), 8)
            modulate(0, 8, "g_pre_mix")
            dve.wait_ge(S("gain"), 1)
            normalize("pre1", lambda k: gain[:, k:k + 1], lambda k: mod[:, k:k + 1])

            def rope(n):
                src = ropein[:, n % 2, :]
                dve.wait_ge(S("ropein"), n + 1)
                if n == VC:
                    dve.tensor_copy(proj[:, n, :], src).then_inc(S("roped"), 1)
                    own("roped")
                    return
                scale = -DH ** -0.5 if QD <= n < QD + 4 or n >= QN else 1.0
                do(dve.scalar_tensor_tensor(out=ropet[:, 0, :], in0=src, scalar=scale, in1=cos,
                                            op0=ALU.mult, op1=ALU.mult))
                dve.wait_ge(S("turned"), n + 1 - (n > VC))
                do(dve.scalar_tensor_tensor(out=ropet[:, 1, :], in0=bank[:, 4 + n % 2, :], scalar=scale, in1=sin,
                                            op0=ALU.mult, op1=ALU.mult))
                dve.tensor_tensor(proj[:, n, :], ropet[:, 0, :], ropet[:, 1, :], ALU.add).then_inc(S("roped"), 1)
                own("roped")

            def index_score(j):
                t, i = 1 + j // 4, j % 4
                kv = (t + 1) * P
                dve.wait_ge(S("relu_logits"), j + 1)
                s = score[:, t - 1, 0:kv]
                r = relu_t[:, j % 2, 0:kv]
                if i == 0:
                    dve.tensor_scalar(s, r, widx[:, t, 0:1], None, ALU.mult).then_inc(S("scored"), 1)
                    own("scored")
                else:
                    dve.wait_ge(S("scored"), j)
                    dve.scalar_tensor_tensor(out=s, in0=r, scalar=widx[:, t, i:i + 1], in1=s, op0=ALU.mult,
                                             op1=ALU.add).then_inc(S("scored"), 1)
                    own("scored")
                if i == 3:
                    dve.wait_ge(S("scored"), j + 1)
                    do(dve.tensor_tensor(s, s, const("causal")[:, T - kv:T], ALU.subtract))

            def top_round(r):
                t, n = 1 + r // ROUNDS, r % ROUNDS
                s = score[:, t - 1, 0:(t + 1) * P]
                do(dve.max(best8[:, :], s))
                do(dve.match_replace(s, best8[:, :], s, -3.0 * NEG))
                if n == ROUNDS - 1:
                    do(dve.tensor_scalar(s, s, -2.0 * NEG, NEG, ALU.is_gt, ALU.mult))

            dve.wait_ge(S("cossin"), 1)
            dve.wait_ge(S("gates"), 2)
            rounds = 0
            lo(4)
            for n in range(16):
                if n >= 1:
                    rope(n - 1)
                ahead("w_in", n, ("w_in", 15))
                if 4 <= n < 7:
                    for j in range(4 * (n - 4), 4 * (n - 4) + 4):
                        index_score(j)
                if n >= 1:
                    mod_cols(8 + n - 1)
                while n >= 7 and rounds < 48 * (n - 6) // 9:
                    top_round(rounds)
                    rounds += 1
            rope(15)
            mod_cols(NADA - 1)
            dve.wait_ge(S("mod"), NADA)
            dve.tensor_tensor(gain[:, 8:16], mod[:, 16:24], vec("g_post_mix", 0, 8), ALU.mult).then_inc(S("gain"), 1)
            own("gain")
            modulate(2, 32, "g_pre_ffn")
            dve.tensor_tensor(gain[:, 24:32], mod[:, 40:48], vec("g_post_ffn", 0, 8), ALU.mult).then_inc(S("gain"), 1)
            own("gain")
            dve.wait_ge(S("gain"), 4)
            if stop < 2:
                return
            do(dve.memset(blk, 0.0))
            for m, (src, pe_name) in enumerate(((KC, "pe_k"), (VC, "pe_v"))):
                dve.wait_ge(S("roped"), src + 1)
                if m:
                    dve.wait_ge(S("cmp_hid"), 1)
                for half in range(2):
                    v = proj[:, src, 256 * 0 + 16 * half:16 * half + 16 * 31].rearrange("p (n l) -> p l n", l=16)
                    pe_b = vec(pe_name, 16 * half, 16)[:, :, None].to_broadcast([P, 16, 31])
                    ins = dve.tensor_tensor(blk[:, 16 * half:16 * half + 16, 0:31], v, pe_b, ALU.add)
                    if half == 0:
                        do(ins)
                ins.then_inc(S("cmp_blocks"), 1)
                own("cmp_blocks")
            do(dve.memset(vcmp, 0.0))
            dve.wait_ge(S("cmp_out"), 1)
            do(dve.tensor_copy(kcmp, bank[:, 5, 0:CMP_N]))
            for g in range(2):
                for i in range(4):
                    do(dve.tensor_copy(vcmp[32 * i:32 * i + 32, g, i * DH:(i + 1) * DH],
                                       bank[32 * i:32 * i + 32, 5, 64 + 64 * g:128 + 64 * g]))
            dve.sem_inc(S("cmp_kv"), 1)
            if stop < 3:
                return
            lo(PINDEX["w_out", 2])

            def masked(j):
                t, br, hh = jobs[j]
                kv = (t + 1) * P
                dve.wait_ge(S("scores"), j + 1)
                if j >= 3:
                    dve.wait_ge(S("probs"), j - 2)
                mask = score[:, t - 1, 0:kv] if br == 2 and t else const("causal")[:, T - kv:T]
                dve.tensor_tensor_reduce(sneg[j % 3][:, 0:kv], bank[:, j % 3, 0:kv], mask, 1.0, 3e38, ALU.add, ALU.min,
                                         smin[:, j % 3:j % 3 + 1]).then_inc(S("smin"), 1)

            def probs_turned(j):
                kv = (jobs[j][0] + 1) * P
                dve.wait_ge(S("probs_turned"), j + 1)
                if j >= 3:
                    dve.wait_ge(S("pv"), j - 2)
                dve.tensor_copy(probT[j % 3][:, 0:kv], bank[:, 3 + j % 2, 0:kv]).then_inc(S("probT"), 1)

            def wide(c):
                return c[:, :, None].to_broadcast([P, HEADS, DH])

            def add_heads(o):
                t, br = o // 3, o % 3
                dve.wait_ge(S("pv"), 8 * o + 8)
                do(dve.reciprocal(coef[:, :], ssum[:, o % 2, :]))
                pvb = bank[:, 5 + o % 2, :].rearrange("p (a b) -> p a b", a=HEADS)
                if br == 2:
                    if t >= 2:
                        dve.wait_ge(S("out_turned"), 2 * (t - 1))
                    dve.tensor_tensor(otok[:, t % 2, T:D].rearrange("p (a b) -> p a b", a=HEADS), pvb,
                                      wide(coef), ALU.mult).then_inc(S("otok"), 1)
                    own("otok")
                    return
                gate = gates[:, t, :].rearrange("p (h i) -> p h i", i=3)[:, :, br + 1]
                do(dve.tensor_tensor(coef2[:, :], coef[:, :], gate, ALU.mult))
                do(dve.tensor_tensor(heads8, pvb, wide(coef2), ALU.mult))
                dst = otok[:, t % 2, 0:T]
                dve.tensor_tensor(dst, dst, heads8.rearrange("p a b -> p (a b)"), ALU.add).then_inc(S("otok"), 1)
                own("otok")

            def turned_out(t):
                for half in range(2):
                    at = 2 * t + half + 1
                    dve.wait_ge(S("oT_hi"), at)
                    chunks = slice(4 * half, 4 * half + 4)
                    dve.tensor_tensor(hs[:, 1, chunks, t * P:(t + 1) * P], bank[:, 7, :].rearrange("p (c t) -> p c t", c=4),
                                      hs[:, 0, chunks, t * P:(t + 1) * P].bitcast(F32), ALU.subtract)\
                       .then_inc(S("oT"), 1)

            def cmp_masked(t):
                keep = const("cmp_keep")[:, t * CMP_N:(t + 1) * CMP_N]
                drop = const("cmp_drop")[:, t * CMP_N:(t + 1) * CMP_N]
                c0 = cs[:, 0, :, :]
                dve.wait_ge(S("cmp_scores"), t + 1)
                dve.tensor_tensor(c0, bank[:, 7, 0:256].rearrange("p (a b) -> p a b", a=HEADS),
                                  keep[:, None, :].to_broadcast([P, HEADS, CMP_N]), ALU.mult)\
                   .then_inc(S("cmp_masked"), 1)
                own("cmp_masked")
                dve.wait_ge(S("cmp_masked"), t + 1)
                do(dve.tensor_tensor(c0, c0, drop[:, None, :].to_broadcast([P, HEADS, CMP_N]), ALU.add))
                do(dve.tensor_reduce(cmin[:, :], c0, AX.X, ALU.min))
                dve.tensor_tensor(c0, c0, cmin[:, :, None].to_broadcast([P, HEADS, CMP_N]), ALU.subtract)\
                   .then_inc(S("cmp_shift"), 1)
                own("cmp_shift")

            def cmp_probs(t):
                keep = const("cmp_keep")[:, t * CMP_N:(t + 1) * CMP_N]
                c1 = cs[:, 1, :, :]
                dve.wait_ge(S("cmp_exp"), t + 1)
                do(dve.tensor_reduce(cmin[:, :], c1, AX.X, ALU.add))
                do(dve.reciprocal(coef[:, :], cmin[:, :]))
                gate = gates[:, t, :].rearrange("p (h i) -> p h i", i=3)[:, :, 0]
                do(dve.tensor_tensor(coef2[:, :], coef[:, :], gate, ALU.mult))
                do(dve.tensor_tensor(c1, c1, keep[:, None, :].to_broadcast([P, HEADS, CMP_N]), ALU.mult))
                dve.tensor_tensor(c1, c1, coef2[:, :, None].to_broadcast([P, HEADS, CMP_N]), ALU.mult)\
                   .then_inc(S("cmp_probs"), 1)
                own("cmp_probs")

            n = len(jobs)
            for j in range(n + 3):
                if j < n:
                    masked(j)
                    t = j // 24
                    if j % 24 == 0:
                        cmp_masked(t)
                    if j % 24 == 2:
                        cmp_probs(t)
                    if j % 24 == 5:
                        dve.wait_ge(S("cmp_turned"), t + 1)
                        dve.tensor_copy(cpt.rearrange("p a b -> p (a b)"), bank[:, 7, 0:256]).then_inc(S("cmp_probT"), 1)
                        own("cmp_probT")
                    if j % 24 == 8:
                        dve.wait_ge(S("cmp_pv"), t + 1)
                        if t >= 2:
                            dve.wait_ge(S("out_turned"), 2 * (t - 1))
                        dve.tensor_copy(otok[:, t % 2, 0:T], bank[:, 7, :]).then_inc(S("cmp_otok"), 1)
                        own("cmp_otok")
                        dve.wait_ge(S("cmp_otok"), t + 1)
                if 2 <= j < n + 2:
                    probs_turned(j - 2)
                if j >= 24 and j % 24 == 11:
                    turned_out(j // 24 - 1)
                if j >= 11 and (j - 11) % 8 == 0:
                    add_heads((j - 11) // 8)
            add_heads(11)
            turned_out(NT - 1)
            if stop < 4:
                return

            def post(tag, name, n_parts, part):
                for nn in range(KD):
                    at = KD * (int(tag) - 1 + part) + nn + 1
                    dve.wait_ge(S("y_full"), at)
                    if part == 0:
                        ins = dve.tensor_copy(ybuf[:, nn, :], bank[:, nn % 4, :])
                    else:
                        ins = dve.tensor_tensor(ybuf[:, nn, :], ybuf[:, nn, :], bank[:, nn % 4, :], ALU.add)
                    ins.then_inc(S("y_read"), 1)
                    ahead(name, n_parts * nn + part)
                dve.wait_ge(S("y_read"), KD * (int(tag) + part))

            def post_norm(tag, g_at):
                dve.wait_ge(S("rms"), NORMS.index("post" + tag) + 1)
                for nn in range(KD):
                    do(dve.tensor_tensor(ybuf[:, nn, :], ybuf[:, nn, :], rstd, ALU.mult))
                    dve.scalar_tensor_tensor(out=x[:, nn, :], in0=ybuf[:, nn, :], scalar=gain[:, g_at + nn:g_at + nn + 1],
                                             in1=x[:, nn, :], op0=ALU.mult, op1=ALU.add).then_inc(S("x_post"), 1)
                    own("x_post")

            post("1", "w_out", 1, 0)
            post_norm("1", 8)
            normalize("f1", lambda k: gain[:, 16 + k:17 + k], lambda k: mod[:, 24 + k:25 + k])
            if stop < 5:
                return
            for q in range(FF1_PARTS):
                for n in range(8):
                    nn = 8 * q + n
                    v = ftmp[:, n % 2, :]
                    ahead("w_up", nn)
                    dve.wait_ge(S("hid_hi"), nn + 1)
                    do(dve.tensor_tensor(v, v, v, ALU.mult))
                    dve.tensor_tensor(hids[:, 1, n, :], v, hids[:, 0, n, :].bitcast(F32), ALU.subtract)\
                       .then_inc(S("hid"), 1)
                post("2", "w_down", FF1_PARTS, q)
            post_norm("2", 24)
            normalize("g1", lambda k: vec("norm_ffn1_2", k))
            if stop < 6:
                return

            def swiglu(m, i):
                for half in range(2):
                    for nn in range(NG):
                        v = NG * (2 * (int(m) - 1) + half) + nn + 1
                        f = ftmp[:, nn % 2, :]
                        ahead("gate" + m, NG * half + nn)
                        dve.wait_ge(S("silu"), v)
                        dve.wait_ge(S("gate_up_full"), v)
                        dve.tensor_tensor(f, f, bank[:, 2 * (nn % 2) + 1, :], ALU.mult).then_inc(S("gated"), 1)
                        ahead("up" + m, NG * half + nn)
                        dve.wait_ge(S("hid2_hi"), v)
                        dve.tensor_tensor(hids[:, 1, nn, :], f, hids[:, 0, nn, :].bitcast(F32), ALU.subtract)\
                           .then_inc(S("hid2"), 1)
                    add_to_x(i + half, 0.5, "down" + m, 2, half)

            def add_to_x(i, scale, name, n_parts, part):
                for nn in range(KD):
                    dve.wait_ge(S("add_full"), KD * i + nn + 1)
                    dve.scalar_tensor_tensor(out=x[:, nn, :], in0=bank[:, nn % 4, :], scalar=scale, in1=x[:, nn, :],
                                             op0=ALU.mult, op1=ALU.add).then_inc(S("x_added"), 1)
                    ahead(name, n_parts * nn + part)
                dve.wait_ge(S("x_added"), KD * (i + 1))

            swiglu("1", 0)
            normalize("mix", lambda k: vec("norm_mix_2", k))
            if stop < 7:
                return
            do(dve.tensor_scalar(sbg[:, 0:1], vec("sb_q"), DH ** -0.5, None, ALU.mult))
            do(dve.tensor_copy(sbg[:, 1:2], vec("sb_k")))
            for nn in range(8):
                ahead("w_in2", nn)
                dve.wait_ge(S("qk_root"), nn + 1)
                dve.scalar_tensor_tensor(out=qk2[:, nn, :], in0=bank[:, nn % 4, :], scalar=sbg[:, nn // 4:nn // 4 + 1],
                                         in1=ropet[:, nn % 2, :], op0=ALU.mult, op1=ALU.mult).then_inc(S("qk2"), 1)
                own("qk2")
            for j in range(4):
                ahead("w_v2", j)
            if stop < 8:
                return
            for nn in range(SLOTS):
                for s in slot_steps[nn]:
                    hh, c = steps[s]
                    w = T - c * P
                    d = sp[:, hh % 2, AT0[c]:AT0[c] + w]
                    dve.wait_ge(S("log1p"), s + 1)
                    if s >= 8 and s % 4 == 0:
                        dve.wait_ge(S("sb_suffix"), s - 4)
                    do(dve.scalar_tensor_tensor(out=d, in0=bank[:, 2 + s % 3, 0:w], scalar=0.0,
                                                in1=att[:, hh % 2, AT0[c]:AT0[c] + w], op0=ALU.max, op1=ALU.add))
                    dve.tensor_tensor(d[:, 0:P], d[:, 0:P], const("before"), ALU.mult).then_inc(S("softplus"), 1)
                    own("softplus")
                ahead("w_in2", 8 + nn, ("w_out2", 0))
                for s in slot_steps[nn]:
                    hh, c = steps[s]
                    w = T - c * P
                    dve.wait_ge(S("sb_suffix"), s + 1)
                    dve.tensor_tensor(att[:, hh % 2, AT0[c]:AT0[c] + w], bank[:, 2 + s % 3, 0:w],
                                      const("notbefore")[:, 0:w], ALU.add).then_inc(S("att_copy"), 1)
                    own("att_copy")
            if stop < 9:
                return
            for nn in range(4):
                dve.wait_ge(S("osb_root"), nn + 1)
                dve.scalar_tensor_tensor(out=osb[:, nn, :], in0=osb[:, nn, :], scalar=vec("sb_out", nn),
                                         in1=osb_tmp[:, 2 + nn % 2, :], op0=ALU.mult, op1=ALU.mult)\
                   .then_inc(S("osb_normed"), 1)
                dve.wait_ge(S("o_sb_hi"), nn + 1)
                dve.tensor_tensor(hs[:, 1, nn, :], osb[:, nn, :], hs[:, 0, nn, :].bitcast(F32), ALU.subtract)\
                   .then_inc(S("o_sb"), 1)
            dve.wait_ge(S("o_sb"), 4)
            dve.wait_ge(S("shifted"), 14)
            do(dve.memset(reset, 1.0))
            do(dve.memset(reset.rearrange("p (c t) -> p c t", t=CHUNK)[:, :, 0:1], 0.0))
            do(dve.tensor_scalar(omka[:, :], vec("rw_k_a", 0, 4), -1.0, 1.0, ALU.mult, ALU.add))
            for c in range(4):
                kk, r, kx = ropein[:, 0, :], u[:, UR + c, :], u[:, UK + c, :]

                def wins(v):
                    return v.rearrange("p (w t) -> p w t", w=NT)

                if c:
                    dve.wait_ge(S("wkv_in"), c)
                dve.tensor_scalar(kk, kx, vec("rw_k_k", c), None, ALU.mult).then_inc(S("kk0"), 1)
                own("kk0")
                dve.wait_ge(S("sg"), c + 1)
                if c:
                    dve.wait_ge(S("exps"), 3 * c)
                dve.tensor_tensor_scan(csum, reset, sg, 0.0, ALU.mult, ALU.add).then_inc(S("csum"), 1)
                own("csum")
                dve.wait_ge(S("csum"), 2 * c + 1)
                dve.tensor_tensor(e3, csum, sg, ALU.subtract).then_inc(S("csum"), 1)
                own("csum")
                dve.wait_ge(S("av"), c + 1)
                do(dve.tensor_scalar(sg, av, vec("rw_k_a", c), omka[:, c:c + 1], ALU.mult, ALU.add))
                do(dve.tensor_tensor(sg, sg, kx, ALU.mult))
                if c:
                    dve.wait_ge(S("bonus_full"), c)
                dve.scalar_tensor_tensor(out=ropet[:, 1, :], in0=r, scalar=vec("rw_r_k", c), in1=sg,
                                         op0=ALU.mult, op1=ALU.mult).then_inc(S("rkr"), 1)
                own("rkr")
                dve.wait_ge(S("kk_ms"), c + 1)
                dve.tensor_scalar(ropet[:, 0, :], bank[:, 6, :], 1e-24, None, ALU.max).then_inc(S("kk_max"), 1)
                dve.wait_ge(S("kk_root"), c + 1)
                do(dve.tensor_tensor(kk, kk, ropet[:, 0, :], ALU.mult))
                dve.wait_ge(S("exps"), 3 * c + 3)
                do(dve.tensor_tensor(kt[:, c, :], sg, e2, ALU.mult))
                do(dve.scalar_tensor_tensor(out=ar[:, c, :, 0, :], in0=wins(kk), scalar=-1.0, in1=wins(e3),
                                            op0=ALU.mult, op1=ALU.mult))
                do(dve.tensor_tensor(ar[:, c, :, 1, :], wins(r), wins(e1), ALU.mult))
                do(dve.tensor_tensor(kk, kk, av, ALU.mult))
                do(dve.tensor_tensor(bt[:, c, :], kk, e2, ALU.mult))
                do(dve.tensor_copy(ends[:, c, :], e1.rearrange("p (j t) -> p j t", t=CHUNK)[:, :, CHUNK - 1]))
                dve.wait_ge(S("bonus_full"), c + 1)
                dve.wait_ge(S("v_turned"), NT)
                dve.tensor_tensor(u[:, UV + c, :], bank[:, 7, :], u[:, UV + c, :], ALU.mult).then_inc(S("bonus"), 1)
                own("bonus")
                dve.wait_ge(S("bonus"), c + 1)
                dve.sem_inc(S("wkv_in"), 1)
            if stop < 10:
                return
            dve.memset(St[:, :, :, :], 0.0).then_inc(S("state0"), 1)
            own("state0")
            dve.wait_ge(S("state0"), 1)
            quad = [P, 4, P]
            for w in range(NT):
                for hf in range(2):
                    g = 2 * w + hf
                    for i in range(4):
                        dve.wait_ge(S("pairs_full"), 4 * g + i + 1)
                        dve.tensor_tensor(AT[:, i, :], bank[:, i, :], const("chunk4"), ALU.mult).then_inc(S("pairs"), 1)
                    dve.wait_ge(S("power_full"), 5 * g + 1)
                    for i in range(2):
                        ins = dve.tensor_tensor(PP[:, 0, 0, :].rearrange("p (a o b) -> p a o b", a=2, o=2)[:, :, i, :],
                                                bank[:, 4 + 3 * i, 0:256].rearrange("p (a b) -> p a b", a=2),
                                                const("chunkT")[:, None, :].to_broadcast([P, 2, P]), ALU.mult)
                        if i == 0:
                            do(ins)
                    ins.then_inc(S("power"), 1)
                    own("power")
                    dve.wait_ge(S("tok3"), 3 * w + 3)
                    dve.wait_ge(S("z_full"), 7 * g + 1)
                    do(dve.tensor_copy(Z[:, :, DH:P], bank[:, 5, 0:256].rearrange("p (a b) -> p a b", a=4)))
                    dve.tensor_copy(Z[:, :, 0:DH], tok3[:, 0, 256 * hf:256 * hf + 256].rearrange("p (a b) -> p a b", a=4))\
                       .then_inc(S("z"), 1)
                    own("z")
                    for lv in range(6):
                        if lv < 4:
                            dve.wait_ge(S("power_full"), 5 * g + lv + 2)
                            dve.tensor_copy(PP[:, (lv + 1) % 2, 0, :], bank[:, 4, :]).then_inc(S("power"), 1)
                            own("power")
                        dve.wait_ge(S("z_full"), 7 * g + lv + 2)
                        dve.wait_ge(S("z"), 7 * g + lv + 1)
                        dve.tensor_tensor(Z[:, :, :], Z[:, :, :], bank[:, 5, :].rearrange("p (a b) -> p a b", a=4),
                                          ALU.add).then_inc(S("z"), 1)
                        own("z")
                    dve.wait_ge(S("mt_full"), g + 1)
                    rr = ar[:, 2 * hf:2 * hf + 2, w, 1, :]
                    do(dve.tensor_tensor(rr, rr, bank[:, 7, 0:256].rearrange("p (c t) -> p c t", c=2), ALU.add))
                    for j in range(2):
                        ins = dve.tensor_tensor(MT[:, j, 2 * hf:2 * hf + 2, :],
                                                bank[:, 3 + 3 * j, 0:P].rearrange("p (c k) -> p c k", c=2),
                                                const("ident64")[:, None, :].to_broadcast([P, 2, DH]), ALU.add)
                        if j == 0:
                            do(ins)
                    ins.then_inc(S("mt"), 1)
                    own("mt")
                    for j in range(2):
                        n2 = 2 * g + j
                        dve.wait_ge(S("state_full"), n2 + 1)
                        if j == 1:
                            dve.wait_ge(S("wkv_full"), g + 1)
                        e = ends[:, 2 * hf:2 * hf + 2, 2 * w + j:2 * w + j + 1].to_broadcast([P, 2, DH])
                        dve.tensor_tensor(St[:, (j + 1) % 2, 2 * hf:2 * hf + 2, :],
                                          bank[:, 1 + j, 0:128].rearrange("p (c v) -> p c v", c=2), e, ALU.mult)\
                           .then_inc(S("state"), 1)
                        own("state")
            if stop < 11:
                return
            for c in range(4):
                yy, yc = ywkv[:, c, :], ropein[:, 0, :]
                dve.wait_ge(S("y_sum"), c + 1)
                dve.scalar_tensor_tensor(out=yc, in0=bank[:, 0, :], scalar=-1.0 / DH, in1=yy, op0=ALU.mult,
                                         op1=ALU.add).then_inc(S("yc"), 1)
                own("yc")
                dve.wait_ge(S("y_root"), c + 1)
                do(dve.tensor_tensor(yc, yc, ropet[:, 0, :], ALU.mult))
                do(dve.tensor_scalar(yc, yc, vec("rw_ln_w", c), vec("rw_ln_b", c), ALU.mult, ALU.add))
                do(dve.tensor_tensor(yc, yc, u[:, UV + c, :], ALU.add))
                dve.wait_ge(S("g_full"), c + 1)
                dve.tensor_tensor(yc, yc, bank[:, 2, :], ALU.mult).then_inc(S("y_gated"), 1)
                dve.wait_ge(S("o_rw_hi"), c + 1)
                dve.tensor_tensor(hs[:, 1, 4 + c, :], yc, hs[:, 0, 4 + c, :].bitcast(F32), ALU.subtract)\
                   .then_inc(S("o_rw"), 1)
                own("o_rw")
            lo(PINDEX["w_out2", 2])
            add_to_x(2, 1.0, "w_out2", 1, 0)
            normalize("g2", lambda k: vec("norm_ffn2_2", k))
            if stop < 12:
                return
            swiglu("2", 3)

        @block.gpsimd
        def _(pool):
            step = [0]

            mine = {"ada_acc": 8}

            def own(name):
                mine[name] = mine.get(name, 0) + 1
                pool.wait_ge(S(name), mine[name])

            def do(ins):
                step[0] += 1
                ins.then_inc(S("pool_step"), 1)
                pool.wait_ge(S("pool_step"), step[0])

            pool.wait_ge(S("ada_acc"), 8)
            for i in range(8, NADA):
                v = ada_in[:, i % 2, :, :]
                pool.wait_ge(S("ada_scaled"), i - 7)
                pool.wait_ge(S("ada_cols"), i - 1)
                do(pool.tensor_tensor(v[:, 0:4, :], v[:, 0:4, :], v[:, 4:8, :], ALU.add))
                do(pool.tensor_tensor(v[:, 0:2, :], v[:, 0:2, :], v[:, 2:4, :], ALU.add))
                pool.tensor_tensor(ada_acc[:, i % 2, :], v[:, 0, :], v[:, 1, :], ALU.add).then_inc(S("ada_acc"), 1)
                own("ada_acc")
            if stop < 8:
                return
            for n in range(SLOTS):
                f = u[:, RW_ORDER[n], :]
                d = shift[:, n % 2, :]
                pool.wait_ge(S("u_raw"), n + 1)
                do(pool.tensor_scalar(d[:, 0:1], f[:, 0:1], -1.0, None, ALU.mult))
                do(pool.tensor_tensor(d[:, 1:T], f[:, 0:T - 1], f[:, 1:T], ALU.subtract))
                do(pool.tensor_scalar(d, d, vec("rw_mu", RW_ORDER[n]), None, ALU.mult))
                pool.tensor_tensor(f, f, d, ALU.add).then_inc(S("shifted"), 1)
                own("shifted")

        @block.sync
        def _(sp_eng):
            sy = sp_eng

            def ada_load(i):
                if i >= 2:
                    sy.wait_ge(S("ada_acc"), i - 1)
                sy.dma_start(ada_in[:, i % 2, :, :].rearrange("p k n -> p (k n)"), ada[i]).then_inc(S(f"ada_in{i % 2}"), 16)

            def tile_load(i):
                name, n, size = STREAM[i]
                if i >= RING:
                    sy.wait_ge(*tile_done[i - RING])
                sy.dma_start(ring[:, i % RING, 0:size], mats[name][n]).then_inc(S(f"slot{i % RING}"), 16)

            sy.dma_start(x[:, :, :].rearrange("p k t -> p (k t)"), xt).then_inc(S("x_in"), 16)
            sy.dma_start(cst[:, :], consts).then_inc(S("consts"), 16)
            sy.dma_start(ropet[:, 0, :].bitcast(I32), pos.to_broadcast([P, T])).then_inc(S("pos_in"), 16)
            sy.dma_start(col[:, :], cols).then_inc(S("cols_in"), 16)
            sy.wait_ge(S("cols_in"), 16)
            sy.dma_start(ext[:, :], extra).then_inc(S("ext_in"), 16)
            sy.wait_ge(S("ext_in"), 16)
            for i in range(8):
                ada_load(i)
                if i == 5:
                    tile_load(0)
                    tile_load(1)
            for i in range(2, len(tile_done)):
                name, n, size = STREAM[i]
                if name == "w_in" and n >= 3:
                    ada_load(n + 5)
                if STREAM[i][:2] == ("cmp1k", 0):
                    for n in range(13, 16):
                        ada_load(n + 8)
                tile_load(i)
            if stop >= 12:
                for n in range(KD):
                    sy.wait_ge(S("x_added"), 4 * KD + n + 1)
                    sy.dma_start(out[:, n * T:(n + 1) * T], x[:, n, :]).then_inc(S("stored"), 16)
                sy.wait_ge(S("stored"), 16 * KD)
            else:
                env = dict(x=x[:, :, :], h=hs[:, 0, :, :].bitcast(F32), arena=arena[:, :], mod=mod[:, :], gates=gates[:, :, :], ends=ends[:, :, :])
                for nm, val in dumps["wait"]:
                    sy.wait_ge(S(nm), val)
                for nm, dst in dumps["out"].items():
                    v = env[nm] if nm in env else arena[:, int(nm.split("_")[1]) * K:int(nm.split("_")[2]) * K]
                    if len(v.shape) == 3:
                        v = v.rearrange("p a b -> p (a b)")
                    sy.dma_start(dst, v).then_inc(S("stored"), 16)
                sy.wait_ge(S("stored"), 16 * len(dumps["out"]))
        if dumps is not None:
            dumps["nsem"] = len(sems)


def columns(v):
    return np.ascontiguousarray(np.asarray(v).reshape(-1, P).T)


def tiles(w, parts=1):
    kd, n = w.shape
    kc = kd // P // parts
    t = w.reshape(parts, kc, P, n // P, P).transpose(3, 0, 2, 1, 4)
    return np.ascontiguousarray(t.reshape(n // P * parts, P, kc * P))


def lay_out(inp):
    f = {k: np.asarray(v) for k, v in inp.items()}
    w_in = f["w_in"][0]
    cuts = np.cumsum([0, 512, 128, 128, 128, 128, 128, 128, 24, 512, 64, 64, 256, 64, 4])
    qn, kc, vc, ksl, vsl, kw, vw, gl, qd, kd, vd, qi, ki, wi = [w_in[:, a:b] for a, b in zip(cuts[:-1], cuts[1:])]
    qn = qn.reshape(D, 2, 4, DH).transpose(0, 2, 1, 3).reshape(D, 512)
    feat = np.concatenate([qi, ki, ki, qd, kd, kd, kc, vc, ksl, kw, qn], 1)
    tok = np.concatenate([vsl, vw, vd, gl, wi], 1)
    mats = {"w_in": tiles(feat),
            "w_v": np.ascontiguousarray(tok.reshape(2, 4, P, VCOLS).transpose(0, 2, 1, 3).reshape(2, P, 4 * VCOLS))}
    for name in ("k", "v"):
        w1 = f["cmp_w1_" + name][0].reshape(CMP_L, DH, P).transpose(1, 0, 2)
        w1 = np.concatenate([w1, w1], 0)
        w1 = np.concatenate([w1, np.zeros((P, 1, P), np.float32)], 1)
        mats["cmp1" + name] = np.ascontiguousarray(w1.reshape(P, 3, SLOT).transpose(1, 0, 2))
    mats["w_out"] = tiles(f["w_out"][0])
    mats["w_up"] = tiles(f["w_up"][0])
    mats["w_down"] = tiles(f["w_down"][0], 4)
    for m in ("1", "2"):
        mats["gate" + m] = tiles(f[f"ffn{m}_gate_2"][0])
        mats["up" + m] = tiles(f[f"ffn{m}_up_2"][0])
        mats["down" + m] = tiles(f[f"ffn{m}_down_2"][0], 2)
    w2 = f["w_in_2"][0]
    u = w2[:, 1536:].reshape(D, 14, P)[:, [12] + list(range(4, 8)) + list(range(4)) + list(range(8, 12)) + [13]]
    mats["w_in2"] = tiles(np.concatenate([w2[:, 0:1024], u.reshape(D, -1)], 1))
    mats["w_v2"] = np.ascontiguousarray(w2[:, 1024:1536].reshape(4, 2, P, T).transpose(0, 2, 1, 3).reshape(4, P, 2 * T))
    mats["w_out2"] = tiles(f["w_out_2"][0])
    ada = np.ascontiguousarray(f["w_ada"][0].reshape(KD, P, NADA, ADA).transpose(2, 1, 0, 3).reshape(NADA, P, KD * ADA))
    pair = lambda v: np.concatenate([v, v], -1)
    cols = [columns(f["c"][0]), columns(f["b_ada"][0])] + [columns(f[n][0]) for n in (
        "g_pre_mix", "g_post_mix", "g_pre_ffn", "g_post_ffn", "norm_ffn1_2", "norm_mix_2", "norm_ffn2_2")]
    cols += [columns(pair(f["sb_q_norm_2"][0])), columns(pair(f["sb_k_norm_2"][0])), columns(f["sb_out_norm_2"][0])]
    cols += [columns(f[n][0]) for n in ("rw_mu_2", "rw_w0_2", "rw_a0_2", "rw_k_k_2", "rw_k_a_2", "rw_r_k_2",
                                        "rw_ln_w_2", "rw_ln_b_2")]
    cols += [np.concatenate([f["cmp_pe_" + n][0].T] * 2, 0) for n in ("k", "v")]
    cols = np.ascontiguousarray(np.concatenate(cols, 1))
    lora = np.concatenate([f["rw_w2_2"][0], f["rw_a2_2"][0]], 0)
    extra = np.ascontiguousarray(np.concatenate([lora, f["rw_g2_2"][0], f["cmp_w2_k"][0], f["cmp_w2_v"][0]], 1))
    xt = np.ascontiguousarray(f["x"][0].T.reshape(KD, P, T).transpose(1, 0, 2).reshape(P, KD * T))
    arrays = {"xt": xt, "consts": CONSTS, "cols": cols, "pos": np.ascontiguousarray(f["positions"]), "ada": ada,
              "extra": extra}
    arrays.update({"m_" + k: v for k, v in mats.items()})
    return arrays


def declare(nc, arrays):
    aps = {}
    for name, a in arrays.items():
        aps[name] = nc.dram_tensor(name, a.shape, mybir.dt.from_np(a.dtype), kind="ExternalInput").ap()
    return aps


def kernel(**inputs):
    from concourse import bacc
    from concourse.bass_utils import run_bass_kernel_spmd

    nc = bacc.Bacc("TRN2", target_bir_lowering=False, num_devices=1)
    arrays = lay_out(inputs)
    aps = declare(nc, arrays)
    out = nc.dram_tensor("out", (P, KD * T), F32, kind="ExternalOutput").ap()
    mats = {k[2:]: v for k, v in aps.items() if k.startswith("m_")}
    build(nc, aps["xt"], aps["consts"], aps["cols"], aps["pos"], aps["ada"], mats, aps["extra"], out)
    r = run_bass_kernel_spmd(nc, [arrays], core_ids=[0])
    y = r.results[0]["out"]
    return np.ascontiguousarray(y.reshape(P, KD, T).transpose(2, 1, 0).reshape(1, T, D))
```

```python
from contextlib import ExitStack

import numpy as np

import concourse.bass as bass
from concourse import mybir

F32 = mybir.dt.float32
F32R = mybir.dt.float32r
I32 = mybir.dt.int32
ALU = mybir.AluOpType
ACT = mybir.ActivationFunctionType
AX = mybir.AxisListType

P = 128
T = 512
D = 1024
KD = D // P
NT = T // P
DH = 64
HEADS = 8
FF1 = 4096
FF2 = 2816
NEG = 1e30
EPS = 1e-6
LNX_EPS = 64e-5
TOPK = 128
ROUNDS = TOPK // 8
CMP_N = 32
CMP_L = 32
CHUNK = 64
NCH = T // CHUNK
DECAY = float(np.exp(np.float32(-0.5)))
TWO_PI_INV = float(np.float32(1.0 / (2.0 * np.pi)))
PI_A = 6.28125
PI_B = float(np.float32(1.9353071795e-3) - np.float32(1.9353071795e-3) % np.float32(2.0 ** -21))
PI_C = float(2.0 * np.pi - PI_A - PI_B)
MAGIC = 12582912.0
PI_SAFE = 3.1415925

CONST = {}
_parts = []


def _const(name, a):
    at = sum(x.shape[1] for x in _parts)
    CONST[name] = (at, at + a.shape[1])
    _parts.append(np.asarray(a, np.float32))


_i = np.arange(P)
_eye = np.eye(P, dtype=np.float32)
_const("ident", _eye)
_const("ones", np.ones((P, P)))
_const("pair", (_i[:, None] // DH == _i[None, :] // DH))
_const("turn", np.where(_i[None, :] % DH < 32, -(_i[:, None] == _i[None, :] + 32).astype(np.float32),
                        (_i[:, None] == _i[None, :] - 32).astype(np.float32)))
_const("causal", np.concatenate([np.zeros((P, T - P)), NEG * (_i[None, :] > _i[:, None])], 1))
_ends = np.arange(CMP_N) * 16 + CMP_L - 1
_cm = np.stack([(_ends[None, :] <= (t * P + _i)[:, None]) for t in range(NT)], 1).astype(np.float32)
_const("cmp_keep", _cm.reshape(P, -1))
_const("cmp_drop", (NEG * (1.0 - _cm)).reshape(P, -1))
_same = _i[:, None] // CHUNK == _i[None, :] // CHUNK
_lt = (_same & (_i[:, None] < _i[None, :])).astype(np.float32)
_le = (_same & (_i[:, None] <= _i[None, :])).astype(np.float32)
_const("chunk4", np.concatenate([_lt, _le, _lt, _le], 1))
_const("chunkT", _lt.T)
_const("suffix", -(_i[:, None] >= _i[None, :]).astype(np.float32))
_const("minus", -np.ones((P, P)))
_const("before", (_i[:, None] < _i[None, :]))
_const("notbefore", np.concatenate([-NEG * (_i[:, None] >= _i[None, :]), np.zeros((P, T - P))], 1))
_const("ident64", (_i[:, None] % DH == np.arange(DH)[None, :]))
_half = np.float32(10000.0) ** (-np.arange(32, dtype=np.float32) / np.float32(32))
_const("inv", np.tile(_half, 4)[:, None])
CONSTS = np.ascontiguousarray(np.concatenate(_parts, 1), np.float32)
NCONST = CONSTS.shape[1]

COLS = {}
_at = 0
for _name, _n in [("c", 8), ("b_ada", 48), ("g_pre_mix", 8), ("g_post_mix", 8), ("g_pre_ffn", 8),
                  ("g_post_ffn", 8), ("norm_ffn1_2", 8), ("norm_mix_2", 8), ("norm_ffn2_2", 8),
                  ("sb_q", 1), ("sb_k", 1), ("sb_out", 4), ("rw_mu", 14), ("rw_w0", 4), ("rw_a0", 4),
                  ("rw_k_k", 4), ("rw_k_a", 4), ("rw_r_k", 4), ("rw_ln_w", 4), ("rw_ln_b", 4),
                  ("pe_k", 32), ("pe_v", 32)]:
    COLS[_name] = (_at, _at + _n)
    _at += _n
NCOLS = _at

SBUF_START = 16896
SLOT = 11 * P
RING = 4
SPLIT = 3
FF1_PARTS = 4
NG = FF2 // P // 2
VCOLS = 348
ADA = 256
NADA = 6 * D // ADA


def weight_stream():
    out = [("w_v", n, 4 * VCOLS) for n in range(2)]
    out += [("w_in", n, 8 * P) for n in range(12)] + [("cmp1k", n, SLOT) for n in range(3)]
    out += [("w_in", n, 8 * P) for n in range(12, 16)] + [("cmp1v", n, SLOT) for n in range(3)]
    out += [("w_out", n, 8 * P) for n in range(8)]
    for q in range(FF1_PARTS):
        out += [("w_up", 8 * q + n, 8 * P) for n in range(8)]
        out += [("w_down", FF1_PARTS * n + q, 8 * P) for n in range(KD)]
    for m in ("1", "2"):
        for half in range(2):
            out += [(w + m, NG * half + n, 8 * P) for n in range(NG) for w in ("gate", "up")]
            out += [("down" + m, 2 * n + half, NG * P) for n in range(KD)]
        if m == "1":
            out += [("w_in2", n, 8 * P) for n in range(8)]
            out += [("w_v2", n, 2 * T) for n in range(4)]
            out += [("w_in2", n, 8 * P) for n in range(8, 22)]
            out += [("w_out2", n, 8 * P) for n in range(8)]
    return out


STREAM = weight_stream()


WHOLE = [i for i, t in enumerate(STREAM) if t[0].startswith("cmp1")]
PARTED = [i for i in range(len(STREAM)) if i not in WHOLE]
PINDEX = {STREAM[i][:2]: s for s, i in enumerate(PARTED)}
def build(nc, xt, consts, cols, pos, ada, mats, extra, out):
    ctx = ExitStack()
    with ctx:
        sems = {}

        def S(name):
            if name not in sems:
                sems[name] = ctx.enter_context(nc.semaphore(name))
            return sems[name]

        def sb(name, shape, dt=F32):
            return ctx.enter_context(nc.sbuf_tensor(name, shape, dt))

        place = [SBUF_START]

        def at(name, shape, dt=F32, offset=None):
            size = 4 * int(np.prod(shape[1:]))
            if offset is None:
                offset = place[0]
                place[0] += (size + 31) // 32 * 32
            return nc.alloc_sbuf_tensor_at(name, shape, dt, offset=offset), offset

        x, _ = at("x", [P, KD, T])
        hs, _ = at("hs", [P, 2, KD, T], F32R)
        ring, _ = at("ring", [P, RING, SLOT])
        wsp, wsp_at = at("wsp", [P, SPLIT, 2, SLOT], F32R)
        wal, _ = at("wal", [P, SPLIT * 2 * SLOT], F32, wsp_at)
        cst, _ = at("cst", [P, NCONST])
        col, _ = at("col", [P, NCOLS])
        ext, _ = at("ext", [P, 2 * T + 2 * DH])
        tmp, _ = at("tmp", [P, 6, T])
        arena, arena_at = at("arena", [P, 74 * 256])
        hids, _ = at("hids", [P, 2, NG, T], F32R, arena_at)
        mod, _ = at("mod", [P, 48])
        gain, _ = at("gain", [P, 32])
        gates, _ = at("gates", [P, NT, 24])
        widx, _ = at("widx", [P, NT, 4])
        best8, _ = at("best8", [P, 8])
        smin, _ = at("smin", [P, 3])
        ssum, _ = at("ssum", [P, 4])
        coef, _ = at("coef", [P, HEADS])
        hidc, _ = at("hidc", [P, 2, 2, CMP_N])
        rsum, _ = at("rsum", [P, 4])
        coef2, _ = at("coef2", [P, HEADS])
        cmin, _ = at("cmin", [P, HEADS])
        epsc, _ = at("epsc", [P, 3])
        sbg, _ = at("sbg", [P, 2])
        omka, _ = at("omka", [P, 4])
        ends, _ = at("ends", [P, 4, NCH])
        ropein, ropet, relu_t = tmp[:, 0:2, :], tmp[:, 2:4, :], tmp[:, 4:6, :]
        bank = ctx.enter_context(nc.psum_tensor("bank", [P, 8, T], F32))

        def const(name):
            a, b = CONST[name]
            return cst[:, a:b]

        def vec(name, i=0, n=1):
            return col[:, COLS[name][0] + i:COLS[name][0] + i + n]

        def area(at, shape):
            n = int(np.prod(shape))
            v = arena[:, at:at + n]
            if len(shape) == 2:
                v = v.rearrange("p (a b) -> p a b", a=shape[0])
            if len(shape) == 3:
                v = v.rearrange("p (a b c) -> p a b c", a=shape[0], b=shape[1])
            if len(shape) == 4:
                v = v.rearrange("p (a b c d) -> p a b c d", a=shape[0], b=shape[1], c=shape[2])
            return v

        K = 1024 // 4
        ybuf, sq = area(38 * K, (KD, T)), area(54 * K, (KD, T))
        ftmp, ht = tmp[:, 0:2, :], tmp[:, 0:4, :]
        rstd = tmp[:, 4, :]
        ada_in = [area(at * K, (KD, ADA)) for at in (0, 8, 18, 26)]
        ada_acc = [area(at * K, (ADA,)) for at in (16, 17, 34, 35)]
        proj = area(18 * K, (16, T))
        cos, sin = area(50 * K, (T,)), area(52 * K, (T,))
        vtok = area(54 * K, (NT, VCOLS))
        score = area(60 * K, (3, T))
        QI, KI, QD, KDD, KC, VC, KSL, KW, QN = 0, 2, 3, 7, 8, 9, 10, 11, 12
        blk = area(66 * K, (CMP_L, 2, CMP_N))
        kcmp = area(4 * K + 128, (CMP_N,))
        vcmp = area(5 * K, (2, 4 * DH))
        cs = area(7 * K, (2, HEADS, CMP_N))
        cpt = area(9 * K, (2, P))
        sneg = [area(at * K, (T,)) for at in (66, 68, 70)]
        prob = [area(at * K, (T,)) for at in (10, 12, 14, 16)]
        probT = [tmp[:, at, :] for at in (2, 3, 4, 5)]
        qk2 = area(0, (8, T))
        vtok2 = area(16 * K, (NT, T))
        AT0 = (0, 512, 896, 1152)
        sp = area(24 * K, (2, 1280))
        att = area(34 * K, (2, 1280))
        u = area(44 * K, (14, T))
        osb, shift = tmp[:, 0:4, :], tmp[:, 4:6, :]
        osb_sq, osb_r = area(0, (4, T)), area(8 * K, (4, T))
        ar = area(0, (4, NT, 2, P))
        bt, kt = area(16 * K, (4, T)), area(24 * K, (4, T))
        kr = area(32 * K, (4, T))
        csum, kf = area(40 * K, (T,)), area(42 * K, (T,))
        knorm, ksq, e2s = bt, kt, tmp[:, 4:6, :]
        sg, av = [wal[:, at * K:(at + 8) * K].rearrange("p (a b) -> p a b", a=4) for at in (8, 16)]
        e1s, e3s = [wal[:, at * K:(at + 4) * K].rearrange("p (a b) -> p a b", a=2) for at in (24, 28)]
        AT = area(32 * K, (4, 4 * P))
        Z = area(44 * K, (4, P))
        MT = area(48 * K, (2, 4, DH))
        St = area(50 * K, (2, 4, DH))
        ywkv = area(52 * K, (4, T))
        reset = area(72 * K, (T,))
        yc, yr = area(0, (4, T)), area(8 * K, (4, T))
        vtk = wal[:, 0:NT * T].rearrange("p (a b) -> p a b", a=NT)
        tok3 = wal[:, 8 * K:14 * K].rearrange("p (a b) -> p a b", a=3)
        PP = wal[:, 14 * K:22 * K].rearrange("p (a b c) -> p a b c", a=2, b=2)
        UR, UK, UV, UWA, UG = 0, 4, 8, 12, 13
        RW_ORDER = [12] + list(range(4, 8)) + list(range(0, 4)) + list(range(8, 12)) + [13]

        jobs = [(t, br, hh) for t in range(NT) for br in range(3) for hh in range(HEADS)]
        steps = [(hh, c) for hh in range(HEADS) for c in (3, 2, 1, 0)]
        SLOTS = 14
        slot_steps = [list(range(3 * n, min(3 * n + 3, 32))) for n in range(SLOTS)]

        NORMS = ["pre1", "post1", "f1", "post2", "g1", "mix", "g2"]
        LATE = ["post1", "post2", "mix", "g2"]
        HNORMS = ["pre1", "f1", "g1", "mix", "g2"]
        def piece_slot(i):
            return i % 4 if i < 8 else i % 2

        def pieces_in(i):
            n = sum(piece_slot(k) == piece_slot(i) for k in range(i + 1))
            return S(f"ada_in{piece_slot(i)}"), 16 * n

        BY_GPSIMD = [1, 3, 5, 7] + list(range(8, NADA))
        last = {}
        tile_done = []
        parts_done = []
        block = ctx.enter_context(nc.Block())

        @block.tensor
        def _(pe):
            def claim(b, sem, value):
                if b in last:
                    pe.wait_ge(*last[b])
                last[b] = (S(sem), value)

            def take_whole(name, sem, value):
                i = len(tile_done)
                assert STREAM[i][0] == name, (STREAM[i], name)
                tile_done.append((S(sem), value))
                pe.wait_ge(S(f"slot{i % RING}"), 16 * (i // RING + 1))
                return ring[:, i % RING, 0:STREAM[i][2]]

            def take(name, width, sem, value):
                i, s = len(tile_done), len(parts_done)
                assert STREAM[i][0] == name, (STREAM[i], name)
                tile_done.append((S("w_lo"), s + 1))
                parts_done.append((S(sem), value))
                pe.wait_ge(S("w_lo"), s + 1)
                return [wsp[:, s % SPLIT, part, 0:STREAM[i][2]].rearrange("p (k m) -> p k m", m=width) for part in (0, 1)]

            def product(out, lhs, rhs, start, stop):
                pe.matmul(out, lhs[0], rhs[0], start=start, stop=False)
                pe.matmul(out, lhs[0], rhs[1], start=False, stop=False)
                return pe.matmul(out, lhs[1], rhs[0], start=False, stop=stop)

            def gemm(name, b, kc, src, full, value, ready=None):
                gemms([(name, b, full, value)], kc, src, ready)

            def gemms(outs, kc, src, ready=None):
                ws = [take(name, P, full, value) for name, b, full, value in outs]
                for k in range(kc):
                    if ready and ready[1] + k >= 0:
                        pe.wait_ge(S(ready[0]), ready[1] + k + 1)
                    for w, (name, b, full, value) in zip(ws, outs):
                        mm = product(bank[:, b, :], [v[:, k, :] for v in w], [src[:, part, k, :] for part in (0, 1)],
                                     k == 0, k == kc - 1)
                        if k == kc - 1:
                            mm.then_inc(S(full), 1)

            def token_gemm(name, tiles, kc, width, full, freed):
                for t in range(NT):
                    claim(t, freed, t + 1)
                for j in range(tiles):
                    end = j == tiles - 1
                    w = take(name, width, full if end else name + "_part", NT if end else j + 1)
                    for kk in range(kc):
                        k = kc * j + kk
                        if name == "w_v":
                            pe.wait_ge(S("h"), k + 1)
                        for t in range(NT):
                            mm = product(bank[:, t, 0:width], [hs[:, part, k, t * P:(t + 1) * P] for part in (0, 1)],
                                         [v[:, kk, :] for v in w], k == 0, k == KD - 1)
                            if k == KD - 1:
                                mm.then_inc(S(full), 1)
                    if not end:
                        mm.then_inc(S(name + "_part"), 1)

            def sumsq(tag, k):
                pe.wait_ge(S("sq"), KD * NORMS.index(tag) + k + 1)
                mm = pe.matmul(bank[:, 4, :], const("ones"), sq[:, k, :], start=(k == 0), stop=(k == KD - 1))
                if k == KD - 1:
                    mm.then_inc(S("ms"), 1)

            def late_sumsq(tag):
                claim(4, "rms", NORMS.index(tag) + 1)
                pe.wait_ge(S("sq_sum"), (KD - 2) * (LATE.index(tag) + 1))
                pe.matmul(bank[:, 4, :], const("ones"), sq[:, 0, :], start=True, stop=False)
                pe.wait_ge(S("sq"), KD * (NORMS.index(tag) + 1))
                pe.matmul(bank[:, 4, :], const("ones"), sq[:, KD - 1, :], start=False, stop=True).then_inc(S("ms"), 1)

            def norm(tag):
                claim(4, "rms", NORMS.index(tag) + 1)
                for k in range(KD):
                    sumsq(tag, k)

            def ada_cols(i):
                pe.wait_ge(S(f"ada_acc{i % 2}"), i // 2 + 1)
                claim(7, "mod", i + 1)
                for j in range(2):
                    mm = pe.matmul(bank[:, 7, 2 * i + j:2 * i + j + 1], ada_acc[piece_slot(i)][:, j * P:(j + 1) * P],
                                   const("ones")[:, 0:1], start=True, stop=True)
                mm.then_inc(S("ada_cols"), 1)

            pe.wait_ge(S("consts"), 16)
            ada_cols(0)
            ada_cols(1)
            norm("pre1")
            for i in range(2, 8):
                ada_cols(i)
            token_gemm("w_v", 2, 4, VCOLS, "vtok_full", "vtok")

            def turn(n):
                pe.wait_ge(S("ropein"), n + 1)
                if n == VC:
                    return
                claim(4 + n % 2, "roped", n + 1)
                pe.matmul(bank[:, 4 + n % 2, :], const("turn"), ropein[:, n % 2, :], start=True, stop=True)\
                  .then_inc(S("turned"), 1)

            def logits(j):
                t, i = 1 + j // 4, j % 4
                pe.wait_ge(S("roped"), 3)
                claim(6, "relu_logits", j + 1)
                b = 64 * (i % 2)
                pe.matmul(bank[:, 6, 0:(t + 1) * P], proj[b:b + DH, QI + i // 2, t * P:(t + 1) * P],
                          proj[b:b + DH, KI, 0:(t + 1) * P], start=True, stop=True).then_inc(S("logits"), 1)

            def compress(m):
                ws = [take_whole("cmp1" + "kv"[m], "cmp_hid", m + 1).rearrange("p (l m) -> p l m", m=P) for _ in range(3)]
                pe.wait_ge(S("cmp_blocks"), m + 1)
                b = (6, 0)[m]
                claim(b, "cmp_gelu", m + 1)
                for l in range(CMP_L):
                    mm = pe.matmul(bank[:, b, 0:2 * CMP_N], ws[l // 11][:, l % 11, :],
                                   blk[:, l, :, :].rearrange("p g n -> p (g n)"), start=(l == 0), stop=(l == CMP_L - 1))
                mm.then_inc(S("cmp_hid"), 1)

            for n in range(16):
                claim(n % 4, "ropein", n + 1)
                if 4 <= n < 10:
                    logits(2 * (n - 4))
                gemm("w_in", n % 4, KD, hs, "proj_full", n + 1)
                if 4 <= n < 10:
                    logits(2 * (n - 4) + 1)
                if n >= 1:
                    turn(n - 1)
                if n >= 2:
                    ada_cols(8 + n - 2)
                if n == 11:
                    compress(0)
            turn(15)
            ada_cols(NADA - 2)
            ada_cols(NADA - 1)
            compress(1)
            pe.wait_ge(S("ext_in"), 16)
            pe.wait_ge(S("cmp_gelu"), 2)
            claim(5, "cmp_kv", 1)
            for g in range(2):
                pe.matmul(bank[64 * g:64 * g + DH, 5, 0:CMP_N], ext[:, 2 * T:2 * T + DH], hidc[:, 0, g, :],
                          start=True, stop=True)
                for i in range(4):
                    mm = pe.matmul(bank[32 * i:32 * i + CMP_N, 5, 64 + 64 * g:128 + 64 * g], hidc[:, 1, g, :],
                                   ext[:, 2 * T + DH:2 * T + 2 * DH], start=True, stop=True)
            mm.then_inc(S("cmp_out"), 1)

            def qk(j):
                t, br, hh = jobs[j]
                kv = (t + 1) * P
                b = 64 * (hh // 4) if br < 2 else 64 * (hh % 2)
                q = QN + hh % 4 if br < 2 else QD + hh // 2
                claim(j % 3, "smin", j + 1)
                pe.matmul(bank[:, j % 3, 0:kv], proj[b:b + DH, q, t * P:(t + 1) * P],
                          proj[b:b + DH, (KSL, KW, KDD)[br], 0:kv], start=True, stop=True).then_inc(S("scores"), 1)

            def turn_probs(j):
                pe.wait_ge(S("probs_scaled"), j + 1)
                claim(3 + j % 2, "probT", j + 1)
                for i in range(jobs[j][0] + 1):
                    mm = pe.transpose(bank[:, 3 + j % 2, i * P:(i + 1) * P], prob[j % 4][:, i * P:(i + 1) * P],
                                      const("ident"))
                mm.then_inc(S("probs_turned"), 1)

            def pv(j):
                t, br, hh = jobs[j]
                vc = ((hh // 4) * DH, P + (hh // 4) * DH, 2 * P)[br]
                pe.wait_ge(S("probT"), j + 1)
                half = br // 2
                if hh == 0 and br != 1:
                    claim(5 + half, "oT", 2 * t + half + 1)
                b, c = DH * (hh % 2), hh // 2
                for i in range(t + 1):
                    mm = pe.matmul(bank[b:b + DH, 5 + half, c * P:(c + 1) * P], vtok[:, i, vc:vc + DH],
                                   probT[j % 4][:, i * P:(i + 1) * P], start=(i == 0 and hh < 2 and br != 1),
                                   stop=False, skip_group_check=True)
                mm.then_inc(S("pv"), 1)

            def cmp_scores(t):
                claim(7, "cmp_masked", t + 1)
                for hh in range(HEADS):
                    b = 64 * (hh // 4)
                    mm = pe.matmul(bank[:, 7, hh * CMP_N:(hh + 1) * CMP_N],
                                   proj[b:b + DH, QN + hh % 4, t * P:(t + 1) * P], kcmp[b:b + DH, :],
                                   start=True, stop=True)
                    if hh == 3:
                        mm.then_inc(S("cmp_half"), 1)
                        pe.wait_ge(S("cmp_half"), t + 1)
                mm.then_inc(S("cmp_scores"), 1)

            def cmp_turn(t):
                pe.wait_ge(S("cmp_probs"), t + 1)
                claim(7, "cmp_probT", t + 1)
                for g in range(2):
                    mm = pe.transpose(bank[:, 7, g * P:(g + 1) * P],
                                      cs[:, 1, 4 * g:4 * g + 4, :].rearrange("p a b -> p (a b)"), const("ident"))
                mm.then_inc(S("cmp_turned"), 1)

            def cmp_out(t):
                pe.wait_ge(S("cmp_probT"), t + 1)
                for g in range(2):
                    for c in range(2):
                        pe.matmul(bank[:, 5, (2 * g + c) * P:(2 * g + c + 1) * P], vcmp[:, g, c * P:(c + 1) * P],
                                  cpt[:, g, :], start=False, stop=False, skip_group_check=True)

            pe.wait_ge(S("cmp_kv"), 1)
            pe.wait_ge(S("roped"), 16)
            n = len(jobs)
            for j in range(n + 3):
                if j < n:
                    qk(j)
                    if j % 24 == 0:
                        cmp_scores(j // 24)
                    if j % 24 == 4:
                        cmp_turn(j // 24)
                    if j % 24 == 7:
                        cmp_out(j // 24)
                if 2 <= j < n + 2:
                    turn_probs(j - 2)
                if 3 <= j:
                    pv(j - 3)

            def post_gemm(tag, name, n_parts, part, kc, src, ready, at):
                for n in range(KD):
                    v = KD * (int(tag) - 1 + part) + n + 1
                    claim(n % 4, "y_read", v)
                    gemm(name, n % 4, kc, src, "y_full", v, (ready, at) if n == 0 else None)
                if part == n_parts - 1:
                    late_sumsq("post" + tag)

            pe.wait_ge(S("oT"), 2 * NT)
            post_gemm("1", "w_out", 1, 0, KD, hs, "oT", 0)
            norm("f1")
            for q in range(FF1_PARTS):
                for n in range(0, 8, 2):
                    for i in (n, n + 1):
                        claim(i % 4, "relu", 8 * q + i + 1)
                    if q == 0 and n == 0:
                        gemms([("w_up", i, "up_full", i + 1) for i in (0, 1)], KD, hs, ("h", KD * HNORMS.index("f1")))
                    else:
                        for i in (n, n + 1):
                            gemm("w_up", i % 4, KD, hs, "up_full", 8 * q + i + 1)
                post_gemm("2", "w_down", FF1_PARTS, q, 8, hids, "hid", 8 * q)
            norm("g1")

            def swiglu_gemms(m, i, tag=None):
                for half in range(2):
                    for n in range(NG):
                        b = 2 * (n % 2)
                        v = NG * (2 * (int(m) - 1) + half) + n + 1
                        claim(b, "silu", v)
                        claim(b + 1, "gated", v)
                        if n == 0 and half == 0:
                            gemms([("gate" + m, 0, "gate_full", v), ("up" + m, 1, "gate_up_full", v)], KD, hs,
                                  ("h", KD * HNORMS.index("g" + m)))
                        else:
                            gemm("gate" + m, b, KD, hs, "gate_full", v)
                            gemm("up" + m, b + 1, KD, hs, "gate_up_full", v)
                    for n in range(KD):
                        v = KD * (i + half) + n + 1
                        claim(n % 4, "x_added", v)
                        gemm("down" + m, n % 4, NG, hids, "add_full", v,
                             ("hid2", NG * (2 * (int(m) - 1) + half)) if n == 0 else None)
                if tag:
                    late_sumsq(tag)

            swiglu_gemms("1", 0, "mix")

            def head_norm(n):
                pe.wait_ge(S("qk_sq"), n + 1)
                claim(4 + n % 2, "qk_root", n + 1)
                pe.matmul(bank[:, 4 + n % 2, :], const("pair"), ropein[:, n % 2, :], start=True, stop=True)\
                  .then_inc(S("qk_ms"), 1)

            for n in range(8):
                claim(n % 4, "qk2", n + 1)
                if n == 1:
                    gemms([("w_in2", i, "qk_full", i + 1) for i in (0, 1)], KD, hs, ("h", KD * HNORMS.index("mix")))
                elif n > 1:
                    gemm("w_in2", n % 4, KD, hs, "qk_full", n + 1)
                if n >= 1:
                    head_norm(n - 1)
            head_norm(7)
            token_gemm("w_v2", 4, 2, T, "vtok2_full", "vtok2")

            def sb_scores(s):
                hh, c = steps[s]
                b = 64 * (hh % 2)
                claim(2 + s % 3, "att_copy", s + 1)
                pe.matmul(bank[:, 2 + s % 3, 0:T - c * P], qk2[b:b + DH, 4 + hh // 2, c * P:(c + 1) * P],
                          qk2[b:b + DH, hh // 2, c * P:T], start=True, stop=True).then_inc(S("sb_scores"), 1)

            def sb_suffix(s):
                hh, c = steps[s]
                pe.wait_ge(S("softplus"), s + 1)
                w = T - c * P
                mm = pe.matmul(bank[:, 2 + s % 3, 0:w], const("suffix"), sp[:, hh % 2, AT0[c]:AT0[c] + w],
                               start=False, stop=(c == 3), skip_group_check=True)
                for cc in range(c + 1, NT):
                    ww = T - cc * P
                    mm = pe.matmul(bank[:, 2 + s % 3, w - ww:w], const("minus"), sp[:, hh % 2, AT0[cc]:AT0[cc] + ww],
                                   start=False, stop=(cc == NT - 1), skip_group_check=True)
                mm.then_inc(S("sb_suffix"), 1)

            def sb_pv(hh):
                pe.wait_ge(S("att"), 4 * hh + 4)
                b, o = 64 * (hh % 2), 5 + (hh // 2) % 2
                if hh % 2 == 0:
                    claim(o, "osb", hh // 2 + 1)
                for c in range(NT):
                    mm = pe.matmul(bank[b:b + DH, o, c * P:T], vtok2[:, c, hh * DH:(hh + 1) * DH],
                                   att[:, hh % 2, AT0[c]:AT0[c] + T - c * P], start=(c == 0), stop=(c == NT - 1),
                                   skip_group_check=True)
                mm.then_inc(S("sb_pv"), 1)

            pe.wait_ge(S("qk2"), 8)
            pe.wait_ge(S("vtok2"), NT)
            for n in range(SLOTS):
                for s in slot_steps[n]:
                    sb_scores(s)
                claim(n % 2, "u_raw", n + 1)
                gemm("w_in2", n % 2, KD, hs, "u_full", n + 1)
                if n >= 1:
                    for s in slot_steps[n - 1]:
                        if s % 4 == 3:
                            sb_pv(s // 4)
                for s in slot_steps[n]:
                    sb_suffix(s)
                if n == 12:
                    for i in range(4):
                        pe.wait_ge(S("osb_sq"), i + 1)
                        b = (2, 3, 4, 7)[i]
                        claim(b, "logs", i + 1)
                        pe.matmul(bank[:, b, :], const("pair"), osb_sq[:, i, :], start=True, stop=True)\
                          .then_inc(S("osb_ms"), 1)
                    for c in range(4):
                        pe.wait_ge(S("kk_sq"), c + 1)
                        b = (5, 6, 2, 3)[c]
                        claim(b, "kk_max", c + 1)
                        pe.matmul(bank[:, b, :], const("pair"), ksq[:, c, :], start=True, stop=True)\
                          .then_inc(S("kk_ms"), 1)
            pe.wait_ge(S("shifted"), 13)
            for t in range(NT):
                claim(4 + t % 2, "vtk", t + 1)
                for c in range(4):
                    mm = pe.transpose(bank[:, 4 + t % 2, c * P:(c + 1) * P], u[:, UV + c, t * P:(t + 1) * P],
                                      const("ident"))
                mm.then_inc(S("v_turned"), 1)
            pe.wait_ge(S("tanh"), 1)
            for c in range(4):
                claim(c % 2, "sg", c + 1)
                pe.matmul(bank[:, c % 2, :], ext[0:DH, c * P:(c + 1) * P], u[0:DH, UWA, :], start=True, stop=True)\
                  .then_inc(S("w_full"), 1)
                claim(2 + c % 2, "av", c + 1)
                pe.matmul(bank[:, 2 + c % 2, :], ext[DH:P, c * P:(c + 1) * P], u[DH:P, UWA, :], start=True, stop=True)\
                  .then_inc(S("a_full"), 1)
            for c in range(4):
                pe.wait_ge(S("rkr"), c + 1)
                claim(6 + c % 2, "bonus", c + 1)
                pe.matmul(bank[:, 6 + c % 2, :], const("pair"), kr[:, c, :], start=True, stop=True)\
                  .then_inc(S("bonus_full"), 1)
            pe.wait_ge(S("wkv_in"), 4)
            pe.wait_ge(S("bonus"), 4)
            pe.wait_ge(S("vtk"), NT)
            pe.wait_ge(S("state0"), 1)

            def head_at(hf, i):
                hh = 4 * hf + i
                return hh, hh // 2, 64 * (hh % 2)

            for w in range(NT):
                for i, src in enumerate(("a", "b", "k")):
                    claim(5 + i, "tok3", 3 * w + i + 1)
                    for c in range(4):
                        f = ar[:, c, w, 0, :] if i == 0 else (bt, kt)[i - 1][:, c, w * P:(w + 1) * P]
                        mm = pe.transpose(bank[:, 5 + i, c * P:(c + 1) * P], f, const("ident"))
                    mm.then_inc(S("tok3_full"), 1)
                for hf in range(2):
                    g = 2 * w + hf
                    for i in range(4):
                        hh, c, b = head_at(hf, i)
                        claim(i, "pairs", 4 * g + i + 1)
                        arw = ar[b:b + DH, c, w, :, :].rearrange("p a t -> p (a t)")
                        pe.matmul(bank[:, i, 0:256], bt[b:b + DH, c, w * P:(w + 1) * P], arw, start=True, stop=True)
                        pe.matmul(bank[:, i, 256:512], kt[b:b + DH, c, w * P:(w + 1) * P], arw,
                                  start=True, stop=True).then_inc(S("pairs_full"), 1)
                    claim(4, "power", 5 * g + 1)
                    claim(7, "power", 5 * g + 1)
                    for i in range(4):
                        hh, c, b = head_at(hf, i)
                        mm = pe.matmul(bank[:, 4 + 3 * (i % 2), (i // 2) * P:(i // 2 + 1) * P], ar[b:b + DH, c, w, 0, :],
                                       bt[b:b + DH, c, w * P:(w + 1) * P], start=True, stop=True)
                    mm.then_inc(S("power_full"), 1)
                    claim(5, "z", 7 * g + 1)
                    for i in range(4):
                        hh, c, b = head_at(hf, i)
                        pe.wait_ge(S("pairs"), 4 * g + i + 1)
                        mm = pe.matmul(bank[:, 5, i * DH:(i + 1) * DH], AT[:, i, 2 * P:3 * P],
                                       vtk[:, w, hh * DH:(hh + 1) * DH], start=True, stop=True)
                    mm.then_inc(S("z_full"), 1)
                    for lv in range(6):
                        now, nxt = lv % 2, (lv + 1) % 2

                        def powT(i):
                            return AT[:, i, 0:P] if lv == 0 else PP[:, now, 1, i * P:(i + 1) * P]

                        pe.wait_ge(S("power"), 5 * g + min(lv, 4) + 1)
                        if lv >= 1:
                            pe.wait_ge(S("powerT"), 5 * g + lv)
                        if lv < 5:
                            claim(6, "powerT", 5 * g + lv + 1)
                            for i in range(4):
                                mm = pe.matmul(bank[:, 6, i * P:(i + 1) * P], PP[:, now, 0, i * P:(i + 1) * P],
                                               powT(i), start=True, stop=True)
                            mm.then_inc(S("powerT_full"), 1)
                            if lv < 4:
                                claim(4, "power", 5 * g + lv + 2)
                                for i in range(4):
                                    mm = pe.matmul(bank[:, 4, i * P:(i + 1) * P], powT(i),
                                                   PP[:, now, 0, i * P:(i + 1) * P], start=True, stop=True)
                                mm.then_inc(S("power_full"), 1)
                        pe.wait_ge(S("z"), 7 * g + lv + 1)
                        claim(5, "z", 7 * g + lv + 2)
                        for i in range(4):
                            mm = pe.matmul(bank[:, 5, i * P:(i + 1) * P], powT(i), Z[:, i, :], start=True, stop=True)
                        mm.then_inc(S("z_full"), 1)
                    pe.wait_ge(S("z"), 7 * g + 7)
                    for bb in (7, 3, 6):
                        claim(bb, "mt", g + 1)
                    for i in range(4):
                        hh, c, b = head_at(hf, i)
                        pe.matmul(bank[b:b + DH, 7, (i // 2) * P:(i // 2 + 1) * P], Z[:, i, 0:DH], AT[:, i, P:2 * P],
                                  start=True, stop=True)
                        for j in range(2):
                            mm = pe.matmul(bank[b:b + DH, 3 + 3 * j, (i // 2) * DH:(i // 2 + 1) * DH],
                                           Z[64 * j:64 * j + DH, i, 0:DH],
                                           tok3[64 * j:64 * j + DH, 1, hh * DH:(hh + 1) * DH], start=True, stop=True)
                    mm.then_inc(S("mt_full"), 1)
                    claim(0, "wkv", g + 1)
                    for i in range(4):
                        hh, c, b = head_at(hf, i)
                        o = bank[b:b + DH, 0, (i // 2) * P:(i // 2 + 1) * P]
                        pe.matmul(o, vtk[:, w, hh * DH:(hh + 1) * DH], AT[:, i, 3 * P:4 * P], start=(i < 2), stop=False,
                                  skip_group_check=True)
                        pe.matmul(o, Z[:, i, DH:P], AT[:, i, P:2 * P], start=False, stop=False, skip_group_check=True)
                    for j in range(2):
                        claim(1 + j, "state", 2 * g + j + 1)
                        for i in range(4):
                            hh, c, b = head_at(hf, i)
                            rows = slice(64 * j, 64 * j + DH)
                            o = bank[b:b + DH, 1 + j, (i // 2) * DH:(i // 2 + 1) * DH]
                            pe.matmul(o, tok3[rows, 1, hh * DH:(hh + 1) * DH], Z[rows, i, DH:P], start=(i < 2), stop=False,
                                      skip_group_check=True)
                            mm = pe.matmul(o, tok3[rows, 2, hh * DH:(hh + 1) * DH], vtk[rows, w, hh * DH:(hh + 1) * DH],
                                           start=False, stop=False, skip_group_check=True)
                        mm.then_inc(S("state_part"), 1)
                    pe.wait_ge(S("mt"), g + 1)
                    pe.wait_ge(S("state_part"), 2 * g + 2)
                    for j in range(2):
                        n2 = 2 * g + j
                        if n2 >= 1:
                            pe.wait_ge(S("state"), n2)
                        for i in range(4):
                            hh, c, b = head_at(hf, i)
                            o = bank[b:b + DH, 1 + j, (i // 2) * DH:(i // 2 + 1) * DH]
                            mm = pe.matmul(o, MT[b:b + DH, j, c, :], St[b:b + DH, 0, c, :] if j == 0 else St[b:b + DH, 1, c, :],
                                           start=False, stop=True, skip_group_check=True)
                        mm.then_inc(S("state_full"), 1)
                        for i in range(4):
                            hh, c, b = head_at(hf, i)
                            mm = pe.matmul(bank[b:b + DH, 0, (i // 2) * P + 64 * j:(i // 2) * P + 64 * j + 64],
                                           St[b:b + DH, j, c, :], ar[b:b + DH, c, w, 1, 64 * j:64 * j + 64],
                                           start=False, stop=(j == 1), skip_group_check=True)
                    mm.then_inc(S("wkv_full"), 1)
            pe.wait_ge(S("wkv"), 8)
            pe.wait_ge(S("sig_g"), 1)
            for c in range(4):
                claim(c, "yc", c + 1)
                pe.matmul(bank[:, c, :], const("pair"), ywkv[:, c, :], start=True, stop=True).then_inc(S("y_sum"), 1)
            for c in range(4):
                claim(4 + c, "y_gated", c + 1)
                pe.matmul(bank[:, 4 + c, :], ext[:, T + c * P:T + (c + 1) * P], u[:, UG, :], start=True, stop=True)\
                  .then_inc(S("g_full"), 1)
            for c in range(4):
                pe.wait_ge(S("yc_sq"), c + 1)
                claim(c, "logs", 8 + c + 1)
                pe.matmul(bank[:, c, :], const("pair"), yr[:, c, :], start=True, stop=True).then_inc(S("y_ms"), 1)
            pe.wait_ge(S("o_sb"), 4)
            for n in range(KD):
                claim(n % 4, "x_added", KD * 2 + n + 1)
                if n == 1:
                    gemms([("w_out2", i, "add_full", KD * 2 + i + 1) for i in (0, 1)], KD, hs, ("o_rw", -4))
                elif n > 1:
                    gemm("w_out2", n % 4, KD, hs, "add_full", KD * 2 + n + 1)
            late_sumsq("g2")
            swiglu_gemms("2", 3)

        @block.scalar
        def _(act):
            step = [0]

            mine = {}

            def own(name):
                mine[name] = mine.get(name, 0) + 1
                act.wait_ge(S(name), mine[name])

            def do(ins):
                step[0] += 1
                ins.then_inc(S("act_step"), 1)
                act.wait_ge(S("act_step"), step[0])

            def split(upto):
                while mine.get("w_hi", 0) <= upto:
                    s = mine.get("w_hi", 0)
                    i = PARTED[s]
                    size = STREAM[i][2]
                    act.wait_ge(S(f"slot{i % RING}"), 16 * (i // RING + 1))
                    if s >= SPLIT:
                        act.wait_ge(*parts_done[s - SPLIT])
                    act.activation(wsp[:, s % SPLIT, 0, 0:size], ring[:, i % RING, 0:size], ACT.Copy)\
                       .then_inc(S("w_hi"), 1)
                    mine["w_hi"] = s + 1

            def ahead(name, n, last=None):
                split(min(PINDEX[name, n] + SPLIT, PINDEX[last or STREAM[PARTED[-1]][:2]]))

            def squares(tag, k, src):
                act.activation(sq[:, k, :], src, ACT.Square).then_inc(S("sq"), 1)

            def inverse_root(dst, src, width, eps, name):
                do(act.activation(dst, src, ACT.Ln, scale=1.0 / width, bias=eps))
                act.activation(dst, dst, ACT.Exp, scale=-0.5).then_inc(S(name), 1)
                own(name)

            def root(tag):
                act.wait_ge(S("ms"), NORMS.index(tag) + 1)
                inverse_root(rstd, bank[:, 4, :], D, epsc[:, 0:1], "rms")

            def norm_high(tag, add=None):
                for k in range(KD):
                    act.wait_ge(S("normed"), KD * HNORMS.index(tag) + k + 1)
                    if add:
                        ins = act.activation(hs[:, 0, k, :], ht[:, k % 4, :], ACT.Identity, bias=add(k))
                    else:
                        ins = act.activation(hs[:, 0, k, :], ht[:, k % 4, :], ACT.Copy)
                    ins.then_inc(S("h_hi"), 1)

            def ada_scale(i):
                act.wait_ge(*pieces_in(i))
                for kk in range(KD):
                    ins = act.activation(ada_in[piece_slot(i)][:, kk, :], ada_in[piece_slot(i)][:, kk, :], ACT.Copy, scale=vec("c", kk))
                ins.then_inc(S("ada_scaled"), 1)

            act.wait_ge(S("eps"), 3)
            act.wait_ge(S("cols_in"), 16)
            ada_scale(1)
            act.wait_ge(S("x_in"), 16)
            for k in range(KD):
                squares("pre1", k, x[:, k, :])
            ada_scale(3)
            ada_scale(5)
            root("pre1")
            ada_scale(7)
            act.wait_ge(S("angles"), 2)
            do(act.activation(sin, sin, ACT.Sin))
            do(act.activation(cos, cos, ACT.Sin))
            act.sem_inc(S("cossin"), 1)
            split(2)
            norm_high("pre1", lambda k: mod[:, k:k + 1])
            for t in range(NT):
                act.wait_ge(S("vtok_full"), t + 1)
                act.activation(vtok[:, t, :], bank[:, t, 0:VCOLS], ACT.Copy).then_inc(S("vtok"), 1)
                own("vtok")
            act.wait_ge(S("vtok"), NT)
            act.activation(gates[:, :, :], vtok[:, :, 320:344], ACT.Sigmoid).then_inc(S("gates"), 1)
            own("gates")
            act.activation(widx[:, :, :], vtok[:, :, 344:348], ACT.Copy, scale=1.0 / 16).then_inc(S("gates"), 1)
            own("gates")
            split(4)

            def relu_logits(j):
                t = 1 + j // 4
                act.wait_ge(S("logits"), j + 1)
                if j >= 2:
                    act.wait_ge(S("scored"), j - 1)
                act.activation(relu_t[:, j % 2, 0:(t + 1) * P], bank[:, 6, 0:(t + 1) * P], ACT.Relu)\
                   .then_inc(S("relu_logits"), 1)

            for n in range(16):
                ahead("w_in", n, ("w_in", 12 if n in (10, 11) else 15))
                if 4 <= n < 10:
                    relu_logits(2 * (n - 4))
                act.wait_ge(S("proj_full"), n + 1)
                if n >= 2:
                    act.wait_ge(S("roped"), n - 1)
                act.activation(ropein[:, n % 2, :], bank[:, n % 4, :], ACT.Copy).then_inc(S("ropein"), 1)
                own("ropein")
                if 4 <= n < 10:
                    relu_logits(2 * (n - 4) + 1)
                if n < NADA - 8:
                    ada_scale(n + 8)
            for m in range(2):
                act.wait_ge(S("cmp_hid"), m + 1)
                act.activation(hidc[:, m, :, :].rearrange("p g n -> p (g n)"), bank[:, (6, 0)[m], 0:2 * CMP_N],
                               ACT.Gelu_apprx_tanh).then_inc(S("cmp_gelu"), 1)
            split(PINDEX["w_out", 2])

            def probs_turned(j):
                kv = (jobs[j][0] + 1) * P
                act.wait_ge(S("probs_turned"), j + 1)
                if j >= 4:
                    act.wait_ge(S("pv"), j - 3)
                act.activation(probT[j % 4][:, 0:kv], bank[:, 3 + j % 2, 0:kv], ACT.Copy).then_inc(S("probT"), 1)

            def outputs(t, half):
                act.wait_ge(S("pv"), 24 * t + 16 + 8 * half)
                act.activation(hs[:, 0, 4 * half:4 * half + 4, t * P:(t + 1) * P],
                               bank[:, 5 + half, :].rearrange("p (c t) -> p c t", c=4), ACT.Copy).then_inc(S("oT_hi"), 1)

            for j, (t, br, hh) in enumerate(jobs):
                kv = (t + 1) * P
                act.wait_ge(S("smin"), j + 1)
                if j >= 4:
                    act.wait_ge(S("probs_turned"), j - 3)
                act.activation(prob[j % 4][:, 0:kv], sneg[j % 3][:, 0:kv], ACT.Exp, scale=-1.0,
                               bias=smin[:, j % 3:j % 3 + 1], accum_out=ssum[:, j % 4:j % 4 + 1])\
                   .then_inc(S("probs"), 1)
                if j % 24 == 0:
                    act.wait_ge(S("cmp_shift"), t + 1)
                    act.activation(cs[:, 1, :, :], cs[:, 0, :, :], ACT.Exp, scale=-1.0).then_inc(S("cmp_exp"), 1)
                    own("cmp_exp")
                if j >= 2:
                    probs_turned(j - 2)
                if j % 24 == 19:
                    outputs(t, 0)
                if j >= 24 and j % 24 == 3:
                    outputs(t - 1, 1)
            probs_turned(len(jobs) - 2)
            probs_turned(len(jobs) - 1)
            outputs(NT - 1, 1)

            def post(tag, name, n_parts, part):
                for n in range(KD):
                    ahead(name, n_parts * n + part)
                    if part == n_parts - 1:
                        act.wait_ge(S("y_read"), KD * (int(tag) - 1 + part) + n + 1)
                        squares("post" + tag, n, ybuf[:, n, :])
                if part == n_parts - 1:
                    root("post" + tag)

            def pre(tag, ready, at, add=None):
                for k in range(KD):
                    act.wait_ge(S(ready), at + k + 1)
                    squares(tag, k, x[:, k, :])
                root(tag)
                norm_high(tag, add)

            post("1", "w_out", 1, 0)
            pre("f1", "x_post", 0, lambda k: mod[:, 24 + k:25 + k])
            for q in range(FF1_PARTS):
                for n in range(8):
                    nn = 8 * q + n
                    ahead("w_up", nn)
                    act.wait_ge(S("up_full"), nn + 1)
                    if nn >= 2:
                        act.wait_ge(S("hid"), nn - 1)
                    act.activation(ftmp[:, n % 2, :], bank[:, n % 4, :], ACT.Relu).then_inc(S("relu"), 1)
                    own("relu")
                    act.activation(hids[:, 0, n, :], ftmp[:, n % 2, :], ACT.Square).then_inc(S("hid_hi"), 1)
                post("2", "w_down", FF1_PARTS, q)
            pre("g1", "x_post", KD)

            def silu(m, i, tag=None):
                for half in range(2):
                    for n in range(NG):
                        v = NG * (2 * (int(m) - 1) + half) + n
                        ahead("gate" + m, NG * half + n)
                        act.wait_ge(S("gate_full"), v + 1)
                        if v >= 2:
                            act.wait_ge(S("hid2"), v - 1)
                        act.activation(ftmp[:, n % 2, :], bank[:, 2 * (n % 2), :], ACT.Silu).then_inc(S("silu"), 1)
                        ahead("up" + m, NG * half + n)
                        act.wait_ge(S("gated"), v + 1)
                        act.activation(hids[:, 0, n, :], ftmp[:, n % 2, :], ACT.Copy).then_inc(S("hid2_hi"), 1)
                    for n in range(KD):
                        ahead("down" + m, 2 * n + half)
                        if tag and half:
                            act.wait_ge(S("x_added"), KD * (i + half) + n + 1)
                            squares(tag, n, x[:, n, :])

            silu("1", 0, "mix")
            root("mix")
            norm_high("mix")
            for n in range(8):
                ahead("w_in2", n)
                act.wait_ge(S("qk_full"), n + 1)
                act.activation(ropein[:, n % 2, :], bank[:, n % 4, :], ACT.Square).then_inc(S("qk_sq"), 1)
                own("qk_sq")
                act.wait_ge(S("qk_ms"), n + 1)
                if n >= 2:
                    act.wait_ge(S("qk2"), n - 1)
                inverse_root(ropet[:, n % 2, :], bank[:, 4 + n % 2, :], DH, epsc[:, 0:1], "qk_root")
            for j in range(3):
                ahead("w_v2", j)
            for t in range(NT):
                act.wait_ge(S("vtok2_full"), t + 1)
                act.activation(vtok2[:, t, :], bank[:, t, :], ACT.Copy).then_inc(S("vtok2"), 1)
                own("vtok2")
            ahead("w_v2", 3)
            for n in range(SLOTS + 1):
                if n == 12:
                    act.wait_ge(S("shifted"), 1)
                    act.activation(u[0:DH, UWA, :], u[0:DH, UWA, :], ACT.Tanh).then_inc(S("tanh"), 1)
                    for i in range(4):
                        act.wait_ge(S("osb"), i + 1)
                        act.activation(osb_sq[:, i, :], osb[:, i, :], ACT.Square).then_inc(S("osb_sq"), 1)
                    for c in range(4):
                        act.wait_ge(S("kk0"), c + 1)
                        act.activation(ksq[:, c, :], knorm[:, c, :], ACT.Square).then_inc(S("kk_sq"), 1)
                if n == 13:
                    for i in range(4):
                        act.wait_ge(S("osb_ms"), i + 1)
                        act.activation(osb_r[:, i, :], bank[:, (2, 3, 4, 7)[i], :], ACT.Ln, scale=1.0 / DH,
                                       bias=epsc[:, 0:1]).then_inc(S("logs"), 1)
                    for c in range(4):
                        act.wait_ge(S("kk_max"), c + 1)
                        act.activation(kr[:, c, :], kr[:, c, :], ACT.Ln).then_inc(S("logs"), 1)
                    act.wait_ge(S("logs"), 8)
                    for i in range(4):
                        act.activation(osb_r[:, i, :], osb_r[:, i, :], ACT.Exp, scale=-0.5).then_inc(S("osb_root"), 1)
                    for c in range(4):
                        act.activation(kr[:, c, :], kr[:, c, :], ACT.Exp, scale=-0.5).then_inc(S("kk_root"), 1)
                if n < SLOTS:
                    for s in slot_steps[n]:
                        w = T - steps[s][1] * P
                        hh, c = steps[s]
                        z = att[:, hh % 2, AT0[c]:AT0[c] + w]
                        act.wait_ge(S("sb_scores"), s + 1)
                        if hh >= 2 and c == 3:
                            act.wait_ge(S("sb_pv"), hh - 1)
                        do(act.activation(z, bank[:, 2 + s % 3, 0:w], ACT.Abs))
                        act.activation(z, z, ACT.Exp, scale=-1.0).then_inc(S("sb_exp"), 1)
                    for s in slot_steps[n]:
                        hh, c = steps[s]
                        z = att[:, hh % 2, AT0[c]:AT0[c] + T - c * P]
                        act.wait_ge(S("sb_exp"), s + 1)
                        act.activation(z, z, ACT.Ln, bias=epsc[:, 2:3]).then_inc(S("log1p"), 1)
                    ahead("w_in2", 8 + n, ("w_in2", 21))
                    act.wait_ge(S("u_full"), n + 1)
                    act.activation(u[:, RW_ORDER[n], :], bank[:, n % 2, :], ACT.Copy).then_inc(S("u_raw"), 1)
                    own("u_raw")
                    for s in slot_steps[n]:
                        hh, c = steps[s]
                        a = att[:, hh % 2, AT0[c]:AT0[c] + T - c * P]
                        act.wait_ge(S("att_copy"), s + 1)
                        act.activation(a, a, ACT.Exp).then_inc(S("att"), 1)
                        own("att")
                if n >= 1:
                    for s in slot_steps[n - 1]:
                        hh = s // 4
                        if s % 8 == 7:
                            act.wait_ge(S("sb_pv"), hh + 1)
                            act.activation(osb[:, hh // 2, :], bank[:, 5 + (hh // 2) % 2, :], ACT.Copy)\
                               .then_inc(S("osb"), 1)
                            own("osb")
            for n in range(4):
                act.wait_ge(S("osb_normed"), n + 1)
                act.activation(hs[:, 0, n, :], osb[:, n, :], ACT.Copy).then_inc(S("o_sb_hi"), 1)
            for t in range(NT):
                act.wait_ge(S("v_turned"), t + 1)
                act.activation(vtk[:, t, :], bank[:, 4 + t % 2, :], ACT.Copy).then_inc(S("vtk"), 1)
                own("vtk")
            act.wait_ge(S("shifted"), 14)
            act.activation(u[:, UG, :], u[:, UG, :], ACT.Sigmoid).then_inc(S("sig_g"), 1)
            for c in range(4):
                act.wait_ge(S("w_full"), c + 1)
                act.activation(sg[:, c, :], bank[:, c % 2, :], ACT.Sigmoid, bias=vec("rw_w0", c)).then_inc(S("sg"), 1)
                act.wait_ge(S("a_full"), c + 1)
                act.activation(av[:, c, :], bank[:, 2 + c % 2, :], ACT.Sigmoid, bias=vec("rw_a0", c)).then_inc(S("av"), 1)
            for c in range(4):
                if c >= 2:
                    act.wait_ge(S("wkv_in"), c - 1)
                act.wait_ge(S("csum"), 2 * c + 1)
                act.activation(e1s[:, c % 2, :], csum, ACT.Exp, scale=-DECAY).then_inc(S("exps"), 1)
                act.activation(e2s[:, c % 2, :], csum, ACT.Exp, scale=DECAY).then_inc(S("exps"), 1)
                act.wait_ge(S("csum"), 2 * c + 2)
                act.activation(e3s[:, c % 2, :], e3s[:, c % 2, :], ACT.Exp, scale=-DECAY).then_inc(S("exps"), 1)
            for w in range(NT):
                for i in range(3):
                    act.wait_ge(S("tok3_full"), 3 * w + i + 1)
                    act.activation(tok3[:, i, :], bank[:, 5 + i, :], ACT.Copy).then_inc(S("tok3"), 1)
                    own("tok3")
                for hf in range(2):
                    g = 2 * w + hf
                    for lv in range(5):
                        act.wait_ge(S("powerT_full"), 5 * g + lv + 1)
                        act.activation(PP[:, (lv + 1) % 2, 1, :], bank[:, 6, :], ACT.Copy).then_inc(S("powerT"), 1)
                        own("powerT")
                    act.wait_ge(S("wkv_full"), g + 1)
                    act.activation(ywkv[:, 2 * hf:2 * hf + 2, w * P:(w + 1) * P],
                                   bank[:, 0, 0:256].rearrange("p (c t) -> p c t", c=2), ACT.Copy).then_inc(S("wkv"), 1)
                    own("wkv")
            split(PINDEX["w_out2", 2])
            for c in range(4):
                act.wait_ge(S("yc"), c + 1)
                act.activation(yr[:, c, :], yc[:, c, :], ACT.Square).then_inc(S("yc_sq"), 1)
            for c in range(4):
                act.wait_ge(S("y_ms"), c + 1)
                act.activation(yr[:, c, :], bank[:, c, :], ACT.Ln, scale=1.0 / DH, bias=epsc[:, 1:2]).then_inc(S("logs"), 1)
            for c in range(4):
                act.wait_ge(S("logs"), 8 + c + 1)
                act.activation(yr[:, c, :], yr[:, c, :], ACT.Exp, scale=-0.5).then_inc(S("y_root"), 1)
            for c in range(4):
                act.wait_ge(S("y_gated"), c + 1)
                act.activation(hs[:, 0, 4 + c, :], yc[:, c, :], ACT.Copy).then_inc(S("o_rw_hi"), 1)
            for n in range(KD):
                ahead("w_out2", n)
                act.wait_ge(S("x_added"), KD * 2 + n + 1)
                squares("g2", n, x[:, n, :])
            root("g2")
            norm_high("g2")
            silu("2", 3)

        @block.vector
        def _(dve):
            step = [0]

            mine = {}

            def own(name):
                mine[name] = mine.get(name, 0) + 1
                dve.wait_ge(S(name), mine[name])

            def do(ins):
                step[0] += 1
                ins.then_inc(S("dve_step"), 1)
                dve.wait_ge(S("dve_step"), step[0])

            for i, e in enumerate((EPS, LNX_EPS, 1.0)):
                dve.memset(epsc[:, i:i + 1], e).then_inc(S("eps"), 1)
                own("eps")
            def lo(upto):
                while mine.get("w_lo", 0) <= upto:
                    s = mine.get("w_lo", 0)
                    i = PARTED[s]
                    size = STREAM[i][2]
                    dve.wait_ge(S("w_hi"), s + 1)
                    dve.tensor_tensor(wsp[:, s % SPLIT, 1, 0:size], ring[:, i % RING, 0:size],
                                      wsp[:, s % SPLIT, 0, 0:size].bitcast(F32), ALU.subtract).then_inc(S("w_lo"), 1)
                    mine["w_lo"] = s + 1

            def ahead(name, n, last=None):
                lo(min(PINDEX[name, n] + SPLIT, PINDEX[last or STREAM[PARTED[-1]][:2]]))

            def ada_piece(i):
                if i == 0:
                    dve.wait_ge(S("cols_in"), 16)
                dve.wait_ge(*pieces_in(i))
                if i >= 4:
                    dve.wait_ge(S("ada_cols"), i - 3)
                acc = ada_acc[piece_slot(i)]
                do(dve.tensor_scalar(acc, ada_in[piece_slot(i)][:, 0, :], vec("c", 0), None, ALU.mult))
                for kk in range(1, KD):
                    ins = dve.scalar_tensor_tensor(out=acc, in0=ada_in[piece_slot(i)][:, kk, :], scalar=vec("c", kk),
                                                   in1=acc, op0=ALU.mult, op1=ALU.add)
                    if kk < KD - 1:
                        do(ins)
                ins.then_inc(S(f"ada_acc{i % 2}"), 1)
                own(f"ada_acc{i % 2}")

            def mod_cols(i):
                dve.wait_ge(S("ada_cols"), i + 1)
                dve.tensor_tensor(mod[:, 2 * i:2 * i + 2], bank[:, 7, 2 * i:2 * i + 2], vec("b_ada", 2 * i, 2),
                                  ALU.add).then_inc(S("mod"), 1)
                own("mod")

            def modulate(i, scale_at, g):
                dve.scalar_tensor_tensor(out=gain[:, 8 * i:8 * i + 8], in0=mod[:, scale_at:scale_at + 8],
                                         scalar=1.0, in1=vec(g, 0, 8), op0=ALU.add, op1=ALU.mult)\
                   .then_inc(S("gain"), 1)
                own("gain")

            def normalize(tag, scale, add=None):
                at = KD * HNORMS.index(tag)
                dve.wait_ge(S("rms"), NORMS.index(tag) + 1)
                for kk in range(KD + 1):
                    if kk < KD:
                        if kk >= 4:
                            dve.wait_ge(S("h"), at + kk - 3)
                        dve.scalar_tensor_tensor(out=ht[:, kk % 4, :], in0=x[:, kk, :], scalar=scale(kk), in1=rstd,
                                                 op0=ALU.mult, op1=ALU.mult).then_inc(S("normed"), 1)
                    if kk >= 1:
                        k = kk - 1
                        dve.wait_ge(S("h_hi"), at + k + 1)
                        v, high = ht[:, k % 4, :], hs[:, 0, k, :].bitcast(F32)
                        if add:
                            ins = dve.scalar_tensor_tensor(out=hs[:, 1, k, :], in0=v, scalar=add(k), in1=high,
                                                           op0=ALU.add, op1=ALU.subtract)
                        else:
                            ins = dve.tensor_tensor(hs[:, 1, k, :], v, high, ALU.subtract)
                        ins.then_inc(S("h"), 1)

            ada_piece(0)
            ipos = ropet[:, 0, :]
            dve.wait_ge(S("pos_in"), 16)
            dve.wait_ge(S("consts"), 16)
            ang, k = ropein[:, 0, :], ropein[:, 1, :]
            do(dve.tensor_copy(ang, ipos.bitcast(I32)))
            do(dve.tensor_scalar(ang, ang, const("inv"), None, ALU.mult))
            do(dve.tensor_scalar(k, ang, TWO_PI_INV, MAGIC, ALU.mult, ALU.add))
            do(dve.tensor_scalar(k, k, MAGIC, None, ALU.subtract))
            for part in (PI_A, PI_B, PI_C):
                do(dve.scalar_tensor_tensor(out=ang, in0=k, scalar=-part, in1=ang, op0=ALU.mult, op1=ALU.add))
            dve.tensor_scalar(sin, ang, -PI_SAFE, PI_SAFE, ALU.max, ALU.min).then_inc(S("angles"), 1)
            own("angles")
            do(dve.tensor_scalar(k, ang, -1.0, None, ALU.mult))
            do(dve.tensor_tensor(k, k, ang, ALU.max))
            dve.tensor_scalar(cos, k, -1.0, float(np.pi / 2), ALU.mult, ALU.add).then_inc(S("angles"), 1)
            own("angles")

            for i in (2, 4, 6):
                ada_piece(i)
                mod_cols(i - 2)
                mod_cols(i - 1)
            mod_cols(6)
            mod_cols(7)
            lo(2)
            dve.wait_ge(S("mod"), 8)
            modulate(0, 8, "g_pre_mix")
            dve.wait_ge(S("gain"), 1)
            normalize("pre1", lambda k: gain[:, k:k + 1], lambda k: mod[:, k:k + 1])

            def rope(n):
                src = ropein[:, n % 2, :]
                dve.wait_ge(S("ropein"), n + 1)
                if n == VC:
                    dve.tensor_copy(proj[:, n, :], src).then_inc(S("roped"), 1)
                    own("roped")
                    return
                scale = -DH ** -0.5 if QD <= n < QD + 4 or n >= QN else 1.0
                do(dve.scalar_tensor_tensor(out=ropet[:, 0, :], in0=src, scalar=scale, in1=cos,
                                            op0=ALU.mult, op1=ALU.mult))
                dve.wait_ge(S("turned"), n + 1 - (n > VC))
                do(dve.scalar_tensor_tensor(out=ropet[:, 1, :], in0=bank[:, 4 + n % 2, :], scalar=scale, in1=sin,
                                            op0=ALU.mult, op1=ALU.mult))
                dve.tensor_tensor(proj[:, n, :], ropet[:, 0, :], ropet[:, 1, :], ALU.add).then_inc(S("roped"), 1)
                own("roped")

            def index_score(j):
                t, i = 1 + j // 4, j % 4
                kv = (t + 1) * P
                dve.wait_ge(S("relu_logits"), j + 1)
                s = score[:, t - 1, 0:kv]
                r = relu_t[:, j % 2, 0:kv]
                if i == 0:
                    dve.tensor_scalar(s, r, widx[:, t, 0:1], None, ALU.mult).then_inc(S("scored"), 1)
                    own("scored")
                else:
                    dve.wait_ge(S("scored"), j)
                    dve.scalar_tensor_tensor(out=s, in0=r, scalar=widx[:, t, i:i + 1], in1=s, op0=ALU.mult,
                                             op1=ALU.add).then_inc(S("scored"), 1)
                    own("scored")
                if i == 3:
                    dve.wait_ge(S("scored"), j + 1)
                    do(dve.tensor_tensor(s, s, const("causal")[:, T - kv:T], ALU.subtract))

            def cmp_blocks(m):
                src, pe_name = ((KC, "pe_k"), (VC, "pe_v"))[m]
                dve.wait_ge(S("roped"), src + 1)
                if m:
                    dve.wait_ge(S("cmp_hid"), 1)
                for half in range(2):
                    for g in range(2):
                        rows = slice(DH * g, DH * g + DH)
                        v = proj[rows, src, 16 * half:16 * half + 16 * 31].rearrange("p (n l) -> p l n", l=16)
                        pe_b = vec(pe_name, 16 * half, 16)[rows, :, None].to_broadcast([DH, 16, 31])
                        ins = dve.tensor_tensor(blk[rows, 16 * half:16 * half + 16, g, 0:31], v, pe_b, ALU.add)
                        if half + g < 2:
                            do(ins)
                ins.then_inc(S("cmp_blocks"), 1)
                own("cmp_blocks")

            def top_round(r):
                t, n = 1 + r // ROUNDS, r % ROUNDS
                s = score[:, t - 1, 0:(t + 1) * P]
                do(dve.max(best8[:, :], s))
                do(dve.match_replace(s, best8[:, :], s, -3.0 * NEG))
                if n == ROUNDS - 1:
                    do(dve.tensor_scalar(s, s, -2.0 * NEG, NEG, ALU.is_gt, ALU.mult))

            dve.wait_ge(S("cossin"), 1)
            dve.wait_ge(S("gates"), 2)
            rounds = 0
            lo(4)
            for n in range(16):
                if n >= 1:
                    rope(n - 1)
                ahead("w_in", n, ("w_in", 12 if n in (10, 11) else 15))
                if 4 <= n < 10:
                    index_score(2 * (n - 4))
                    index_score(2 * (n - 4) + 1)
                if n >= 2:
                    mod_cols(8 + n - 2)
                if n == 6:
                    do(dve.memset(blk, 0.0))
                if n in (10, 12):
                    cmp_blocks((n - 10) // 2)
                while n >= 7 and rounds < ROUNDS * (n - 6) // 9:
                    top_round(rounds)
                    rounds += 1
            rope(15)
            mod_cols(NADA - 2)
            mod_cols(NADA - 1)
            dve.wait_ge(S("mod"), NADA)
            dve.tensor_tensor(gain[:, 8:16], mod[:, 16:24], vec("g_post_mix", 0, 8), ALU.mult).then_inc(S("gain"), 1)
            own("gain")
            modulate(2, 32, "g_pre_ffn")
            dve.tensor_tensor(gain[:, 24:32], mod[:, 40:48], vec("g_post_ffn", 0, 8), ALU.mult).then_inc(S("gain"), 1)
            own("gain")
            dve.wait_ge(S("gain"), 4)
            do(dve.memset(vcmp, 0.0))
            dve.wait_ge(S("cmp_out"), 1)
            do(dve.tensor_copy(kcmp, bank[:, 5, 0:CMP_N]))
            for g in range(2):
                for i in range(4):
                    do(dve.tensor_copy(vcmp[32 * i:32 * i + 32, g, i * DH:(i + 1) * DH],
                                       bank[32 * i:32 * i + 32, 5, 64 + 64 * g:128 + 64 * g]))
            dve.sem_inc(S("cmp_kv"), 1)
            lo(PINDEX["w_out", 2])

            def masked(j):
                t, br, hh = jobs[j]
                kv = (t + 1) * P
                dve.wait_ge(S("scores"), j + 1)
                if j >= 3:
                    dve.wait_ge(S("probs"), j - 2)
                mask = score[:, t - 1, 0:kv] if br == 2 and t else const("causal")[:, T - kv:T]
                dve.tensor_tensor_reduce(sneg[j % 3][:, 0:kv], bank[:, j % 3, 0:kv], mask, 1.0, 3e38, ALU.add, ALU.min,
                                         smin[:, j % 3:j % 3 + 1]).then_inc(S("smin"), 1)

            def scaled(j):
                t, br, hh = jobs[j]
                p = prob[j % 4][:, 0:(t + 1) * P]
                dve.wait_ge(S("probs"), j + 1)
                r = rsum[:, j % 4:j % 4 + 1]
                do(dve.reciprocal(r, ssum[:, j % 4:j % 4 + 1]))
                gate = 3 * hh + br + 1
                if br < 2:
                    ins = dve.tensor_scalar(p, p, r, gates[:, t, gate:gate + 1], ALU.mult, ALU.mult)
                else:
                    ins = dve.tensor_scalar(p, p, r, None, ALU.mult)
                ins.then_inc(S("probs_scaled"), 1)

            def outputs(t, half):
                dve.wait_ge(S("oT_hi"), 2 * t + half + 1)
                chunks = slice(4 * half, 4 * half + 4)
                dve.tensor_tensor(hs[:, 1, chunks, t * P:(t + 1) * P], bank[:, 5 + half, :].rearrange("p (c t) -> p c t", c=4),
                                  hs[:, 0, chunks, t * P:(t + 1) * P].bitcast(F32), ALU.subtract).then_inc(S("oT"), 1)

            def cmp_masked(t):
                keep = const("cmp_keep")[:, t * CMP_N:(t + 1) * CMP_N]
                drop = const("cmp_drop")[:, t * CMP_N:(t + 1) * CMP_N]
                c0 = cs[:, 0, :, :]
                dve.wait_ge(S("cmp_scores"), t + 1)
                dve.tensor_tensor(c0, bank[:, 7, 0:256].rearrange("p (a b) -> p a b", a=HEADS),
                                  keep[:, None, :].to_broadcast([P, HEADS, CMP_N]), ALU.mult)\
                   .then_inc(S("cmp_masked"), 1)
                own("cmp_masked")
                dve.wait_ge(S("cmp_masked"), t + 1)
                do(dve.tensor_tensor(c0, c0, drop[:, None, :].to_broadcast([P, HEADS, CMP_N]), ALU.add))
                do(dve.tensor_reduce(cmin[:, :], c0, AX.X, ALU.min))
                dve.tensor_tensor(c0, c0, cmin[:, :, None].to_broadcast([P, HEADS, CMP_N]), ALU.subtract)\
                   .then_inc(S("cmp_shift"), 1)
                own("cmp_shift")

            def cmp_probs(t):
                keep = const("cmp_keep")[:, t * CMP_N:(t + 1) * CMP_N]
                c1 = cs[:, 1, :, :]
                dve.wait_ge(S("cmp_exp"), t + 1)
                do(dve.tensor_reduce(cmin[:, :], c1, AX.X, ALU.add))
                do(dve.reciprocal(coef[:, :], cmin[:, :]))
                gate = gates[:, t, :].rearrange("p (h i) -> p h i", i=3)[:, :, 0]
                do(dve.tensor_tensor(coef2[:, :], coef[:, :], gate, ALU.mult))
                do(dve.tensor_tensor(c1, c1, keep[:, None, :].to_broadcast([P, HEADS, CMP_N]), ALU.mult))
                dve.tensor_tensor(c1, c1, coef2[:, :, None].to_broadcast([P, HEADS, CMP_N]), ALU.mult)\
                   .then_inc(S("cmp_probs"), 1)
                own("cmp_probs")

            n = len(jobs)
            for j in range(n + 3):
                if j < n:
                    masked(j)
                    t = j // 24
                    if j % 24 == 0:
                        cmp_masked(t)
                    if j % 24 == 2:
                        cmp_probs(t)
                    if j % 24 == 5:
                        dve.wait_ge(S("cmp_turned"), t + 1)
                        dve.tensor_copy(cpt.rearrange("p a b -> p (a b)"), bank[:, 7, 0:256]).then_inc(S("cmp_probT"), 1)
                        own("cmp_probT")
                if 1 <= j < n + 1:
                    scaled(j - 1)
                if j % 24 == 19:
                    outputs(j // 24, 0)
                if j >= 24 and j % 24 == 3 and j < n:
                    outputs(j // 24 - 1, 1)
                if rounds < 3 * ROUNDS and j < n and j >= (8, 8, 24)[rounds // ROUNDS] + 2 * (rounds % ROUNDS):
                    top_round(rounds)
                    rounds += 1
            outputs(NT - 1, 1)

            def post(tag, name, n_parts, part):
                for nn in range(KD):
                    at = KD * (int(tag) - 1 + part) + nn + 1
                    dve.wait_ge(S("y_full"), at)
                    if part == 0:
                        ins = dve.tensor_copy(ybuf[:, nn, :], bank[:, nn % 4, :])
                    else:
                        ins = dve.tensor_tensor(ybuf[:, nn, :], ybuf[:, nn, :], bank[:, nn % 4, :], ALU.add)
                    ins.then_inc(S("y_read"), 1)
                    ahead(name, n_parts * nn + part)
                dve.wait_ge(S("y_read"), KD * (int(tag) + part))

            def post_norm(tag, g_at):
                dve.wait_ge(S("rms"), NORMS.index("post" + tag) + 1)
                for nn in range(KD):
                    do(dve.tensor_tensor(ybuf[:, nn, :], ybuf[:, nn, :], rstd, ALU.mult))
                    dve.scalar_tensor_tensor(out=x[:, nn, :], in0=ybuf[:, nn, :], scalar=gain[:, g_at + nn:g_at + nn + 1],
                                             in1=x[:, nn, :], op0=ALU.mult, op1=ALU.add).then_inc(S("x_post"), 1)
                    own("x_post")

            post("1", "w_out", 1, 0)
            post_norm("1", 8)
            normalize("f1", lambda k: gain[:, 16 + k:17 + k], lambda k: mod[:, 24 + k:25 + k])
            for q in range(FF1_PARTS):
                for n in range(8):
                    nn = 8 * q + n
                    v = ftmp[:, n % 2, :]
                    ahead("w_up", nn)
                    dve.wait_ge(S("hid_hi"), nn + 1)
                    do(dve.tensor_tensor(v, v, v, ALU.mult))
                    dve.tensor_tensor(hids[:, 1, n, :], v, hids[:, 0, n, :].bitcast(F32), ALU.subtract)\
                       .then_inc(S("hid"), 1)
                post("2", "w_down", FF1_PARTS, q)
            post_norm("2", 24)
            normalize("g1", lambda k: vec("norm_ffn1_2", k))

            def swiglu(m, i):
                for half in range(2):
                    for nn in range(NG):
                        v = NG * (2 * (int(m) - 1) + half) + nn + 1
                        f = ftmp[:, nn % 2, :]
                        ahead("gate" + m, NG * half + nn)
                        dve.wait_ge(S("silu"), v)
                        dve.wait_ge(S("gate_up_full"), v)
                        dve.tensor_tensor(f, f, bank[:, 2 * (nn % 2) + 1, :], ALU.mult).then_inc(S("gated"), 1)
                        ahead("up" + m, NG * half + nn)
                        dve.wait_ge(S("hid2_hi"), v)
                        dve.tensor_tensor(hids[:, 1, nn, :], f, hids[:, 0, nn, :].bitcast(F32), ALU.subtract)\
                           .then_inc(S("hid2"), 1)
                    add_to_x(i + half, 0.5, "down" + m, 2, half)

            def add_to_x(i, scale, name, n_parts, part):
                for nn in range(KD):
                    dve.wait_ge(S("add_full"), KD * i + nn + 1)
                    dve.scalar_tensor_tensor(out=x[:, nn, :], in0=bank[:, nn % 4, :], scalar=scale, in1=x[:, nn, :],
                                             op0=ALU.mult, op1=ALU.add).then_inc(S("x_added"), 1)
                    ahead(name, n_parts * nn + part)
                dve.wait_ge(S("x_added"), KD * (i + 1))

            swiglu("1", 0)
            normalize("mix", lambda k: vec("norm_mix_2", k))
            do(dve.tensor_scalar(sbg[:, 0:1], vec("sb_q"), DH ** -0.5, None, ALU.mult))
            do(dve.tensor_copy(sbg[:, 1:2], vec("sb_k")))
            for nn in range(8):
                ahead("w_in2", nn)
                dve.wait_ge(S("qk_root"), nn + 1)
                dve.scalar_tensor_tensor(out=qk2[:, nn, :], in0=bank[:, nn % 4, :], scalar=sbg[:, nn // 4:nn // 4 + 1],
                                         in1=ropet[:, nn % 2, :], op0=ALU.mult, op1=ALU.mult).then_inc(S("qk2"), 1)
                own("qk2")
            for j in range(4):
                ahead("w_v2", j)
            for nn in range(SLOTS):
                if nn == 12:
                    do(dve.memset(reset, 1.0))
                    do(dve.memset(reset.rearrange("p (c t) -> p c t", t=CHUNK)[:, :, 0:1], 0.0))
                    do(dve.tensor_scalar(omka[:, :], vec("rw_k_a", 0, 4), -1.0, 1.0, ALU.mult, ALU.add))
                    dve.wait_ge(S("sb_pv"), HEADS)
                    dve.wait_ge(S("shifted"), 5)
                    for c in range(4):
                        dve.tensor_scalar(knorm[:, c, :], u[:, UK + c, :], vec("rw_k_k", c), None, ALU.mult)\
                           .then_inc(S("kk0"), 1)
                if nn == 13:
                    for c in range(4):
                        dve.wait_ge(S("kk_ms"), c + 1)
                        dve.tensor_scalar(kr[:, c, :], bank[:, (5, 6, 2, 3)[c], :], 1e-24, None, ALU.max)\
                           .then_inc(S("kk_max"), 1)
                    for i in range(4):
                        dve.wait_ge(S("osb_root"), i + 1)
                        dve.scalar_tensor_tensor(out=osb[:, i, :], in0=osb[:, i, :], scalar=vec("sb_out", i),
                                                 in1=osb_r[:, i, :], op0=ALU.mult, op1=ALU.mult)\
                           .then_inc(S("osb_normed"), 1)
                    for c in range(4):
                        dve.wait_ge(S("kk_root"), c + 1)
                        do(dve.tensor_tensor(knorm[:, c, :], knorm[:, c, :], kr[:, c, :], ALU.mult))
                for s in slot_steps[nn]:
                    hh, c = steps[s]
                    w = T - c * P
                    d = sp[:, hh % 2, AT0[c]:AT0[c] + w]
                    dve.wait_ge(S("log1p"), s + 1)
                    if s >= 8 and s % 4 == 0:
                        dve.wait_ge(S("sb_suffix"), s - 4)
                    do(dve.scalar_tensor_tensor(out=d, in0=bank[:, 2 + s % 3, 0:w], scalar=0.0,
                                                in1=att[:, hh % 2, AT0[c]:AT0[c] + w], op0=ALU.max, op1=ALU.add))
                    dve.tensor_tensor(d[:, 0:P], d[:, 0:P], const("before"), ALU.mult).then_inc(S("softplus"), 1)
                    own("softplus")
                ahead("w_in2", 8 + nn, ("w_in2", 21))
                for s in slot_steps[nn]:
                    hh, c = steps[s]
                    w = T - c * P
                    dve.wait_ge(S("sb_suffix"), s + 1)
                    dve.tensor_tensor(att[:, hh % 2, AT0[c]:AT0[c] + w], bank[:, 2 + s % 3, 0:w],
                                      const("notbefore")[:, 0:w], ALU.add).then_inc(S("att_copy"), 1)
                    own("att_copy")
            for nn in range(4):
                dve.wait_ge(S("o_sb_hi"), nn + 1)
                dve.tensor_tensor(hs[:, 1, nn, :], osb[:, nn, :], hs[:, 0, nn, :].bitcast(F32), ALU.subtract)\
                   .then_inc(S("o_sb"), 1)

            def wins(v):
                return v.rearrange("p (w t) -> p w t", w=NT)

            def bonus(c):
                dve.wait_ge(S("bonus_full"), c + 1)
                dve.wait_ge(S("v_turned"), NT)
                dve.tensor_tensor(u[:, UV + c, :], bank[:, 6 + c % 2, :], u[:, UV + c, :], ALU.mult).then_inc(S("bonus"), 1)

            for c in range(4):
                r, kx, k1 = u[:, UR + c, :], u[:, UK + c, :], knorm[:, c, :]
                e1, e2, e3 = e1s[:, c % 2, :], e2s[:, c % 2, :], e3s[:, c % 2, :]
                dve.wait_ge(S("sg"), c + 1)
                if c:
                    dve.wait_ge(S("exps"), 3 * c)
                dve.tensor_tensor_scan(csum, reset, sg[:, c, :], 0.0, ALU.mult, ALU.add).then_inc(S("csum"), 1)
                dve.wait_ge(S("csum"), 2 * c + 1)
                dve.tensor_tensor(e3, csum, sg[:, c, :], ALU.subtract).then_inc(S("csum"), 1)
                dve.wait_ge(S("av"), c + 1)
                do(dve.tensor_scalar(kf, av[:, c, :], vec("rw_k_a", c), omka[:, c:c + 1], ALU.mult, ALU.add))
                do(dve.tensor_tensor(kf, kf, kx, ALU.mult))
                dve.scalar_tensor_tensor(out=kr[:, c, :], in0=r, scalar=vec("rw_r_k", c), in1=kf,
                                         op0=ALU.mult, op1=ALU.mult).then_inc(S("rkr"), 1)
                dve.wait_ge(S("exps"), 3 * c + 3)
                dve.tensor_tensor(kt[:, c, :], kf, e2, ALU.mult)
                dve.tensor_tensor(ar[:, c, :, 1, :], wins(r), wins(e1), ALU.mult)
                do(dve.scalar_tensor_tensor(out=ar[:, c, :, 0, :], in0=wins(k1), scalar=-1.0, in1=wins(e3),
                                            op0=ALU.mult, op1=ALU.mult))
                do(dve.tensor_tensor(k1, k1, av[:, c, :], ALU.mult))
                dve.tensor_tensor(bt[:, c, :], k1, e2, ALU.mult)
                dve.tensor_copy(ends[:, c, :], e1.rearrange("p (j t) -> p j t", t=CHUNK)[:, :, CHUNK - 1])\
                   .then_inc(S("wkv_in"), 1)
                own("wkv_in")
                if c:
                    bonus(c - 1)
            bonus(3)
            dve.memset(St[:, :, :, :], 0.0).then_inc(S("state0"), 1)
            own("state0")
            dve.wait_ge(S("state0"), 1)
            for w in range(NT):
                for hf in range(2):
                    g = 2 * w + hf
                    for i in range(4):
                        dve.wait_ge(S("pairs_full"), 4 * g + i + 1)
                        dve.tensor_tensor(AT[:, i, :], bank[:, i, :], const("chunk4"), ALU.mult).then_inc(S("pairs"), 1)
                    dve.wait_ge(S("power_full"), 5 * g + 1)
                    for i in range(2):
                        ins = dve.tensor_tensor(PP[:, 0, 0, :].rearrange("p (a o b) -> p a o b", a=2, o=2)[:, :, i, :],
                                                bank[:, 4 + 3 * i, 0:256].rearrange("p (a b) -> p a b", a=2),
                                                const("chunkT")[:, None, :].to_broadcast([P, 2, P]), ALU.mult)
                        if i == 0:
                            do(ins)
                    ins.then_inc(S("power"), 1)
                    own("power")
                    dve.wait_ge(S("tok3"), 3 * w + 3)
                    dve.wait_ge(S("z_full"), 7 * g + 1)
                    do(dve.tensor_copy(Z[:, :, DH:P], bank[:, 5, 0:256].rearrange("p (a b) -> p a b", a=4)))
                    dve.tensor_copy(Z[:, :, 0:DH], tok3[:, 0, 256 * hf:256 * hf + 256].rearrange("p (a b) -> p a b", a=4))\
                       .then_inc(S("z"), 1)
                    own("z")
                    for lv in range(6):
                        if lv < 4:
                            dve.wait_ge(S("power_full"), 5 * g + lv + 2)
                            dve.tensor_copy(PP[:, (lv + 1) % 2, 0, :], bank[:, 4, :]).then_inc(S("power"), 1)
                            own("power")
                        dve.wait_ge(S("z_full"), 7 * g + lv + 2)
                        dve.wait_ge(S("z"), 7 * g + lv + 1)
                        dve.tensor_tensor(Z[:, :, :], Z[:, :, :], bank[:, 5, :].rearrange("p (a b) -> p a b", a=4),
                                          ALU.add).then_inc(S("z"), 1)
                        own("z")
                    dve.wait_ge(S("mt_full"), g + 1)
                    rr = ar[:, 2 * hf:2 * hf + 2, w, 1, :]
                    do(dve.tensor_tensor(rr, rr, bank[:, 7, 0:256].rearrange("p (c t) -> p c t", c=2), ALU.add))
                    for j in range(2):
                        ins = dve.tensor_tensor(MT[:, j, 2 * hf:2 * hf + 2, :],
                                                bank[:, 3 + 3 * j, 0:P].rearrange("p (c k) -> p c k", c=2),
                                                const("ident64")[:, None, :].to_broadcast([P, 2, DH]), ALU.add)
                        if j == 0:
                            do(ins)
                    ins.then_inc(S("mt"), 1)
                    own("mt")
                    for j in range(2):
                        n2 = 2 * g + j
                        dve.wait_ge(S("state_full"), n2 + 1)
                        if j == 1:
                            dve.wait_ge(S("wkv_full"), g + 1)
                        e = ends[:, 2 * hf:2 * hf + 2, 2 * w + j:2 * w + j + 1].to_broadcast([P, 2, DH])
                        dve.tensor_tensor(St[:, (j + 1) % 2, 2 * hf:2 * hf + 2, :],
                                          bank[:, 1 + j, 0:128].rearrange("p (c v) -> p c v", c=2), e, ALU.mult)\
                           .then_inc(S("state"), 1)
                        own("state")
            lo(PINDEX["w_out2", 2])
            for c in range(4):
                dve.wait_ge(S("y_sum"), c + 1)
                dve.scalar_tensor_tensor(out=yc[:, c, :], in0=bank[:, c, :], scalar=-1.0 / DH, in1=ywkv[:, c, :],
                                         op0=ALU.mult, op1=ALU.add).then_inc(S("yc"), 1)
            for c in range(4):
                v = yc[:, c, :]
                dve.wait_ge(S("y_root"), c + 1)
                do(dve.tensor_tensor(v, v, yr[:, c, :], ALU.mult))
                do(dve.tensor_scalar(v, v, vec("rw_ln_w", c), vec("rw_ln_b", c), ALU.mult, ALU.add))
                do(dve.tensor_tensor(v, v, u[:, UV + c, :], ALU.add))
                dve.wait_ge(S("g_full"), c + 1)
                dve.tensor_tensor(v, v, bank[:, 4 + c, :], ALU.mult).then_inc(S("y_gated"), 1)
                if c:
                    dve.wait_ge(S("o_rw_hi"), c)
                    dve.tensor_tensor(hs[:, 1, 3 + c, :], yc[:, c - 1, :], hs[:, 0, 3 + c, :].bitcast(F32), ALU.subtract)\
                       .then_inc(S("o_rw"), 1)
            dve.wait_ge(S("o_rw_hi"), 4)
            dve.tensor_tensor(hs[:, 1, 7, :], yc[:, 3, :], hs[:, 0, 7, :].bitcast(F32), ALU.subtract)\
               .then_inc(S("o_rw"), 1)
            add_to_x(2, 1.0, "w_out2", 1, 0)
            normalize("g2", lambda k: vec("norm_ffn2_2", k))
            swiglu("2", 3)

        @block.gpsimd
        def _(pool):
            step = [0]

            mine = {"ada_acc0": 4}

            def own(name):
                mine[name] = mine.get(name, 0) + 1
                pool.wait_ge(S(name), mine[name])

            def do(ins):
                step[0] += 1
                ins.then_inc(S("pool_step"), 1)
                pool.wait_ge(S("pool_step"), step[0])

            for n, i in enumerate(BY_GPSIMD):
                if i == 8:
                    pool.wait_ge(S("ada_acc0"), 4)
                v = ada_in[piece_slot(i)]
                pool.wait_ge(S("ada_scaled"), n + 1)
                if i >= 4:
                    pool.wait_ge(S("ada_cols"), i - 3 if i < 10 else i - 1)
                do(pool.tensor_tensor(v[:, 0:4, :], v[:, 0:4, :], v[:, 4:8, :], ALU.add))
                do(pool.tensor_tensor(v[:, 0:2, :], v[:, 0:2, :], v[:, 2:4, :], ALU.add))
                pool.tensor_tensor(ada_acc[piece_slot(i)], v[:, 0, :], v[:, 1, :], ALU.add)\
                    .then_inc(S(f"ada_acc{i % 2}"), 1)
                own(f"ada_acc{i % 2}")
            def add_squares(tag):
                for k in range(1, KD - 1):
                    pool.wait_ge(S("sq"), KD * NORMS.index(tag) + k + 1)
                    pool.tensor_tensor(sq[:, 0, :], sq[:, 0, :], sq[:, k, :], ALU.add).then_inc(S("sq_sum"), 1)
                    own("sq_sum")

            for tag in LATE[:3]:
                add_squares(tag)
            for n in range(SLOTS):
                f = u[:, RW_ORDER[n], :]
                d = shift[:, n % 2, :]
                pool.wait_ge(S("u_raw"), n + 1)
                do(pool.tensor_scalar(d[:, 0:1], f[:, 0:1], -1.0, None, ALU.mult))
                do(pool.tensor_tensor(d[:, 1:T], f[:, 0:T - 1], f[:, 1:T], ALU.subtract))
                do(pool.tensor_scalar(d, d, vec("rw_mu", RW_ORDER[n]), None, ALU.mult))
                pool.tensor_tensor(f, f, d, ALU.add).then_inc(S("shifted"), 1)
                own("shifted")
            add_squares("g2")

        @block.sync
        def _(sy):
            def ada_load(i):
                if i >= 4:
                    k = i - 4 if i < 10 else i - 2
                    sy.wait_ge(S(f"ada_acc{k % 2}"), k // 2 + 1)
                sem, _ = pieces_in(i)
                sy.dma_start(ada_in[piece_slot(i)].rearrange("p k n -> p (k n)"), ada[i]).then_inc(sem, 16)

            def tile_load(i):
                name, n, size = STREAM[i]
                if i >= RING:
                    sy.wait_ge(*tile_done[i - RING])
                sy.dma_start(ring[:, i % RING, 0:size], mats[name][n]).then_inc(S(f"slot{i % RING}"), 16)

            sy.dma_start(col[:, :], cols).then_inc(S("cols_in"), 16)
            ada_load(0)
            ada_load(1)
            sy.dma_start(cst[:, :], consts).then_inc(S("consts"), 16)
            sy.dma_start(x[:, :, :].rearrange("p k t -> p (k t)"), xt).then_inc(S("x_in"), 16)
            sy.dma_start(ropet[:, 0, :].bitcast(I32), pos.to_broadcast([P, T])).then_inc(S("pos_in"), 16)
            for i in range(2, 8):
                ada_load(i)
                if i == 6:
                    tile_load(0)
                    tile_load(1)
            sy.dma_start(ext[:, :], extra).then_inc(S("ext_in"), 16)
            ada_before = {("w_in", n): [n + 4] for n in range(4, 12)}
            ada_before.update({("w_in", 12): [16, 17], ("w_in", 13): [18, 19, 20], ("w_in", 14): [21], ("cmp1v", 0): [22, 23]})
            for i in range(2, len(tile_done)):
                for piece in ada_before.get(STREAM[i][:2], []):
                    ada_load(piece)
                tile_load(i)
            for n in range(KD):
                sy.wait_ge(S("x_added"), 4 * KD + n + 1)
                sy.dma_start(out[:, n * T:(n + 1) * T], x[:, n, :]).then_inc(S("stored"), 16)
            sy.wait_ge(S("stored"), 16 * KD)


def columns(v):
    return np.ascontiguousarray(np.asarray(v).reshape(-1, P).T)


def tiles(w, parts=1):
    kd, n = w.shape
    kc = kd // P // parts
    t = w.reshape(parts, kc, P, n // P, P).transpose(3, 0, 2, 1, 4)
    return np.ascontiguousarray(t.reshape(n // P * parts, P, kc * P))


def lay_out(inp):
    f = {k: np.asarray(v) for k, v in inp.items()}
    w_in = f["w_in"][0]
    cuts = np.cumsum([0, 512, 128, 128, 128, 128, 128, 128, 24, 512, 64, 64, 256, 64, 4])
    qn, kc, vc, ksl, vsl, kw, vw, gl, qd, kd, vd, qi, ki, wi = [w_in[:, a:b] for a, b in zip(cuts[:-1], cuts[1:])]
    qn = qn.reshape(D, 2, 4, DH).transpose(0, 2, 1, 3).reshape(D, 512)
    feat = np.concatenate([qi, ki, ki, qd, kd, kd, kc, vc, ksl, kw, qn], 1)
    tok = np.concatenate([vsl, vw, vd, gl, wi], 1)
    mats = {"w_in": tiles(feat),
            "w_v": np.ascontiguousarray(tok.reshape(2, 4, P, VCOLS).transpose(0, 2, 1, 3).reshape(2, P, 4 * VCOLS))}
    for name in ("k", "v"):
        w1 = f["cmp_w1_" + name][0].reshape(CMP_L, DH, P).transpose(1, 0, 2)
        w1 = np.concatenate([w1, w1], 0)
        w1 = np.concatenate([w1, np.zeros((P, 1, P), np.float32)], 1)
        mats["cmp1" + name] = np.ascontiguousarray(w1.reshape(P, 3, SLOT).transpose(1, 0, 2))
    mats["w_out"] = tiles(f["w_out"][0])
    mats["w_up"] = tiles(f["w_up"][0])
    mats["w_down"] = tiles(f["w_down"][0], 4)
    for m in ("1", "2"):
        mats["gate" + m] = tiles(f[f"ffn{m}_gate_2"][0])
        mats["up" + m] = tiles(f[f"ffn{m}_up_2"][0])
        mats["down" + m] = tiles(f[f"ffn{m}_down_2"][0], 2)
    w2 = f["w_in_2"][0]
    u = w2[:, 1536:].reshape(D, 14, P)[:, [12] + list(range(4, 8)) + list(range(4)) + list(range(8, 12)) + [13]]
    mats["w_in2"] = tiles(np.concatenate([w2[:, 0:1024], u.reshape(D, -1)], 1))
    mats["w_v2"] = np.ascontiguousarray(w2[:, 1024:1536].reshape(4, 2, P, T).transpose(0, 2, 1, 3).reshape(4, P, 2 * T))
    mats["w_out2"] = tiles(f["w_out_2"][0])
    ada = np.ascontiguousarray(f["w_ada"][0].reshape(KD, P, NADA, ADA).transpose(2, 1, 0, 3).reshape(NADA, P, KD * ADA))
    pair = lambda v: np.concatenate([v, v], -1)
    cols = [columns(f["c"][0]), columns(f["b_ada"][0])] + [columns(f[n][0]) for n in (
        "g_pre_mix", "g_post_mix", "g_pre_ffn", "g_post_ffn", "norm_ffn1_2", "norm_mix_2", "norm_ffn2_2")]
    cols += [columns(pair(f["sb_q_norm_2"][0])), columns(pair(f["sb_k_norm_2"][0])), columns(f["sb_out_norm_2"][0])]
    cols += [columns(f[n][0]) for n in ("rw_mu_2", "rw_w0_2", "rw_a0_2", "rw_k_k_2", "rw_k_a_2", "rw_r_k_2",
                                        "rw_ln_w_2", "rw_ln_b_2")]
    cols += [np.concatenate([f["cmp_pe_" + n][0].T] * 2, 0) for n in ("k", "v")]
    cols = np.ascontiguousarray(np.concatenate(cols, 1))
    lora = np.concatenate([f["rw_w2_2"][0], f["rw_a2_2"][0]], 0)
    extra = np.ascontiguousarray(np.concatenate([lora, f["rw_g2_2"][0], f["cmp_w2_k"][0], f["cmp_w2_v"][0]], 1))
    xt = np.ascontiguousarray(f["x"][0].T.reshape(KD, P, T).transpose(1, 0, 2).reshape(P, KD * T))
    arrays = {"xt": xt, "consts": CONSTS, "cols": cols, "pos": np.ascontiguousarray(f["positions"]), "ada": ada,
              "extra": extra}
    arrays.update({"m_" + k: v for k, v in mats.items()})
    return arrays


def declare(nc, arrays):
    aps = {}
    for name, a in arrays.items():
        aps[name] = nc.dram_tensor(name, a.shape, mybir.dt.from_np(a.dtype), kind="ExternalInput").ap()
    return aps


def kernel(**inputs):
    from concourse import bacc
    from concourse.bass_utils import run_bass_kernel_spmd

    nc = bacc.Bacc("TRN2", target_bir_lowering=False, num_devices=1)
    arrays = lay_out(inputs)
    aps = declare(nc, arrays)
    out = nc.dram_tensor("out", (P, KD * T), F32, kind="ExternalOutput").ap()
    mats = {k[2:]: v for k, v in aps.items() if k.startswith("m_")}
    build(nc, aps["xt"], aps["consts"], aps["cols"], aps["pos"], aps["ada"], mats, aps["extra"], out)
    r = run_bass_kernel_spmd(nc, [arrays], core_ids=[0])
    y = r.results[0]["out"]
    return np.ascontiguousarray(y.reshape(P, KD, T).transpose(2, 1, 0).reshape(1, T, D))
```
